# Optimizing a Trainium2 kernel written in Bass

```python
import jax, jax.numpy as jnp
from jax import lax
import numpy as np

D_MODEL = 2048
BATCH = 1
SEQ = 256
DEPTH = 2

CHUNK = 64
N_META = 16
BLOCK_Q = 128
PAD = BLOCK_Q - N_META
ROPE_THETA = 10000.0
EPS = 1e-6
NEG = -1e30

GROUP_WIDTH = D_MODEL // 4
A_HEAD_DIM = 64
A_HEADS = GROUP_WIDTH // A_HEAD_DIM
A_KV_HEADS = A_HEADS // 4
A_WIDTH = A_HEADS * A_HEAD_DIM
A_WIN = 128
A_WIN_CHUNKS = A_WIN // CHUNK
B_NOPE = 128
B_ROPE = 64
B_VDIM = 128
B_HEADS = GROUP_WIDTH // B_VDIM
B_WIDTH = B_HEADS * B_VDIM
B_Q_RANK = GROUP_WIDTH
B_KV_RANK = GROUP_WIDTH // 2
C_WIDTH = GROUP_WIDTH
C_CONV = 3
D_WIDTH = GROUP_WIDTH
D_CONV = 31

D_MIX = A_WIDTH + B_WIDTH + C_WIDTH + D_WIDTH
IN_SPLITS = (
    A_WIDTH, A_KV_HEADS * A_HEAD_DIM, A_KV_HEADS * A_HEAD_DIM, A_WIDTH,
    B_Q_RANK, B_KV_RANK, B_ROPE, B_WIDTH,
    C_WIDTH, C_WIDTH, C_WIDTH, C_WIDTH,
    2 * D_WIDTH, D_WIDTH,
)
IN_TOTAL = sum(IN_SPLITS)

kernel_name = "hymba_style_chunk_causal_hybrid"

def _split(t, sizes):
    idx = []
    acc = 0
    for s in sizes[:-1]:
        acc += s
        idx.append(acc)
    return jnp.split(t, idx, axis=-1)

def rms_norm(x, w):
    xf = x.astype(jnp.float32)
    y = xf * lax.rsqrt(jnp.mean(xf * xf, axis=-1, keepdims=True) + EPS)
    return (y * w.astype(jnp.float32)).astype(x.dtype)

def layer_norm(x, w, b):
    xf = x.astype(jnp.float32)
    mu = jnp.mean(xf, axis=-1, keepdims=True)
    xc = xf - mu
    y = xc * lax.rsqrt(jnp.mean(xc * xc, axis=-1, keepdims=True) + EPS)
    return (y * w.astype(jnp.float32) + b.astype(jnp.float32)).astype(x.dtype)

def rope_tables(n_pos, dim):
    inv = 1.0 / (ROPE_THETA ** (jnp.arange(0, dim, 2, dtype=jnp.float32) / dim))
    ang = jnp.arange(n_pos, dtype=jnp.float32)[:, None] * inv[None, :]
    return jnp.cos(ang), jnp.sin(ang)

def apply_rope(x, cos, sin):
    xf = x.astype(jnp.float32)
    x1, x2 = jnp.split(xf, 2, axis=-1)
    c = cos[None, :, None, :]
    s = sin[None, :, None, :]
    return jnp.concatenate([x1 * c - x2 * s, x2 * c + x1 * s], axis=-1).astype(x.dtype)

def pad_front(t):
    return jnp.pad(t, ((0, 0), (PAD, 0)) + ((0, 0),) * (t.ndim - 2))

def causal_dwconv(x, w):
    k, c = w.shape
    return lax.conv_general_dilated(
        x, w[:, None, :].astype(x.dtype), window_strides=(1,), padding=[(k - 1, 0)],
        dimension_numbers=('NWC', 'WIO', 'NWC'), feature_group_count=c)

def swa_sink_attention(q, k, v, sinks):
    bn, L, H, dh = q.shape
    G = H // A_KV_HEADS
    qp, kp, vp = pad_front(q), pad_front(k), pad_front(v)
    Lp = L + PAD
    nc = Lp // CHUNK
    qc = qp.reshape(bn, nc, CHUNK, A_KV_HEADS, G, dh)
    kc = kp.reshape(bn, nc, CHUNK, A_KV_HEADS, dh)
    vc = vp.reshape(bn, nc, CHUNK, A_KV_HEADS, dh)

    def band(t):
        parts = [jnp.pad(t, ((0, 0), (w, 0), (0, 0), (0, 0), (0, 0)))[:, :nc]
                 for w in range(A_WIN_CHUNKS - 1, -1, -1)]
        return jnp.concatenate(parts, axis=2)

    kb, vb = band(kc), band(vc)
    k_meta = kp[:, PAD:PAD + N_META]
    v_meta = vp[:, PAD:PAD + N_META]
    scale = dh ** -0.5
    s_band = jnp.einsum('bcqhgd,bckhd->bchgqk', qc, kb, preferred_element_type=jnp.float32) * scale
    s_meta = jnp.einsum('bcqhgd,bmhd->bchgqm', qc, k_meta, preferred_element_type=jnp.float32) * scale
    c_idx = jnp.arange(nc)
    nb = A_WIN_CHUNKS * CHUNK
    key_pos = (c_idx[:, None] - (A_WIN_CHUNKS - 1)) * CHUNK + jnp.arange(nb)[None, :]
    band_ok = key_pos >= PAD
    meta_chunk = PAD // CHUNK
    meta_ok = c_idx > meta_chunk + A_WIN_CHUNKS - 1
    s_band = jnp.where(band_ok[None, :, None, None, None, :], s_band, NEG)
    s_meta = jnp.where(meta_ok[None, :, None, None, None, None], s_meta, NEG)
    sink = jnp.broadcast_to(sinks.astype(jnp.float32).reshape(1, 1, A_KV_HEADS, G, 1, 1),
                            s_band.shape[:-1] + (1,))
    p = jax.nn.softmax(jnp.concatenate([s_band, s_meta, sink], axis=-1), axis=-1)
    o = (jnp.einsum('bchgqk,bckhd->bcqhgd', p[..., :nb].astype(v.dtype), vb)
         + jnp.einsum('bchgqm,bmhd->bcqhgd', p[..., nb:nb + N_META].astype(v.dtype), v_meta))
    return o.reshape(bn, Lp, H * dh)[:, PAD:]

def mla_attention(q_nope, q_rope, k_nope, k_rope, v):
    bn, L, H, _ = q_nope.shape
    q = jnp.concatenate([q_nope, q_rope], axis=-1)
    k = jnp.concatenate([k_nope, jnp.broadcast_to(k_rope[:, :, None, :], (bn, L, H, B_ROPE))], axis=-1)
    qp, kp, vp = pad_front(q), pad_front(k), pad_front(v)
    Lp = L + PAD
    nqb = Lp // BLOCK_Q
    dqk = q.shape[-1]
    scale = dqk ** -0.5
    key_pos = jnp.arange(Lp)
    key_chunk = key_pos // CHUNK
    key_ok = key_pos >= PAD
    qblocks = qp.reshape(bn, nqb, BLOCK_Q, H, dqk).transpose(1, 0, 2, 3, 4)

    def block(args):
        qblk, i = args
        q_chunk = (i * BLOCK_Q + jnp.arange(BLOCK_Q)) // CHUNK
        allowed = (key_chunk[None, :] <= q_chunk[:, None]) & key_ok[None, :]
        s = jnp.einsum('bqhd,bkhd->bhqk', qblk, kp, preferred_element_type=jnp.float32) * scale
        s = jnp.where(allowed[None, None], s, NEG)
        p = jax.nn.softmax(s, axis=-1)
        return jnp.einsum('bhqk,bkhd->bqhd', p.astype(vp.dtype), vp)

    o = lax.map(block, (qblocks, jnp.arange(nqb)))
    o = o.transpose(1, 0, 2, 3, 4).reshape(bn, Lp, H * B_VDIM)
    return o[:, PAD:]

def setup_inputs(seed: int = 0) -> dict:
    key = jax.random.key(seed)
    ks = jax.random.split(key, 16)
    f32 = jnp.float32
    nrm = lambda k, shape, s: jax.random.normal(k, shape, f32) * s
    return {
        "x": nrm(ks[0], (BATCH, SEQ, D_MODEL), 1.0),
        "meta_tokens": nrm(ks[1], (N_META, D_MODEL), 1.0),
        "norm_w": 1.0 + nrm(ks[2], (DEPTH, D_MODEL), 0.02),
        "w_in": nrm(ks[3], (DEPTH, D_MODEL, IN_TOTAL), D_MODEL ** -0.5),
        "a_sinks": nrm(ks[4], (DEPTH, A_HEADS), 0.5),
        "b_q_norm": 1.0 + nrm(ks[5], (DEPTH, B_Q_RANK), 0.02),
        "b_kv_norm": 1.0 + nrm(ks[6], (DEPTH, B_KV_RANK), 0.02),
        "b_w_uq": nrm(ks[7], (DEPTH, B_Q_RANK, B_HEADS * (B_NOPE + B_ROPE)), B_Q_RANK ** -0.5),
        "b_w_ukv": nrm(ks[8], (DEPTH, B_KV_RANK, B_HEADS * (B_NOPE + B_VDIM)), B_KV_RANK ** -0.5),
        "c_conv_w": nrm(ks[9], (DEPTH, C_CONV, C_WIDTH), C_CONV ** -0.5),
        "d_conv_w": nrm(ks[10], (DEPTH, D_CONV, D_WIDTH), D_CONV ** -0.5),
        "d_conv_b": nrm(ks[11], (DEPTH, D_WIDTH), 0.02),
        "d_ln_w": 1.0 + nrm(ks[12], (DEPTH, D_WIDTH), 0.02),
        "d_ln_b": nrm(ks[13], (DEPTH, D_WIDTH), 0.02),
        "w_out": nrm(ks[14], (DEPTH, D_MIX, D_MODEL), D_MIX ** -0.5),
        "final_norm_w": 1.0 + nrm(ks[15], (D_MODEL,), 0.02),
    }

def reference(x, meta_tokens, norm_w, w_in, a_sinks, b_q_norm, b_kv_norm, b_w_uq, b_w_ukv,
              c_conv_w, d_conv_w, d_conv_b, d_ln_w, d_ln_b, w_out, final_norm_w):
    bn = x.shape[0]
    meta = jnp.broadcast_to(meta_tokens[None].astype(x.dtype), (bn, N_META, D_MODEL))
    h_res = jnp.concatenate([meta, x], axis=1)
    L = h_res.shape[1]
    cos_a, sin_a = rope_tables(L, A_HEAD_DIM)
    cos_b, sin_b = rope_tables(L, B_ROPE)

    for l in range(DEPTH):
        h = rms_norm(h_res, norm_w[l])
        proj = jnp.einsum('bld,de->ble', h, w_in[l])
        (a_q, a_k, a_v, a_g, b_cq, b_ckv, b_kr, b_g,
         c_b, c_c, c_x, c_g, d_u, d_g) = _split(proj, IN_SPLITS)

        qa = apply_rope(a_q.reshape(bn, L, A_HEADS, A_HEAD_DIM), cos_a, sin_a)
        ka = apply_rope(a_k.reshape(bn, L, A_KV_HEADS, A_HEAD_DIM), cos_a, sin_a)
        va = a_v.reshape(bn, L, A_KV_HEADS, A_HEAD_DIM)
        ya = swa_sink_attention(qa, ka, va, a_sinks[l])

        cq = rms_norm(b_cq, b_q_norm[l])
        qm = jnp.einsum('blr,re->ble', cq, b_w_uq[l]).reshape(bn, L, B_HEADS, B_NOPE + B_ROPE)
        qm_nope = qm[..., :B_NOPE]
        qm_rope = apply_rope(qm[..., B_NOPE:], cos_b, sin_b)
        ckv = rms_norm(b_ckv, b_kv_norm[l])
        kvm = jnp.einsum('blr,re->ble', ckv, b_w_ukv[l]).reshape(bn, L, B_HEADS, B_NOPE + B_VDIM)
        km_nope = kvm[..., :B_NOPE]
        vm = kvm[..., B_NOPE:]
        km_rope = apply_rope(b_kr[:, :, None, :], cos_b, sin_b)[:, :, 0]
        yb = mla_attention(qm_nope, qm_rope, km_nope, km_rope, vm)

        yc = c_b * causal_dwconv(c_c * c_x, c_conv_w[l])

        d_a, d_gl = jnp.split(d_u, 2, axis=-1)
        ud = causal_dwconv(d_a * jax.nn.sigmoid(d_gl), d_conv_w[l]) + d_conv_b[l].astype(x.dtype)
        yd = jax.nn.silu(layer_norm(ud, d_ln_w[l], d_ln_b[l]))

        mixed = jnp.concatenate([ya * jax.nn.silu(a_g), yb * jax.nn.silu(b_g),
                                 yc * jax.nn.silu(c_g), yd * jax.nn.silu(d_g)], axis=-1)
        h_res = h_res + jnp.einsum('ble,ed->bld', mixed, w_out[l])

    out = rms_norm(h_res, final_norm_w)
    return out[:, N_META:]


_drawn_inputs = setup_inputs


def setup_inputs(seed=0):
    import zlib

    import numpy as np

    out = dict(_drawn_inputs(seed))
    spreads = {}
    factors = {'norm_w': 3.034,
     'a_sinks': 64.0,
     'b_q_norm': 8.0,
     'b_kv_norm': 8.0,
     'd_conv_b': 5.924,
     'd_ln_w': 46.066,
     'd_ln_b': 43.233,
     'final_norm_w': 7.541}
    for name, (base, spread) in spreads.items():
        noise = np.random.default_rng([zlib.crc32(name.encode()), seed]).standard_normal(out[name].shape)
        drawn = base * np.exp(spread * noise) if base else spread * noise
        out[name] = __import__('jax').numpy.asarray(drawn.astype(out[name].dtype))
    for name, factor in factors.items():
        out[name] = (out[name] * factor).astype(out[name].dtype)
    return out
```

```python
import numpy as np
import concourse.bass as bass
import concourse.mybir as mybir
from concourse.alu_op_type import AluOpType as ALU
from contextlib import ExitStack

ACT = mybir.ActivationFunctionType
AX = mybir.AxisListType.X
F32 = mybir.dt.float32
F32R = mybir.dt.float32r

P = 128
D_MODEL = 2048
DEPTH = 2
META = 16
CHUNK = 64
TOK = 272
KT = D_MODEL // P
GT = KT // 4
UNIT = 1024
HALF = UNIT // P
RING = 4
UNITS = 132
OUTS = 78
EPS = 1e-6
NEG = -1e30
D_TAPS = 31
D_PAD = D_TAPS - 1
C_TAPS = 3
C_PAD = C_TAPS - 1
A_SCALE = 64 ** -0.5
B_SCALE = 192 ** -0.5
B_HEADS = 4
FIRST = 4

OUT_D, OUT_B, OUT_BG, OUT_KR, OUT_QR, OUT_QN, OUT_KN, OUT_V, OUT_A, OUT_C, OUT_O = \
    0, 12, 18, 22, 23, 25, 29, 33, 36, 46, 62
U_KR, U_UQ = 44, 45

B_Q0, B_Q1, B_TAIL, TAIL_M = (0, 128, 144), (128, 128, 272), 240, 32


def flat(ap):
    return ap.rearrange("p a b -> p (a b)")


def out_of_unit(u):
    if u < U_KR:
        return u // 2
    if u < U_UQ + 3:
        return OUT_KR + 2 * (u - U_KR)
    return (u + 24) // 2


class Signal:

    def __init__(self, sem, per, credit=0):
        self.sem, self.per, self.credit = sem, per, credit

    def at(self, layer, k):
        return layer * self.per + (k + self.credit)


def build(nc, stream, ukv_d, x_d, norms_d, bnorm_d, dconv_d, cconv_d, dvec_d, sinks_d, sinks_m_d,
          rope_d, mask_d, mats_d, out_d):
    ctx = ExitStack()
    with ctx:
        def sb(name, shape, dt=F32):
            return ctx.enter_context(nc.sbuf_tensor(name, shape, dt))

        def bank(name):
            return ctx.enter_context(nc.psum_tensor(name, [P, 512], F32))

        def sem(name):
            return ctx.enter_context(nc.semaphore(name))

        def signal(name, per, credit=0):
            return Signal(sem(name), per, credit)

        resid = sb("resid", [P, KT, TOK])
        h_hi = sb("h_hi", [P, KT, TOK], F32R)
        h_lo = sb("h_lo", [P, KT, TOK], F32R)
        mix_hi = sb("mix_hi", [P, KT, TOK], F32R)
        mix_lo = sb("mix_lo", [P, KT, TOK], F32R)
        raw_w = sb("raw_w", [P, RING, UNIT])
        w_hi = sb("w_hi", [P, RING, UNIT], F32R)
        w_lo = sb("w_lo", [P, RING, UNIT], F32R)
        rstd = sb("rstd", [P, TOK])
        lat_rstd = sb("lat_rstd", [P, 2, TOK])
        u_pad = sb("u_pad", [P, GT, D_PAD + TOK])
        conv = sb("conv", [P, GT, TOK])
        conv_tmp = sb("conv_tmp", [P, GT, TOK])
        gate_d = sb("gate_d", [P, GT, TOK])
        gate_ab = sb("gate_ab", [P, 2, GT, TOK])
        work = sb("work", [P, 8, TOK])
        q_nope = sb("q_nope", [P, GT, TOK])
        k_nope = sb("k_nope", [P, GT, TOK])
        q_rope = sb("q_rope", [64 + 5, B_HEADS, TOK])
        k_rope = sb("k_rope", [64 + 5, TOK])
        v_b = sb("v_b", [P, 3, B_HEADS * P])
        attn = sb("attn", [P, 2, UNIT])
        meta_p = sb("meta_p", [P, 2 * META])
        y_tmp = sb("y_tmp", [P, 2, TOK])
        c_pad = sb("c_pad", [P, C_PAD + TOK])
        norms = sb("norms", [P, DEPTH + 1, KT])
        bnorm = sb("bnorm", [P, DEPTH, 6])
        dconv = sb("dconv", [P, DEPTH * GT, D_TAPS])
        cconv = sb("cconv", [P, DEPTH * GT, C_TAPS])
        dvec = sb("dvec", [P, DEPTH, 3, GT])
        sink = sb("sink", [P, DEPTH, 4])
        sink_m = sb("sink_m", [P, DEPTH, 2])
        nsink = sb("nsink", [P, DEPTH, 4])
        nsink_m = sb("nsink_m", [P, DEPTH, 2])
        rope = sb("rope", [P, 2, TOK])
        mats = sb("mats", [P, 3, P])
        eps = sb("eps", [P, 1])
        mx = sb("mx", [P, 8])
        nm = sb("nm", [P, 8])
        rs = sb("rs", [P, 8])
        es = sb("es", [P, 8])
        rd = sb("rd", [P, 8])

        first = slice(FIRST, FIRST + 2)
        meta_o = sb("meta_o", [P, 64])

        ident, ones, rotate = mats[:, 0, :], mats[:, 1, :], mats[:, 2, :]
        cos, sin = rope[:, 0, :], rope[:, 1, :]
        prob = attn[:, 0, :].rearrange("p (b n) -> p b n", b=2)
        prob_t = attn[:, 1, :]
        tail_p, tail_t = work[:, 6, :], work[:, 7, :]
        tail_v = prob_t[0:META, 5 * P:6 * P]
        sumsq = rot_tmp = lat_rstd[:, 1, :]
        meta_t = lat_rstd[0:META, 1, 0:2 * P]
        a_q, a_k = q_nope[:, :, :].rearrange("p t n -> p (t n)"), k_nope[:, 0:2, :]
        a_q_chunks = a_q[:, 4 * META:].rearrange("p (g c i q) -> p g i c q", g=2, c=4, i=2)
        a_v = k_nope[:, 2:4, :].rearrange("p t n -> p (t n)")[:, 0:4 * P].rearrange("p (c n) -> p c n", c=4)
        lat_sq_q = gate_ab[:, 0, :, :]
        lat_sq_kv = q_nope[:, 0:2, :]

        main = [bank("main0"), bank("main1")]
        stat = bank("stat")
        score = [bank("score0"), bank("score1")]
        turn_a, turn_b = bank("turn_a"), bank("turn_b")
        outp = bank("outp")

        ln_stat = stat[:, 64:64 + TOK]

        x_in = [sem(f"x_in{i}") for i in range(4)]
        const_in = [sem(f"const_in{i}") for i in range(15)]
        landed = [signal(f"landed{i}", 16 * UNITS // RING) for i in range(RING)]
        ukv_in = signal("ukv_in", 16)
        hi_done = signal("hi_done", UNITS)
        split_done = signal("split_done", UNITS)
        out_done = signal("out_done", OUTS, 2)
        evacuated = signal("evacuated", OUTS, 2)
        h_hi_done = signal("h_hi_done", KT)
        h_lo_done = signal("h_lo_done", KT)
        sq_done = signal("sq_done", 2 * KT - 1)
        norm_sum = signal("norm_sum", 1)
        norm_root = signal("norm_root", 1)
        norm_done = signal("norm_done", 1)
        glu_gate = signal("glu_gate", GT)
        glu_done = signal("glu_done", GT)
        gate_done = signal("gate_done", 4 * GT)
        tap_done = signal("tap_done", 2 * D_TAPS)
        lat_sq = signal("lat_sq", 2)
        lat_sum = signal("lat_sum", 2)
        lat_root = signal("lat_root", 2)
        lat_recip = signal("lat_recip", 2)
        lat_norm = signal("lat_norm", 6)
        lat_hi = signal("lat_hi", 4)
        lat_lo = signal("lat_lo", 4)
        rotated = signal("rotated", 8)
        rope_cos = signal("rope_cos", 8)
        rope_sin = signal("rope_sin", 8)
        roped = signal("roped", 5 + 2 * 4 + 4)
        b_score = signal("b_score", 5)
        b_max = signal("b_max", 9)
        b_negmax = signal("b_negmax", 5)
        b_exp = signal("b_exp", 9)
        b_recip = signal("b_recip", 5)
        b_prob = signal("b_prob", 9)
        b_turned = signal("b_turned", 5)
        b_turn_copied = signal("b_turn_copied", 14)
        b_pv = signal("b_pv", 4)
        v_turned = signal("v_turned", 1)
        v_copied = signal("v_copied", 2)
        a_score = signal("a_score", 5)
        a_max = signal("a_max", 9)
        a_negmax = signal("a_negmax", 5)
        a_sinkarg = signal("a_sinkarg", 1)
        a_exp = signal("a_exp", 2 + 1 + 4 * 5)
        a_den = signal("a_den", 5)
        a_recip = signal("a_recip", 5)
        a_prob = signal("a_prob", 9)
        a_turned = signal("a_turned", 5)
        a_turn_copied = signal("a_turn_copied", 1 + 4 * 3)
        a_meta_pv = signal("a_meta_pv", 1)
        a_pv = signal("a_pv", 4)
        ln_pre = signal("ln_pre", 6)
        ln_sum = signal("ln_sum", 1)
        ln_mean = signal("ln_mean", 1)
        ln_center = signal("ln_center", 1)
        ln_sq = signal("ln_sq", 1)
        ln_var = signal("ln_var", 1)
        ln_root = signal("ln_root", 1)
        ln_recip = signal("ln_recip", 1)
        ln_scaled = signal("ln_scaled", 1)
        ln_silu = signal("ln_silu", GT)
        c_prod = signal("c_prod", GT)
        c_step = signal("c_step", 4 * GT)
        y_parts = signal("y_parts", GT)
        meta_out = signal("meta_out", 1)
        y_done = signal("y_done", KT)
        y_hi = signal("y_hi", KT)
        mix_done = signal("mix_done", KT)
        zeroed = sem("zeroed")
        nsink_done = sem("nsink_done")
        final_done = sem("final_done")
        out_sent = [sem(f"out_sent{i}") for i in range(4)]

        MIX_D, MIX_B, MIX_A, MIX_C = 0, GT, 2 * GT, 3 * GT
        Y_B_LAST, Y_A1 = 4, 8

        block = ctx.enter_context(nc.Block())

        @block.sync
        def _(sp):
            def fetch(turn, slot):
                sp.dma_start(raw_w[:, slot, :], stream[bass.ds(turn, 1), slot, :, :].rearrange("u p n -> p (u n)")).then_inc(landed[slot].sem, 16)

            def const(i, dst, src):
                sp.dma_start(dst, src).then_inc(const_in[i], 16)

            const(0, norms[:, :, :], norms_d)
            for q in range(4):
                sp.dma_start(resid[:, 4 * q:4 * q + 4, :], x_d[:, 4 * q:4 * q + 4, :]).then_inc(x_in[q], 16)
                fetch(0, q)
            const(1, mats[:, :, :], mats_d)
            const(2, bnorm[:, :, :], bnorm_d)
            const(3, dconv[:, :, :], dconv_d)
            const(4, cconv[:, :, :], cconv_d)
            const(5, dvec[:, :, :, :], dvec_d)
            const(6, rope[:, :, :], rope_d)
            const(7, k_rope[64:69, :], mask_d[:, 1, :])
            const(14, q_rope[64:69, :, :], mask_d[:, 0:1, :].broadcast_to([5, B_HEADS, TOK]))
            for i in range(2):
                const(8 + i, sink[64 * i:64 * i + 64, :, :].rearrange("p l c -> p (l c)"),
                      sinks_d[i:i + 1, :].broadcast_to([64, DEPTH * 4]))
            for i in range(4):
                const(10 + i, sink_m[32 * i:32 * i + 32, :, :].rearrange("p l g -> p (l g)"),
                      sinks_m_d[i:i + 1, :].broadcast_to([32, DEPTH * 2]))
            with sp.Fori(1, DEPTH * UNITS // RING) as turn:
                for s in range(RING):
                    sp.wait_ge(split_done.sem, (turn - 1) * RING + (s + 1))
                    fetch(turn, s)
            for q in range(4):
                sp.wait_ge(final_done, 4 * q + 4)
                sp.dma_start(out_d[:, 4 * q:4 * q + 4, :], resid[:, 4 * q:4 * q + 4, META:TOK]
                             ).then_inc(out_sent[q], 16)
            for q in range(4):
                sp.wait_ge(out_sent[q], 16)

        @block.tensor
        def _(pe):
            mm = nc.tensor.matmul

            def split_product(dst, pairs, last):
                n = len(pairs)
                for i, (whi, wlo, xhi, xlo) in enumerate(pairs):
                    mm(dst, wlo, xhi, start=(i == 0 and last[0]), stop=False)
                    mm(dst, whi, xlo, start=False, stop=False)
                    ins = mm(dst, whi, xhi, start=False, stop=(i == n - 1 and last[1]))
                return ins

            def tile(l, out, u, b, slot, hi, lo, ready=None):
                pe.wait_ge(evacuated.sem, evacuated.at(l, out - 1))
                for half in range(2):
                    pe.wait_ge(split_done.sem, split_done.at(l, u + (half + 1)))
                    s = slot + half
                    for kk in range(HALF):
                        k = half * HALF + kk
                        if ready:
                            ready(k)
                        c = slice(kk * P, kk * P + P)
                        ins = split_product(main[b][:, 0:TOK],
                                            [(w_hi[:, s, c], w_lo[:, s, c], hi[:, k, :], lo[:, k, :])],
                                            (k == 0, k == KT - 1))
                ins.then_inc(out_done.sem, 1)

            def pair(l, out, u, hi, lo, ready=None, between=None):
                tile(l, out, u, 0, 0, hi, lo, ready)
                if between:
                    pe.wait_ge(*between)
                tile(l, out + 1, u + 2, 1, 2, hi, lo)

            def norm_stat(l):
                pe.wait_ge(sq_done.sem, sq_done.at(l, 2 * KT - 1))
                mm(stat[:, 0:TOK], ones, sumsq[:, :], start=True, stop=True).then_inc(norm_sum.sem, 1)

            def main_out(l, out, rows=P, n=TOK):
                pe.wait_ge(evacuated.sem, evacuated.at(l, out - 1))
                return main[out % 2][0:rows, 0:n]

            def b_up(l):
                dst = main_out(l, OUT_KR, 64)
                pe.wait_ge(split_done.sem, split_done.at(l, U_KR + 1))
                split_product(dst, [(w_hi[:, 0, 64 * k:64 * k + 64], w_lo[:, 0, 64 * k:64 * k + 64],
                                     h_hi[:, k, :], h_lo[:, k, :]) for k in range(KT)],
                              (True, True)).then_inc(out_done.sem, 1)
                pe.wait_ge(lat_lo.sem, lat_lo.at(l, 4))
                for n in range(6):
                    out = OUT_QR + n
                    s = 1 + n // 2
                    dst = main_out(l, out)
                    pe.wait_ge(split_done.sem, split_done.at(l, U_UQ + n // 2 + 1))
                    cols = [slice(256 * k + P * (n % 2), 256 * k + P * (n % 2) + P) for k in range(GT)]
                    split_product(dst, [(w_hi[:, s, c], w_lo[:, s, c], mix_hi[:, MIX_C + k, :], mix_lo[:, MIX_C + k, :])
                                        for k, c in enumerate(cols)], (True, True)).then_inc(out_done.sem, 1)
                pe.wait_ge(lat_norm.sem, lat_norm.at(l, 6))
                pe.wait_ge(ukv_in.sem, ukv_in.at(l, 16))
                for h in range(B_HEADS):
                    dst = main_out(l, OUT_KN + h)
                    for k in range(2):
                        ins = mm(dst, attn[:, k, P * h:P * h + P], work[:, 4 + k, :], start=(k == 0), stop=(k == 1))
                    ins.then_inc(out_done.sem, 1)
                for t in range(3):
                    rows = min(P, TOK - P * t)
                    dst = main_out(l, OUT_V + t, rows, 512)
                    for k in range(2):
                        ins = mm(dst, work[:, 4 + k, P * t:P * t + rows], attn[:, k, 512:1024],
                                 start=(k == 0), stop=(k == 1))
                    ins.then_inc(out_done.sem, 1)
                pe.wait_ge(evacuated.sem, evacuated.at(l, OUT_QR + 2))
                for dst, src, r in ((score[0], 0, P), (score[1], 1, P), (stat, 6, 64)):
                    mm(dst[0:r, 0:TOK], rotate[0:r, 0:r], work[0:r, src, :], start=True, stop=True).then_inc(rotated.sem, 1)

            def b_tail_scores(l):
                pe.wait_ge(roped.sem, roped.at(l, 5))
                pe.wait_ge(evacuated.sem, evacuated.at(l, OUT_V + 3))
                for h in range(B_HEADS):
                    dst = turn_b[32 * h:32 * h + 32, 0:TOK]
                    mm(dst, q_nope[:, h, B_TAIL:TOK], k_nope[:, h, :], start=True, stop=False)
                    ins = mm(dst, q_rope[0:64, h, B_TAIL:TOK], k_rope[0:64, :], start=False, stop=True)
                ins.then_inc(b_score.sem, 1)

            def b_scores(l, h):
                if h >= 2:
                    pe.wait_ge(b_exp.sem, b_exp.at(l, 2 * h - 1))
                for (q0, n, keys), at in ((B_Q0, 0), (B_Q1, B_Q0[2])):
                    dst = score[h % 2][:, at:at + keys]
                    mm(dst, q_nope[:, h, q0:q0 + n], k_nope[:, h, 0:keys], start=True, stop=False)
                    ins = mm(dst, q_rope[:, h, q0:q0 + n], k_rope[:, 0:keys], start=False, stop=True)
                ins.then_inc(b_score.sem, 1)

            def b_turn_tail(l):
                pe.wait_ge(b_prob.sem, b_prob.at(l, 1))
                nc.tensor.transpose(turn_a[:, 0:P], tail_p[:, 0:P], ident)
                nc.tensor.transpose(turn_a[:, P:2 * P], tail_p[:, P:2 * P], ident)
                nc.tensor.transpose(turn_a[0:META, 2 * P:3 * P], tail_p[:, 2 * P:TOK], ident).then_inc(b_turned.sem, 1)

            def b_turn(l, h):
                pe.wait_ge(b_prob.sem, b_prob.at(l, 3 + 2 * h))
                pe.wait_ge(b_turn_copied.sem, b_turn_copied.at(l, 2 + 3 * h))
                p = prob[:, h % 2, :]
                nc.tensor.transpose(turn_a[:, 0:P], p[:, 0:P], ident)
                nc.tensor.transpose(turn_a[:, P:2 * P], p[:, 144:144 + P], ident)
                nc.tensor.transpose(turn_a[:, 2 * P:3 * P], p[:, 144 + P:144 + 2 * P], ident)
                nc.tensor.transpose(turn_a[0:META, 3 * P:4 * P], p[:, P:144], ident)
                nc.tensor.transpose(turn_b[0:META, 0:P], p[:, 144 + 2 * P:144 + TOK], ident).then_inc(b_turned.sem, 1)

            def b_values(l, h):
                pe.wait_ge(b_turn_copied.sem, b_turn_copied.at(l, 2 + 3 * (h + 1)))
                if h:
                    pe.wait_ge(y_done.sem, y_done.at(l, h))
                v = [v_b[0:rows, t, P * h:P * h + P] for t, rows in ((0, P), (1, P), (2, META))]
                c = slice(32 * h + 16, 32 * h + 32)
                groups = (((0, P), (v[0], prob_t[:, 0:P]), (v_b[0:META, 1, P * h:P * h + P], prob_t[0:META, 3 * P:4 * P])),
                          ((P, 2 * P), (v[0], prob_t[:, P:2 * P]), (v[1], prob_t[:, 2 * P:3 * P]),
                           (v[2], prob_t[0:META, 4 * P:5 * P])),
                          ((2 * P, TOK), (v[0], tail_t[:, c]), (v[1], tail_t[:, P + c.start:P + c.stop]),
                           (v[2], tail_v[:, c])))
                for (a, b), *terms in groups:
                    for i, (val, pt) in enumerate(terms):
                        ins = mm(outp[:, a:b], val, pt, start=(i == 0), stop=(i == len(terms) - 1))
                ins.then_inc(b_pv.sem, 1)

            def a_rotate(l, n):
                if n in (0, 1):
                    pe.wait_ge(b_exp.sem, b_exp.at(l, 9))
                if n in (2, 3):
                    pe.wait_ge(roped.sem, roped.at(l, 5 + 2 * (n - 1)))
                if n == 4:
                    pe.wait_ge(evacuated.sem, evacuated.at(l, OUT_A + 6))
                dst = stat if n == 4 else score[n % 2]
                mm(dst[:, 0:TOK], rotate, work[:, n, :], start=True, stop=True).then_inc(rotated.sem, 1)

            def a_turn_values(l):
                pe.wait_ge(b_turn_copied.sem, b_turn_copied.at(l, 14))
                nc.tensor.transpose(turn_a[0:80, 0:P], work[:, 5, 0:80], ident)
                for c in range(3):
                    ins = nc.tensor.transpose(turn_a[:, P * (c + 1):P * (c + 2)],
                                              work[:, 5, META + CHUNK * c:META + CHUNK * c + P], ident)
                ins.then_inc(v_turned.sem, 1)

            def a_meta_scores(l):
                for g in range(2):
                    for i in range(4):
                        r = slice(64 * (i % 2), 64 * (i % 2) + 64)
                        ins = mm(score[0][32 * i:32 * i + 32, META * g:META * g + META],
                                 a_q[r, META * (2 * g + i // 2):META * (2 * g + i // 2) + 32], a_k[r, g, 0:META], start=True, stop=True)
                ins.then_inc(a_score.sem, 1)

            def a_scores(l, n):
                g, par = divmod(n - 1, 2)
                if n >= 2:
                    pe.wait_ge(a_exp.sem, a_exp.at(l, 3 + 5 * (n - 2)))
                r = slice(64 * par, 64 * par + 64)
                dst = score[n % 2]
                queries = [a_q[r, 4 * META + 512 * g + P * c:4 * META + 512 * g + P * c + P] for c in range(4)]
                mm(dst[:, 0:80], queries[0], a_k[r, g, 0:80], start=True, stop=True)
                for c in range(3):
                    at = 80 + 144 * c
                    mm(dst[:, at:at + META], queries[c + 1], a_k[r, g, 0:META], start=True, stop=True)
                    k0 = META + CHUNK * c
                    ins = mm(dst[:, at + META:at + 144], queries[c + 1], a_k[r, g, k0:k0 + P],
                             start=True, stop=True)
                ins.then_inc(a_score.sem, 1)

            def a_turn_meta(l):
                pe.wait_ge(a_prob.sem, a_prob.at(l, 1))
                for g in range(2):
                    ins = nc.tensor.transpose(turn_b[0:META, P * g:P * g + P], meta_p[:, META * g:META * g + META], ident)
                ins.then_inc(a_turned.sem, 1)

            def a_meta_values(l):
                pe.wait_ge(a_turn_copied.sem, a_turn_copied.at(l, 1))
                pe.wait_ge(v_copied.sem, v_copied.at(l, 2))
                pe.wait_ge(ln_root.sem, ln_root.at(l, 1))
                for g in range(2):
                    for par in range(2):
                        pt = meta_t[:, P * g:P * g + P].rearrange("p (i r q) -> p r i q", i=2, r=2)[:, par, :, 0:META]
                        ins = mm(stat[64 * par:64 * par + 64, 32 * g:32 * g + 32], a_v[0:META, 0, 64 * g:64 * g + 64], pt,
                                 start=True, stop=True)
                ins.then_inc(a_meta_pv.sem, 1)

            def a_turn(l, n):
                pe.wait_ge(a_prob.sem, a_prob.at(l, 1 + 2 * n))
                pe.wait_ge(a_turn_copied.sem, a_turn_copied.at(l, 1 + 3 * (n - 1)))
                p = prob[:, n % 2, :]
                nc.tensor.transpose(turn_a[0:80, 0:P], p[:, 0:80], ident)
                for c in range(3):
                    at = 80 + 144 * c
                    nc.tensor.transpose(turn_a[:, P * (c + 1):P * (c + 2)], p[:, at + META:at + 144], ident)
                    ins = nc.tensor.transpose(turn_b[0:META, P * c:P * c + P], p[:, at:at + META], ident)
                ins.then_inc(a_turned.sem, 1)

            def a_values(l, n):
                g, par = divmod(n - 1, 2)
                pe.wait_ge(a_turn_copied.sem, a_turn_copied.at(l, 1 + 3 * n))
                r, cols = slice(64 * par, 64 * par + 64), slice(64 * g, 64 * g + 64)
                if n == 1:
                    pe.wait_ge(y_done.sem, y_done.at(l, Y_B_LAST))
                if n == 3:
                    pe.wait_ge(y_done.sem, y_done.at(l, Y_A1))
                mm(outp[r, 0:P], a_v[0:80, 0, cols], prob_t[0:80, 0:P], start=True, stop=True)
                for c in range(3):
                    d = outp[r, P * (c + 1):P * (c + 2)]
                    mm(d, a_v[:, c + 1, cols], prob_t[:, P * (c + 1):P * (c + 2)], start=True, stop=False)
                    ins = mm(d, a_v[0:META, 0, cols], prob_t[0:META, 512 + P * c:512 + P * c + P], start=False, stop=True)
                ins.then_inc(a_pv.sem, 1)

            def feature_sum(tiles, dst, sig):
                for i, t in enumerate(tiles):
                    ins = mm(dst, ones, t, start=(i == 0), stop=(i == len(tiles) - 1))
                ins.then_inc(sig.sem, 1)

            pe.sem_inc(out_done.sem, 2)
            pe.wait_ge(const_in[1], 16)
            pe.wait_ge(const_in[7], 16)
            pe.wait_ge(const_in[14], 16)
            with pe.Fori(0, DEPTH) as l:
                def resid_ready(k):
                    pe.wait_ge(h_lo_done.sem, h_lo_done.at(l, k + 1))
                    if k == HALF:
                        norm_stat(l)
                pair(l, OUT_D, 0, h_hi, h_lo, resid_ready)
                with pe.Fori(1, 6) as i:
                    pair(l, 2 * i, 4 * i, h_hi, h_lo)
                with pe.Fori(0, 3) as i:
                    pair(l, OUT_B + 2 * i, 2 * OUT_B + 4 * i, h_hi, h_lo)
                pair(l, OUT_BG, 2 * OUT_BG, h_hi, h_lo)
                pe.wait_ge(lat_sq.sem, lat_sq.at(l, 2))
                feature_sum([lat_sq_q[:, t, :] for t in range(4)], stat[:, 0:TOK], lat_sum)
                feature_sum([lat_sq_kv[:, t, :] for t in range(2)], score[0][:, 0:TOK], lat_sum)
                pair(l, OUT_BG + 2, 2 * OUT_BG + 4, h_hi, h_lo)
                b_up(l)
                for i in range(5):
                    pair(l, OUT_A + 2 * i, 48 + 4 * i, h_hi, h_lo)
                    if i == 0:
                        b_tail_scores(l)
                    if i < 4:
                        b_scores(l, i)
                    if i == 1:
                        b_turn_tail(l)
                    if i >= 1:
                        b_turn(l, i - 1)
                    if i >= 2:
                        b_values(l, i - 2)
                a_rotate(l, 0)
                a_rotate(l, 1)
                for i in range(8):
                    pair(l, OUT_C + 2 * i, 68 + 4 * i, h_hi, h_lo,
                         between=(roped.sem, roped.at(l, 17)) if i == 1 else None)
                    if i == 0:
                        b_values(l, 3)
                        for n in (2, 3, 4):
                            a_rotate(l, n)
                        a_turn_values(l)
                    if i == 1:
                        a_meta_scores(l)
                    if 1 <= i <= 4:
                        a_scores(l, i)
                    if i == 2:
                        a_turn_meta(l)
                    if 2 <= i <= 5:
                        a_turn(l, i - 1)
                    if i == 4:
                        a_meta_values(l)
                    if 3 <= i <= 6:
                        a_values(l, i - 2)
                    if i == 1:
                        pe.wait_ge(ln_pre.sem, ln_pre.at(l, 3))
                        feature_sum([conv_tmp[:, 0, :]], ln_stat, ln_sum)
                    if i == 3:
                        pe.wait_ge(ln_pre.sem, ln_pre.at(l, 6))
                        feature_sum([conv_tmp[:, 0, :]], ln_stat, ln_var)
                def mix_ready(k):
                    if k == 0:
                        pe.wait_ge(mix_done.sem, mix_done.at(l, KT - 1))
                    if k == KT - 1:
                        pe.wait_ge(mix_done.sem, mix_done.at(l, KT))
                pair(l, OUT_O, 100, mix_hi, mix_lo, mix_ready)
                with pe.Fori(1, 8) as i:
                    pair(l, OUT_O + 2 * i, 100 + 4 * i, mix_hi, mix_lo)
            norm_stat(DEPTH)

        @block.scalar
        def _(act):
            fn = nc.scalar.activation

            def hi(l, u, slot, freed):
                act.wait_ge(landed[slot].sem, landed[slot].at(l, 4 * (u - slot) + 16))
                act.wait_ge(out_done.sem, out_done.at(l, freed + 1))
                nc.scalar.copy(w_hi[:, slot, :], raw_w[:, slot, :]).then_inc(hi_done.sem, 1)

            def ahead(l, out, u, slot):
                hi(l, u, slot, out - 1)
                hi(l, u + 1, slot + 1, out - 1)

            def root(dst, src, n, done, wait):
                act.wait_ge(wait[0], wait[1])
                fn(dst, src, ACT.Sqrt, bias=eps[:, 0:1], scale=1.0 / n).then_inc(done.sem, 1)

            def norm_root_of(l):
                root(rstd[:, :], stat[:, 0:TOK], D_MODEL, norm_root, (norm_sum.sem, norm_sum.at(l, 1)))

            def silu(l, out, dst):
                act.wait_ge(evacuated.sem, evacuated.at(l, out + 1))
                fn(dst, dst, ACT.Silu).then_inc(gate_done.sem, 1)

            seq = [0]

            def mix_high(l, place):
                k = seq[0]
                seq[0] += 1
                act.wait_ge(y_done.sem, y_done.at(l, k + 1))
                nc.scalar.copy(mix_hi[:, place, :], y_tmp[:, k % 2, :]).then_inc(y_hi.sem, 1)

            def b_exps(l, n):
                act.wait_ge(b_negmax.sem, b_negmax.at(l, n + 1))
                if n == 0:
                    fn(tail_p, turn_b[:, 0:TOK], ACT.Exp, bias=nm[:, FIRST:FIRST + 1], scale=B_SCALE,
                       accum_out=rs[:, FIRST:FIRST + 1]).then_inc(b_exp.sem, 1)
                    return
                h = n - 1
                if h >= 2:
                    act.wait_ge(b_turned.sem, b_turned.at(l, h))
                for j, (a, b) in enumerate(((0, 144), (144, 144 + TOK))):
                    fn(prob[:, h % 2, a:b], score[h % 2][:, a:b], ACT.Exp, bias=nm[:, j:j + 1], scale=B_SCALE,
                       accum_out=rs[:, j:j + 1]).then_inc(b_exp.sem, 1)

            def b_copy_tail(l):
                act.wait_ge(b_turned.sem, b_turned.at(l, 1))
                nc.scalar.copy(tail_t[:, 0:2 * P], turn_a[:, 0:2 * P]).then_inc(b_turn_copied.sem, 1)
                nc.scalar.copy(tail_v, turn_a[0:META, 2 * P:3 * P]).then_inc(b_turn_copied.sem, 1)

            def b_copy(l, h):
                act.wait_ge(b_turned.sem, b_turned.at(l, h + 2))
                if h:
                    act.wait_ge(b_pv.sem, b_pv.at(l, h))
                nc.scalar.copy(prob_t[:, 0:3 * P], turn_a[:, 0:3 * P]).then_inc(b_turn_copied.sem, 1)
                nc.scalar.copy(prob_t[0:META, 3 * P:4 * P], turn_a[0:META, 3 * P:4 * P]).then_inc(b_turn_copied.sem, 1)
                nc.scalar.copy(prob_t[0:META, 4 * P:5 * P], turn_b[0:META, 0:P]).then_inc(b_turn_copied.sem, 1)

            def a_exps(l, n):
                act.wait_ge(a_negmax.sem, a_negmax.at(l, n + 1))
                if n == 0:
                    for g in range(2):
                        c = slice(META * g, META * g + META)
                        fn(meta_p[:, c], score[0][:, c], ACT.Exp, bias=nm[:, FIRST + g:FIRST + g + 1], scale=A_SCALE,
                           accum_out=rs[:, FIRST + g:FIRST + g + 1]).then_inc(a_exp.sem, 1)
                    act.wait_ge(a_sinkarg.sem, a_sinkarg.at(l, 1))
                    fn(es[:, first], es[:, first], ACT.Exp).then_inc(a_exp.sem, 1)
                    return
                if n >= 3:
                    act.wait_ge(a_turned.sem, a_turned.at(l, n - 1))
                for c in range(4):
                    a, b = (0, 80) if c == 0 else (80 + 144 * (c - 1), 80 + 144 * c)
                    fn(prob[:, n % 2, a:b], score[n % 2][:, a:b], ACT.Exp, bias=nm[:, c:c + 1], scale=A_SCALE,
                       accum_out=rs[:, c:c + 1]).then_inc(a_exp.sem, 1)
                fn(es[:, 0:4], nm[:, 0:4], ACT.Exp, bias=sink[:, bass.ds(l, 1), n - 1:n].rearrange("p a b -> p (a b)")
                   ).then_inc(a_exp.sem, 1)

            def a_copy(l, n):
                act.wait_ge(a_turned.sem, a_turned.at(l, n + 1))
                if n == 0:
                    act.wait_ge(ln_center.sem, ln_center.at(l, 1))
                    nc.scalar.copy(meta_t, turn_b[0:META, 0:2 * P]).then_inc(a_turn_copied.sem, 1)
                    return
                if n >= 2:
                    act.wait_ge(a_pv.sem, a_pv.at(l, n - 1))
                nc.scalar.copy(prob_t[:, P:4 * P], turn_a[:, P:4 * P]).then_inc(a_turn_copied.sem, 1)
                nc.scalar.copy(prob_t[0:80, 0:P], turn_a[0:80, 0:P]).then_inc(a_turn_copied.sem, 1)
                nc.scalar.copy(prob_t[0:META, 512:512 + 3 * P], turn_b[0:META, 0:3 * P]).then_inc(a_turn_copied.sem, 1)

            act.wait_ge(const_in[0], 16)
            for k in range(KT):
                if k % 4 == 0:
                    act.wait_ge(x_in[k // 4], 16)
                fn(h_hi[:, k, :], resid[:, k, :], ACT.Copy, scale=norms[:, 0, k:k + 1]).then_inc(h_hi_done.sem, 1)
            act.wait_ge(const_in[5], 16)
            for i in range(8, 14):
                act.wait_ge(const_in[i], 16)
            act.wait_ge(zeroed, 1)
            with act.Fori(0, DEPTH) as l:
                seq[0] = 0
                hi(l, 0, 0, -2)
                hi(l, 1, 1, -2)
                ahead(l, 0, 2, 2)
                norm_root_of(l)
                ahead(l, 1, 4, 0)
                act.dma_start(attn[:, :, :], ukv_d[bass.ds(l, 1), :, :, :].rearrange("l p k n -> p (l k) n")).then_inc(ukv_in.sem, 16)
                def sigmoid(t):
                    act.wait_ge(evacuated.sem, evacuated.at(l, 2 * t + 2))
                    fn(work[:, 1, :], work[:, 1, :], ACT.Sigmoid).then_inc(glu_gate.sem, 1)
                sigmoid(0)
                with act.Fori(1, 4) as i:
                    ahead(l, 2 * i, 4 * i + 2, 2)
                    ahead(l, 2 * i + 1, 4 * i + 4, 0)
                    sigmoid(i)
                with act.Fori(0, 2) as i:
                    ahead(l, 8 + 2 * i, 18 + 4 * i, 2)
                    silu(l, 8 + 2 * i, flat(gate_d[:, bass.ds(2 * i, 1), :]))
                    ahead(l, 9 + 2 * i, 20 + 4 * i, 0)
                    silu(l, 9 + 2 * i, flat(gate_d[:, bass.ds(2 * i + 1, 1), :]))
                with act.Fori(0, 3) as i:
                    ahead(l, OUT_B + 2 * i, 26 + 4 * i, 2)
                    ahead(l, OUT_B + 1 + 2 * i, 28 + 4 * i, 0)
                act.wait_ge(evacuated.sem, evacuated.at(l, OUT_B + 4))
                fn(lat_sq_q, work[:, 0:4, :], ACT.Square).then_inc(lat_sq.sem, 1)
                ahead(l, OUT_BG, 38, 2)
                act.wait_ge(evacuated.sem, evacuated.at(l, OUT_B + 6))
                fn(lat_sq_kv, work[:, 4:6, :], ACT.Square).then_inc(lat_sq.sem, 1)
                silu(l, OUT_BG, gate_ab[:, 1, 0, :])
                ahead(l, OUT_BG + 1, 40, 0)
                silu(l, OUT_BG + 1, gate_ab[:, 1, 1, :])
                ahead(l, OUT_BG + 2, 42, 2)
                root(lat_rstd[:, 0, :], stat[:, 0:TOK], 512, lat_root, (lat_sum.sem, lat_sum.at(l, 1)))
                root(lat_rstd[:, 1, :], score[0][:, 0:TOK], 256, lat_root, (lat_sum.sem, lat_sum.at(l, 2)))
                for k in range(4):
                    act.wait_ge(lat_norm.sem, lat_norm.at(l, k + 1))
                    nc.scalar.copy(mix_hi[:, MIX_C + k, :], work[:, k, :]).then_inc(lat_hi.sem, 1)
                silu(l, OUT_BG + 2, gate_ab[:, 1, 2, :])
                ahead(l, OUT_BG + 3, 44, 0)
                silu(l, OUT_BG + 3, gate_ab[:, 1, 3, :])
                hi(l, 46, 2, OUT_BG + 3)
                hi(l, 47, 3, OUT_BG + 3)
                hi(l, 48, 0, OUT_KR)
                hi(l, 49, 1, OUT_QR + 1)
                def b_attention(i):
                    if i == 0:
                        b_exps(l, 0)
                    if i < 4:
                        b_exps(l, 1 + i)
                    if i == 1:
                        b_copy_tail(l)
                    if i >= 1:
                        b_copy(l, i - 1)
                    if i >= 2:
                        mix_high(l, MIX_B + i - 2)

                for i in range(5):
                    out = OUT_A + 2 * i
                    if i == 0:
                        hi(l, 50, 2, out_of_unit(46))
                        hi(l, 51, 3, out_of_unit(47))
                    else:
                        ahead(l, out, 50 + 4 * i, 2)
                        b_attention(i - 1)
                    ahead(l, out + 1, 52 + 4 * i, 0)
                    if i >= 3:
                        silu(l, out, gate_ab[:, 0, 2 * (i - 3), :])
                    if i >= 4:
                        silu(l, out - 1, gate_ab[:, 0, 1, :])
                def a_attention(i):
                    if i == 0:
                        mix_high(l, MIX_B + 3)
                        act.wait_ge(v_turned.sem, v_turned.at(l, 1))
                        nc.scalar.copy(a_v[0:80, 0, :], turn_a[0:80, 0:P]).then_inc(v_copied.sem, 1)
                        nc.scalar.copy(a_v[:, 1:4, :], turn_a[:, P:4 * P].rearrange("p (c n) -> p c n", c=3)
                                       ).then_inc(v_copied.sem, 1)
                    if i == 1:
                        a_exps(l, 0)
                    if 1 <= i <= 4:
                        a_exps(l, i)
                    if i == 1:
                        act.wait_ge(ln_sum.sem, ln_sum.at(l, 1))
                        nc.scalar.mul(lat_rstd[:, 1, :], ln_stat, 1.0 / 512).then_inc(ln_mean.sem, 1)
                    if i == 2:
                        a_copy(l, 0)
                    if 2 <= i <= 5:
                        a_copy(l, i - 1)
                    if i % 2 == 1:
                        silu(l, OUT_C + 2 * i + 1, work[:, 4 * (i // 2 % 2) + 3, :])
                        mix_high(l, MIX_C + i // 2)
                    if i in (4, 6):
                        mix_high(l, MIX_A + i - 4)
                        mix_high(l, MIX_A + i - 3)

                for i in range(8):
                    out = OUT_C + 2 * i
                    ahead(l, out, 70 + 4 * i, 2)
                    if i == 0:
                        b_attention(4)
                        silu(l, OUT_A + 9, gate_ab[:, 0, 3, :])
                    else:
                        a_attention(i - 1)
                    if i == 4:
                        root(lat_rstd[:, 0, :], ln_stat, 512, ln_root, (ln_var.sem, ln_var.at(l, 1)))
                    if i == 6:
                        mix_high(l, MIX_D)
                        mix_high(l, MIX_D + 1)
                    ahead(l, out + 1, 72 + 4 * i, 0)
                    if i == 5:
                        act.wait_ge(ln_scaled.sem, ln_scaled.at(l, 1))
                        for t in range(GT):
                            fn(conv[:, t, :], conv[:, t, :], ACT.Silu,
                               scale=dvec[:, bass.ds(l, 1), 1, t:t + 1].rearrange("p a b -> p (a b)"),
                               bias=dvec[:, bass.ds(l, 1), 2, t:t + 1].rearrange("p a b -> p (a b)")
                               ).then_inc(ln_silu.sem, 1)
                    if i == 6:
                        mix_high(l, MIX_D + 2)
                        mix_high(l, MIX_D + 3)
                a_attention(7)
                def h_high(k):
                    act.wait_ge(evacuated.sem, evacuated.at(l, OUT_O + k + 1))
                    fn(flat(h_hi[:, bass.ds(k, 1), :]), flat(resid[:, bass.ds(k, 1), :]), ACT.Copy,
                       scale=flat(norms[:, bass.ds(l + 1, 1), bass.ds(k, 1)])).then_inc(h_hi_done.sem, 1)
                with act.Fori(0, 7) as i:
                    ahead(l, OUT_O + 2 * i, 102 + 4 * i, 2)
                    h_high(2 * i)
                    ahead(l, OUT_O + 1 + 2 * i, 104 + 4 * i, 0)
                    h_high(2 * i + 1)
                ahead(l, OUT_O + 14, 130, 2)
                h_high(14)
                h_high(15)
            norm_root_of(DEPTH)

        @block.vector
        def _(dve):
            tt, stt, ts = nc.vector.tensor_tensor, nc.vector.scalar_tensor_tensor, nc.vector.tensor_scalar

            def lo(l, u, slot):
                dve.wait_ge(hi_done.sem, hi_done.at(l, u + 1))
                tt(w_lo[:, slot, :], raw_w[:, slot, :], w_hi[:, slot, :].bitcast(F32), ALU.subtract
                   ).then_inc(split_done.sem, 1)

            def ahead(l, u, slot):
                lo(l, u, slot)
                lo(l, u + 1, slot + 1)

            def evacuate(l, out, b, dst, src_rows=P, rows=None):
                dve.wait_ge(out_done.sem, out_done.at(l, out + 1))
                s = slice(0, src_rows)
                tt(dst, main[b][s, 0:TOK], rstd[s, :], ALU.mult).then_inc(evacuated.sem, 1)

            def take(l, out, dst, rows=P, n=TOK):
                dve.wait_ge(out_done.sem, out_done.at(l, out + 1))
                nc.vector.tensor_copy(dst, main[out % 2][0:rows, 0:n]).then_inc(evacuated.sem, 1)

            def norm(l):
                dve.wait_ge(norm_root.sem, norm_root.at(l, 1))
                nc.vector.reciprocal(rstd[:, :], rstd[:, :]).then_inc(norm_done.sem, 1)
                dve.wait_ge(norm_done.sem, norm_done.at(l, 1))

            seq = [0]

            def mix_low(l, place):
                k = seq[0]
                seq[0] += 1
                dve.wait_ge(y_hi.sem, y_hi.at(l, k + 1))
                tt(mix_lo[:, place, :], y_tmp[:, k % 2, :], mix_hi[:, place, :].bitcast(F32), ALU.subtract
                   ).then_inc(mix_done.sem, 1)

            def y_slot(l):
                if seq[0] >= 2:
                    dve.wait_ge(mix_done.sem, mix_done.at(l, seq[0] - 1))
                return y_tmp[:, seq[0] % 2, :]

            def rope_parts(l, n, src, turned, dst):
                r = dst.shape[0]
                dve.wait_ge(rotated.sem, rotated.at(l, n + 1))
                tt(dst, src, cos[0:r, :], ALU.mult).then_inc(rope_cos.sem, 1)
                tt(rot_tmp[0:r, :], turned[0:r, 0:TOK], sin[0:r, :], ALU.mult).then_inc(rope_sin.sem, 1)
                dve.wait_ge(rope_sin.sem, rope_sin.at(l, n + 1))
                dve.wait_ge(rope_cos.sem, rope_cos.at(l, n + 1))

            def rope_b(l):
                for n in range(2):
                    if n:
                        dve.wait_ge(roped.sem, roped.at(l, 2))
                    part = y_tmp[:, n, :]
                    rope_parts(l, n, work[:, n, :], score[n], part)
                    for half in range(2):
                        r = slice(64 * half, 64 * half + 64)
                        tt(q_rope[0:64, 2 * n + half, :], part[r, :], rot_tmp[r, :], ALU.add).then_inc(roped.sem, 1)
                dve.wait_ge(roped.sem, roped.at(l, 4))
                rope_parts(l, 2, work[0:64, 6, :], stat, k_rope[0:64, :])
                tt(k_rope[0:64, :], k_rope[0:64, :], rot_tmp[0:64, :], ALU.add).then_inc(roped.sem, 1)
                dve.wait_ge(roped.sem, roped.at(l, 5))

            def rope_a_query(l, n):
                part = y_tmp[:, 0, :]
                dve.wait_ge(mix_done.sem, mix_done.at(l, seq[0]))
                rope_parts(l, 3 + n, work[:, n, :], score[n % 2], part)
                tt(a_q[:, META * n:META * n + META], part[:, 0:META], rot_tmp[:, 0:META], ALU.add).then_inc(roped.sem, 1)
                chunks = [x[:, META:TOK].rearrange("p (c q) -> p c q", c=4) for x in (part, rot_tmp)]
                tt(a_q_chunks[:, n // 2, n % 2], chunks[0], chunks[1], ALU.add).then_inc(roped.sem, 1)
                dve.wait_ge(roped.sem, roped.at(l, 5 + 2 * (n + 1)))

            def rope_a_key(l):
                part = y_tmp[:, 0, :]
                rope_parts(l, 7, work[:, 4, :], stat, part)
                for g in range(2):
                    src = slice(64 * g, 64 * g + 64)
                    for half in range(2):
                        tt(a_k[64 * half:64 * half + 64, g, :], part[src, :], rot_tmp[src, :], ALU.add
                           ).then_inc(roped.sem, 1)
                dve.wait_ge(roped.sem, roped.at(l, 17))

            def b_softmax_in(l, n):
                dve.wait_ge(b_score.sem, b_score.at(l, n + 1))
                parts = [turn_b[:, 0:TOK]] if n == 0 else [score[(n - 1) % 2][:, 0:144], score[(n - 1) % 2][:, 144:144 + TOK]]
                c0 = FIRST if n == 0 else 0
                for j, p in enumerate(parts):
                    nc.vector.reduce_max(mx[:, c0 + j:c0 + j + 1], p, AX).then_inc(b_max.sem, 1)
                w = c0 + len(parts)
                dve.wait_ge(b_max.sem, b_max.at(l, 1 if n == 0 else 1 + 2 * n))
                ts(nm[:, c0:w], mx[:, c0:w], -B_SCALE, None, ALU.mult).then_inc(b_negmax.sem, 1)

            def b_softmax_out(l, n):
                c = slice(FIRST, FIRST + 1) if n == 0 else slice(0, 2)
                dve.wait_ge(b_exp.sem, b_exp.at(l, 1 + 2 * n))
                nc.vector.reciprocal(rd[:, c], rs[:, c]).then_inc(b_recip.sem, 1)
                dve.wait_ge(b_recip.sem, b_recip.at(l, n + 1))
                if n == 0:
                    ts(tail_p, tail_p, rd[:, c], None, ALU.mult).then_inc(b_prob.sem, 1)
                    return
                for j, (a, b) in enumerate(((0, 144), (144, 144 + TOK))):
                    p = prob[:, (n - 1) % 2, a:b]
                    ts(p, p, rd[:, j:j + 1], None, ALU.mult).then_inc(b_prob.sem, 1)

            def b_output(l, h):
                dve.wait_ge(b_pv.sem, b_pv.at(l, h + 1))
                dve.wait_ge(gate_done.sem, gate_done.at(l, GT + h + 1))
                tt(y_slot(l), outp[:, 0:TOK], gate_ab[:, 1, h, :], ALU.mult).then_inc(y_done.sem, 1)
                mix_low(l, MIX_B + h)

            def a_softmax_in(l, n):
                dve.wait_ge(a_score.sem, a_score.at(l, n + 1))
                if n == 0:
                    nc.vector.reduce_max(mx[:, first], score[0][:, 0:2 * META].rearrange("p (g k) -> p g k", g=2), AX
                                         ).then_inc(a_max.sem, 1)
                    dve.wait_ge(a_max.sem, a_max.at(l, 1))
                    one = bass.ds(l, 1)
                    stt(out=nm[:, first], in0=mx[:, first], scalar=-A_SCALE,
                        in1=nsink_m[:, one, :].rearrange("p a b -> p (a b)"), op0=ALU.mult, op1=ALU.min
                        ).then_inc(a_negmax.sem, 1)
                    dve.wait_ge(a_negmax.sem, a_negmax.at(l, 1))
                    tt(es[:, first], nm[:, first], sink_m[:, one, :].rearrange("p a b -> p (a b)"), ALU.add
                       ).then_inc(a_sinkarg.sem, 1)
                    return
                s = score[n % 2]
                nc.vector.reduce_max(mx[:, 0:1], s[:, 0:80], AX).then_inc(a_max.sem, 1)
                nc.vector.reduce_max(mx[:, 1:4], s[:, 80:512].rearrange("p (c k) -> p c k", c=3), AX
                                     ).then_inc(a_max.sem, 1)
                dve.wait_ge(a_max.sem, a_max.at(l, 1 + 2 * n))
                ts(nm[:, 0:4], mx[:, 0:4], -A_SCALE, nsink[:, bass.ds(l, 1), n - 1:n].rearrange("p a b -> p (a b)"),
                   ALU.mult, ALU.min).then_inc(a_negmax.sem, 1)

            def a_softmax_out(l, n):
                c = first if n == 0 else slice(0, 4)
                dve.wait_ge(a_exp.sem, a_exp.at(l, 3 + 5 * n))
                tt(rs[:, c], rs[:, c], es[:, c], ALU.add).then_inc(a_den.sem, 1)
                dve.wait_ge(a_den.sem, a_den.at(l, n + 1))
                nc.vector.reciprocal(rd[:, c], rs[:, c]).then_inc(a_recip.sem, 1)
                dve.wait_ge(a_recip.sem, a_recip.at(l, n + 1))
                if n == 0:
                    p = meta_p[:, :].rearrange("p (g k) -> p g k", g=2)
                    tt(p, p, rd[:, first].unsqueeze(2).broadcast_to([P, 2, META]), ALU.mult).then_inc(a_prob.sem, 1)
                    return
                p = prob[:, n % 2, 0:80]
                ts(p, p, rd[:, 0:1], None, ALU.mult).then_inc(a_prob.sem, 1)
                p = prob[:, n % 2, 80:512].rearrange("p (c k) -> p c k", c=3)
                tt(p, p, rd[:, 1:4].unsqueeze(2).broadcast_to([P, 3, 144]), ALU.mult).then_inc(a_prob.sem, 1)

            def a_output(l, g):
                dve.wait_ge(a_pv.sem, a_pv.at(l, 2 * (g + 1)))
                dve.wait_ge(gate_done.sem, gate_done.at(l, 3 * GT))
                dve.wait_ge(meta_out.sem, meta_out.at(l, 1))
                for i in range(2):
                    y, gate = y_slot(l), gate_ab[:, 0, 2 * g + i, :]
                    tt(y[:, META:TOK].rearrange("p (c q) -> p c q", c=4),
                       outp[:, :].rearrange("p (c i q) -> p i c q", c=4, i=2)[:, i],
                       gate[:, META:TOK].rearrange("p (c q) -> p c q", c=4), ALU.mult).then_inc(y_parts.sem, 1)
                    tt(y[:, 0:META], meta_o[:, 32 * g + META * i:32 * g + META * i + META], gate[:, 0:META], ALU.mult
                       ).then_inc(y_done.sem, 1)
                    mix_low(l, MIX_A + 2 * g + i)
            def c_tile(l, t):
                b = 4 * (t % 2)
                lw = [cconv[:, bass.ds(l * GT + t, 1), j:j + 1].rearrange("p a b -> p (a b)") for j in range(C_TAPS)]
                y = y_slot(l)
                dve.wait_ge(c_prod.sem, c_prod.at(l, t + 1))
                ts(y, c_pad[:, 0:TOK], lw[0], None, ALU.mult).then_inc(c_step.sem, 1)
                for j in (1, 2):
                    dve.wait_ge(c_step.sem, c_step.at(l, 4 * t + j))
                    stt(out=y, in0=c_pad[:, j:j + TOK], scalar=lw[j], in1=y, op0=ALU.mult, op1=ALU.add
                        ).then_inc(c_step.sem, 1)
                dve.wait_ge(c_step.sem, c_step.at(l, 4 * t + 3))
                tt(y, y, work[:, b + 2, :], ALU.mult).then_inc(c_step.sem, 1)

            def d_output(l, n):
                dve.wait_ge(ln_silu.sem, ln_silu.at(l, n + 1))
                tt(y_slot(l), conv[:, n, :], gate_d[:, n, :], ALU.mult).then_inc(y_done.sem, 1)
                mix_low(l, MIX_D + n)

            def c_gate(l, t):
                y = y_slot(l)
                dve.wait_ge(c_step.sem, c_step.at(l, 4 * t + 4))
                dve.wait_ge(gate_done.sem, gate_done.at(l, 3 * GT + t + 1))
                tt(y, y, work[:, 4 * (t % 2) + 3, :], ALU.mult).then_inc(y_done.sem, 1)
                mix_low(l, MIX_C + t)

            dve.sem_inc(evacuated.sem, 2)
            nc.vector.memset(eps[:, :], EPS).then_inc(zeroed, 1)
            nc.vector.memset(c_pad[:, 0:C_PAD], 0.0).then_inc(zeroed, 1)
            dve.wait_ge(const_in[0], 16)
            for k in range(KT):
                if k % 4 == 0:
                    dve.wait_ge(x_in[k // 4], 16)
                dve.wait_ge(h_hi_done.sem, k + 1)
                stt(out=h_lo[:, k, :], in0=resid[:, k, :], scalar=norms[:, 0, k:k + 1], in1=h_hi[:, k, :].bitcast(F32),
                    op0=ALU.mult, op1=ALU.subtract).then_inc(h_lo_done.sem, 1)
            for i in (2, 4, 6, 8, 9, 10, 11, 12, 13):
                dve.wait_ge(const_in[i], 16)
            ts(nsink[:, :, :], sink[:, :, :], -1.0, None, ALU.mult).then_inc(nsink_done, 1)
            ts(nsink_m[:, :, :], sink_m[:, :, :], -1.0, None, ALU.mult).then_inc(nsink_done, 1)
            dve.wait_ge(nsink_done, 2)
            dve.wait_ge(zeroed, 2)
            with dve.Fori(0, DEPTH) as l:
                seq[0] = 0
                ahead(l, 0, 0)
                ahead(l, 2, 2)
                norm(l)

                def glu(t):
                    dve.wait_ge(glu_gate.sem, glu_gate.at(l, t + 1))
                    tt(u_pad[:, bass.ds(t, 1), D_PAD:D_PAD + TOK].rearrange("p a n -> p (a n)"),
                       work[:, 0, :], work[:, 1, :], ALU.mult).then_inc(glu_done.sem, 1)

                evacuate(l, 0, 0, work[:, 0, :])
                ahead(l, 4, 0)
                evacuate(l, 1, 1, work[:, 1, :])
                glu(0)
                with dve.Fori(1, 4) as i:
                    ahead(l, 4 * i + 2, 2)
                    dve.wait_ge(glu_done.sem, glu_done.at(l, i))
                    evacuate(l, 2 * i, 0, work[:, 0, :])
                    ahead(l, 4 * i + 4, 0)
                    evacuate(l, 2 * i + 1, 1, work[:, 1, :])
                    glu(i)
                with dve.Fori(0, 2) as i:
                    ahead(l, 18 + 4 * i, 2)
                    evacuate(l, 8 + 2 * i, 0, flat(gate_d[:, bass.ds(2 * i, 1), :]))
                    ahead(l, 20 + 4 * i, 0)
                    evacuate(l, 9 + 2 * i, 1, flat(gate_d[:, bass.ds(2 * i + 1, 1), :]))
                with dve.Fori(0, 3) as i:
                    ahead(l, 26 + 4 * i, 2)
                    evacuate(l, OUT_B + 2 * i, 0, flat(work[:, bass.ds(2 * i, 1), :]))
                    ahead(l, 28 + 4 * i, 0)
                    evacuate(l, OUT_B + 1 + 2 * i, 1, flat(work[:, bass.ds(2 * i + 1, 1), :]))
                ahead(l, 38, 2)
                evacuate(l, OUT_BG, 0, gate_ab[:, 1, 0, :])
                ahead(l, 40, 0)
                evacuate(l, OUT_BG + 1, 1, gate_ab[:, 1, 1, :])

                def latent_norm(j, tiles, w0):
                    dve.wait_ge(lat_root.sem, lat_root.at(l, j + 1))
                    nc.vector.reciprocal(lat_rstd[:, j, :], lat_rstd[:, j, :]).then_inc(lat_recip.sem, 1)
                    dve.wait_ge(lat_recip.sem, lat_recip.at(l, j + 1))
                    for t in tiles:
                        stt(out=work[:, t, :], in0=work[:, t, :],
                            scalar=bnorm[:, bass.ds(l, 1), t:t + 1].rearrange("p a b -> p (a b)"),
                            in1=lat_rstd[:, j, :], op0=ALU.mult, op1=ALU.mult).then_inc(lat_norm.sem, 1)

                ahead(l, 42, 2)
                latent_norm(0, range(4), 0)
                evacuate(l, OUT_BG + 2, 0, gate_ab[:, 1, 2, :])
                ahead(l, 44, 0)
                for k in range(4):
                    dve.wait_ge(lat_hi.sem, lat_hi.at(l, k + 1))
                    tt(mix_lo[:, MIX_C + k, :], work[:, k, :], mix_hi[:, MIX_C + k, :].bitcast(F32), ALU.subtract
                       ).then_inc(lat_lo.sem, 1)
                latent_norm(1, range(4, 6), 4)
                evacuate(l, OUT_BG + 3, 1, gate_ab[:, 1, 3, :])
                ahead(l, 46, 2)
                dve.wait_ge(out_done.sem, out_done.at(l, OUT_KR + 1))
                tt(work[0:64, 6, :], main[0][0:64, 0:TOK], rstd[0:64, :], ALU.mult).then_inc(evacuated.sem, 1)
                take(l, OUT_QR, work[:, 0, :])
                take(l, OUT_QR + 1, work[:, 1, :])
                ahead(l, 48, 0)
                for h in range(B_HEADS):
                    take(l, OUT_QN + h, q_nope[:, h, :])
                for h in range(B_HEADS):
                    take(l, OUT_KN + h, k_nope[:, h, :])
                for t in range(3):
                    rows = min(P, TOK - P * t)
                    take(l, OUT_V + t, v_b[0:rows, t, :], rows, 512)
                dve.wait_ge(evacuated.sem, evacuated.at(l, OUT_QR + 2))
                for i in range(5):
                    out = OUT_A + 2 * i
                    dst = [work[:, 2 * i + j, :] if i < 3 else gate_ab[:, 0, 2 * (i - 3) + j, :] for j in range(2)]
                    if i == 1:
                        b_softmax_in(l, 0)
                    if i >= 1:
                        b_softmax_in(l, i)
                    ahead(l, 50 + 4 * i, 2)
                    if i == 0:
                        rope_b(l)
                    if i == 1:
                        b_softmax_out(l, 0)
                    if i >= 1:
                        b_softmax_out(l, i)
                    if i >= 3:
                        b_output(l, i - 3)
                    evacuate(l, out, 0, dst[0])
                    ahead(l, 52 + 4 * i, 0)
                    evacuate(l, out + 1, 1, dst[1])
                for i in range(8):
                    out, t = OUT_C + 2 * i, i // 2
                    b = 4 * (t % 2) + 2 * (i % 2)
                    if i == 2:
                        a_softmax_in(l, 0)
                    if 2 <= i <= 5:
                        a_softmax_in(l, i - 1)
                    ahead(l, 70 + 4 * i, 2)
                    if i == 0:
                        b_output(l, 2)
                        rope_a_query(l, 0)
                        rope_a_query(l, 1)
                        dve.wait_ge(roped.sem, roped.at(l, 9))
                    if i == 1:
                        b_output(l, 3)
                        rope_a_query(l, 2)
                        rope_a_query(l, 3)
                        rope_a_key(l)
                    if i == 2:
                        a_softmax_out(l, 0)
                    if 2 <= i <= 5:
                        a_softmax_out(l, i - 1)
                    if i in (2, 4, 6):
                        c_gate(l, t - 1)
                    if i == 5:
                        dve.wait_ge(a_meta_pv.sem, a_meta_pv.at(l, 1))
                        nc.vector.tensor_copy(meta_o[:, :], stat[:, 0:64]).then_inc(meta_out.sem, 1)
                    if i in (5, 7):
                        a_output(l, (i - 5) // 2)
                    if i == 6:
                        d_output(l, 0)
                        d_output(l, 1)
                    evacuate(l, out, 0, work[:, b, :])
                    if i % 2 == 1:
                        c_tile(l, t)
                    ahead(l, 72 + 4 * i, 0)
                    if i == 2:
                        dve.wait_ge(ln_mean.sem, ln_mean.at(l, 1))
                        tt(conv[:, :, :], conv[:, :, :], lat_rstd[:, 1:2, :].broadcast_to([P, GT, TOK]), ALU.subtract
                           ).then_inc(ln_center.sem, 1)
                    if i == 4:
                        dve.wait_ge(ln_root.sem, ln_root.at(l, 1))
                        nc.vector.reciprocal(lat_rstd[:, 0, :], lat_rstd[:, 0, :]).then_inc(ln_recip.sem, 1)
                        dve.wait_ge(ln_recip.sem, ln_recip.at(l, 1))
                        tt(conv[:, :, :], conv[:, :, :], lat_rstd[:, 0:1, :].broadcast_to([P, GT, TOK]), ALU.mult
                           ).then_inc(ln_scaled.sem, 1)
                    if i == 6:
                        d_output(l, 2)
                        d_output(l, 3)
                    evacuate(l, out + 1, 1, work[:, b + 1, :])
                    if i % 2 == 0:
                        dve.wait_ge(evacuated.sem, evacuated.at(l, out + 2))
                        tt(c_pad[:, C_PAD:C_PAD + TOK], work[:, b, :], work[:, b + 1, :], ALU.mult
                           ).then_inc(c_prod.sem, 1)
                c_gate(l, GT - 1)

                def add_resid(k, b):
                    dve.wait_ge(out_done.sem, out_done.at(l, OUT_O + k + 1))
                    r = flat(resid[:, bass.ds(k, 1), :])
                    tt(r, main[b][:, 0:TOK], r, ALU.add).then_inc(evacuated.sem, 1)
                    dve.wait_ge(h_hi_done.sem, h_hi_done.at(l + 1, k + 1))
                    stt(out=flat(h_lo[:, bass.ds(k, 1), :]), in0=r, scalar=flat(norms[:, bass.ds(l + 1, 1), bass.ds(k, 1)]),
                        in1=flat(h_hi[:, bass.ds(k, 1), :]).bitcast(F32), op0=ALU.mult, op1=ALU.subtract
                        ).then_inc(h_lo_done.sem, 1)

                with dve.Fori(0, 7) as i:
                    ahead(l, 102 + 4 * i, 2)
                    add_resid(2 * i, 0)
                    ahead(l, 104 + 4 * i, 0)
                    add_resid(2 * i + 1, 1)
                ahead(l, 130, 2)
                add_resid(14, 0)
                add_resid(15, 1)
            norm(DEPTH)
            for k in range(KT):
                stt(out=resid[:, k, META:TOK], in0=resid[:, k, META:TOK], scalar=norms[:, DEPTH, k:k + 1],
                    in1=rstd[:, META:TOK], op0=ALU.mult, op1=ALU.mult).then_inc(final_done, 1)

        @block.gpsimd
        def _(pool):
            tt = nc.gpsimd.tensor_tensor
            squares = conv_tmp[:, 0, :]

            def sum_squares(rnd, k, tile_ready):
                tile_ready(k)
                x = flat(resid[:, bass.ds(k, 1), :])
                if isinstance(k, int) and k == 0:
                    tt(sumsq, x, x, ALU.mult).then_inc(sq_done.sem, 1)
                    return
                pool.wait_ge(sq_done.sem, sq_done.at(rnd, 2 * k - 1))
                tt(squares, x, x, ALU.mult).then_inc(sq_done.sem, 1)
                pool.wait_ge(sq_done.sem, sq_done.at(rnd, 2 * k))
                tt(sumsq, sumsq, squares, ALU.add).then_inc(sq_done.sem, 1)

            nc.gpsimd.memset(u_pad[:, :, 0:D_PAD], 0.0)
            for k in range(KT):
                sum_squares(0, k, lambda k: pool.wait_ge(x_in[k // 4], 16))
            pool.wait_ge(const_in[3], 16)
            pool.wait_ge(const_in[5], 16)
            with pool.Fori(0, DEPTH) as l:
                def tap(j, acc):
                    w = dconv[:, bass.ds(l * GT, GT), bass.ds(j, 1)].broadcast_to([P, GT, TOK])
                    tt(conv_tmp[:, :, :], u_pad[:, :, bass.ds(j, TOK)], w, ALU.mult).then_inc(tap_done.sem, 1)
                    pool.wait_ge(tap_done.sem, tap_done.at(l, 2 * j + 1))
                    tt(conv[:, :, :], acc, conv_tmp[:, :, :], ALU.add).then_inc(tap_done.sem, 1)

                pool.wait_ge(glu_done.sem, glu_done.at(l, GT))
                tap(0, dvec[:, bass.ds(l, 1), 0, :].rearrange("p a b -> p b a").broadcast_to([P, GT, TOK]))
                with pool.Fori(1, D_TAPS) as j:
                    pool.wait_ge(tap_done.sem, tap_done.at(l, 2 * j))
                    tap(j, conv[:, :, :])

                def tile_sums(l, k, src):
                    acc = conv_tmp[:, 0, :]
                    tt(acc, src[:, 0, :], src[:, 1, :], ALU.add).then_inc(ln_pre.sem, 1)
                    for n in (2, 3):
                        pool.wait_ge(ln_pre.sem, ln_pre.at(l, 3 * k + n - 1))
                        tt(acc, acc, src[:, n, :], ALU.add).then_inc(ln_pre.sem, 1)

                pool.wait_ge(tap_done.sem, tap_done.at(l, 2 * D_TAPS))
                tile_sums(l, 0, conv)
                pool.wait_ge(ln_center.sem, ln_center.at(l, 1))
                tt(conv_tmp[:, :, :], conv[:, :, :], conv[:, :, :], ALU.mult).then_inc(ln_sq.sem, 1)
                pool.wait_ge(ln_sq.sem, ln_sq.at(l, 1))
                tile_sums(l, 1, conv_tmp)

                def resid_ready(k):
                    pool.wait_ge(evacuated.sem, evacuated.at(l, OUT_O + k + 1))
                sum_squares(l + 1, 0, resid_ready)
                with pool.Fori(1, KT) as k:
                    sum_squares(l + 1, k, resid_ready)


def kernel(x, meta_tokens, norm_w, w_in, a_sinks, b_q_norm, b_kv_norm, b_w_uq, b_w_ukv,
           c_conv_w, d_conv_w, d_conv_b, d_ln_w, d_ln_b, w_out, final_norm_w):
    import concourse.bacc as bacc
    from concourse.bass_utils import run_bass_kernel_spmd

    arr = {k: np.asarray(v) for k, v in dict(
        x=x, meta=meta_tokens, norm_w=norm_w, w_in=w_in, sinks=a_sinks, bq=b_q_norm, bkv=b_kv_norm, uq=b_w_uq,
        ukv=b_w_ukv, cw=c_conv_w, dw=d_conv_w, db=d_conv_b, lw=d_ln_w, lb=d_ln_b, w_out=w_out, fw=final_norm_w).items()}

    def by_feature(a):
        t = a.reshape(a.shape[:-1] + (a.shape[-1] // P, P))
        return np.ascontiguousarray(np.moveaxis(t, -1, 0))

    sizes = [512, 128, 128, 512, 512, 256, 64, 512, 512, 512, 512, 512, 512, 512, 512]
    names = ["aq", "ak", "av", "ag", "bcq", "bckv", "bkr", "bg", "cb", "cc", "cx", "cg", "da", "dgl", "dg"]
    start = dict(zip(names, np.cumsum([0] + sizes[:-1])))
    w_in_a, uq, w_o = arr["w_in"], arr["uq"], arr["w_out"]
    units = []

    def put(w):
        k, n = w.shape[0] // P, w.shape[1]
        per = UNIT // n
        t = w.reshape(k // per, per, P, n).transpose(0, 2, 1, 3).reshape(k // per, P, UNIT)
        units.extend(t)

    def tile(l, name, t):
        c = start[name] + P * t
        put(w_in_a[l][:, c:c + P])

    for l in range(DEPTH):
        for t in range(GT):
            tile(l, "da", t), tile(l, "dgl", t)
        for t in range(GT):
            tile(l, "dg", t)
        for t in range(GT):
            tile(l, "bcq", t)
        for t in range(2):
            tile(l, "bckv", t)
        for t in range(GT):
            tile(l, "bg", t)
        put(w_in_a[l][:, start["bkr"]:start["bkr"] + 64])
        q = uq[l].reshape(512, B_HEADS, 192)
        put(q[:, :, P:].reshape(512, 256))
        put(q[:, 0:2, :P].reshape(512, 256))
        put(q[:, 2:4, :P].reshape(512, 256))
        for t in range(GT):
            tile(l, "aq", t)
        tile(l, "ak", 0), tile(l, "av", 0)
        for t in range(GT):
            tile(l, "ag", t)
        for t in range(GT):
            tile(l, "cc", t), tile(l, "cx", t), tile(l, "cb", t), tile(l, "cg", t)
        rows = w_o[l].reshape(4, 512, D_MODEL)[[3, 1, 0, 2]].reshape(D_MODEL, D_MODEL)
        for t in range(KT):
            put(rows[:, P * t:P * t + P])
    assert len(units) == DEPTH * UNITS
    stream = np.stack(units).reshape(len(units) // RING, RING, P, UNIT)

    kv = arr["ukv"].reshape(DEPTH, 2, P, B_HEADS, 2, P)
    ukv = np.ascontiguousarray(kv.transpose(0, 2, 1, 4, 3, 5)).reshape(DEPTH, P, 2, UNIT)
    tokens = np.concatenate([arr["meta"], arr["x"][0]], axis=0)
    x_t = np.ascontiguousarray(by_feature(tokens).transpose(0, 2, 1))
    norms = by_feature(np.concatenate([arr["norm_w"], arr["fw"][None]], axis=0))
    bnorm = by_feature(np.concatenate([arr["bq"], arr["bkv"]], axis=1))
    dconv = np.ascontiguousarray(by_feature(arr["dw"]).transpose(0, 1, 3, 2)).reshape(P, DEPTH * GT, D_TAPS)
    cconv = np.ascontiguousarray(by_feature(arr["cw"]).transpose(0, 1, 3, 2)).reshape(P, DEPTH * GT, C_TAPS)
    dvec = by_feature(np.stack([arr["db"], arr["lw"], arr["lb"]], axis=1))

    inv = (1.0 / (np.float32(10000.0) ** (np.arange(0, 64, 2, dtype=np.float32) / np.float32(64)))).astype(np.float32)
    ang = (np.arange(TOK, dtype=np.float32)[:, None] * inv[None, :]).astype(np.float32)
    rope = np.stack([np.tile(np.cos(ang).T, (4, 1)), np.tile(np.sin(ang).T, (4, 1))], axis=1).astype(np.float32)
    chunk = np.where(np.arange(TOK) < META, 0, (np.arange(TOK) - META) // CHUNK + 1)
    mask = np.stack([(chunk[None] == np.arange(5)[:, None]) * 1.0, (chunk[None] > np.arange(5)[:, None]) * NEG],
                    axis=1).astype(np.float32)
    rot = np.zeros((P, P), np.float32)
    for m in range(P):
        if m % 64 < 32:
            rot[m + 32, m] = -1.0
        else:
            rot[m - 32, m] = 1.0
    mats = np.stack([np.eye(P, dtype=np.float32), np.ones((P, P), np.float32), rot], axis=1)

    nc = bacc.Bacc("TRN2", target_bir_lowering=False, num_devices=1)
    arrays = dict(stream=stream, ukv=ukv, x=x_t, norms=norms, bnorm=bnorm, dconv=dconv, cconv=cconv, dvec=dvec,
                  sinks=np.ascontiguousarray(arr["sinks"].reshape(DEPTH, 2, 2, 2).transpose(2, 0, 1, 3)).reshape(2, -1),
                  sinks_m=np.ascontiguousarray(arr["sinks"].reshape(DEPTH, 2, 4).transpose(2, 0, 1)).reshape(4, -1),
                  rope=rope, mask=mask, mats=mats)
    args = [nc.dram_tensor(f"{n}_dram", a.shape, F32, kind="ExternalInput").ap() for n, a in arrays.items()]
    out_ap = nc.dram_tensor("out_dram", (P, KT, TOK - META), F32, kind="ExternalOutput").ap()
    build(nc, *args, out_ap)
    r = run_bass_kernel_spmd(nc, [{f"{n}_dram": a for n, a in arrays.items()}], core_ids=[0])
    y = np.asarray(r.results[0]["out_dram"])
    return np.ascontiguousarray(y.transpose(2, 1, 0)).reshape(1, TOK - META, D_MODEL)
```

```python
import numpy as np
import concourse.bass as bass
import concourse.mybir as mybir
from concourse.alu_op_type import AluOpType as ALU
from contextlib import ExitStack

ACT = mybir.ActivationFunctionType
AX = mybir.AxisListType.X
F32 = mybir.dt.float32
F32R = mybir.dt.float32r

P = 128
D_MODEL = 2048
DEPTH = 2
META = 16
CHUNK = 64
TOK = 272
KT = D_MODEL // P
GT = KT // 4
UNIT = 1024
HALF = UNIT // P
RING = 4
UNITS = 132
OUTS = 78
EPS = 1e-6
NEG = -1e30
D_TAPS = 31
D_PAD = D_TAPS - 1
C_TAPS = 3
C_PAD = C_TAPS - 1
A_SCALE = 64 ** -0.5
B_SCALE = 192 ** -0.5
B_HEADS = 4
FIRST_UNITS = {3: [0], 7: [1], 15: [2, 3]}
FIRST = 4

OUT_D, OUT_B, OUT_BG, OUT_KR, OUT_QR, OUT_QN, OUT_KN, OUT_V, OUT_A, OUT_C, OUT_O = \
    0, 12, 18, 22, 23, 25, 29, 33, 36, 46, 62
U_KR, U_UQ = 44, 45

B_Q0, B_Q1, B_TAIL, TAIL_M = (0, 128, 144), (128, 128, 272), 240, 32


def flat(ap):
    return ap.rearrange("p a b -> p (a b)")


def out_of_unit(u):
    if u < U_KR:
        return u // 2
    if u < U_UQ + 3:
        return OUT_KR + 2 * (u - U_KR)
    return (u + 24) // 2


def wanted(last):
    return slice(META, TOK) if last else slice(0, TOK)


class Signal:

    def __init__(self, sem, per, credit=0):
        self.sem, self.per, self.credit = sem, per, credit

    def at(self, layer, k):
        return layer * self.per + (k + self.credit)


def build(nc, stream, ukv_d, x_d, norms_d, bnorm_d, dconv_d, cconv_d, dvec_d, sinks_d, sinks_m_d,
          rope_d, mask_d, mats_d, out_d):
    ctx = ExitStack()
    with ctx:
        def sb(name, shape, dt=F32):
            return ctx.enter_context(nc.sbuf_tensor(name, shape, dt))

        def bank(name):
            return ctx.enter_context(nc.psum_tensor(name, [P, 512], F32))

        def sem(name):
            return ctx.enter_context(nc.semaphore(name))

        def signal(name, per, credit=0):
            return Signal(sem(name), per, credit)

        resid = sb("resid", [P, KT, TOK])
        h_hi = sb("h_hi", [P, KT, TOK], F32R)
        h_lo = sb("h_lo", [P, KT, TOK], F32R)
        mix_hi = sb("mix_hi", [P, KT, TOK], F32R)
        mix_lo = sb("mix_lo", [P, KT, TOK], F32R)
        raw_w = sb("raw_w", [P, RING, UNIT])
        w_hi = sb("w_hi", [P, RING, UNIT], F32R)
        w_lo = sb("w_lo", [P, RING, UNIT], F32R)
        rstd = sb("rstd", [P, TOK])
        lat_rstd = sb("lat_rstd", [P, 2, TOK])
        u_pad = sb("u_pad", [P, GT, D_PAD + TOK])
        conv = sb("conv", [P, GT, TOK])
        conv_tmp = sb("conv_tmp", [P, GT, TOK])
        gate_d = sb("gate_d", [P, GT, TOK])
        gate_ab = sb("gate_ab", [P, 2, GT, TOK])
        work = sb("work", [P, 8, TOK])
        q_nope = sb("q_nope", [P, GT, TOK])
        k_nope = sb("k_nope", [P, GT, TOK])
        q_rope = sb("q_rope", [64 + 5, B_HEADS, TOK])
        k_rope = sb("k_rope", [64 + 5, TOK])
        v_b = sb("v_b", [P, 3, B_HEADS * P])
        attn = sb("attn", [P, 2, UNIT])
        meta_p = sb("meta_p", [P, 2 * META])
        y_tmp = sb("y_tmp", [P, 2, TOK])
        c_pad = sb("c_pad", [P, C_PAD + TOK])
        norms = sb("norms", [P, DEPTH + 1, KT])
        bnorm = sb("bnorm", [P, DEPTH, 6])
        dconv = sb("dconv", [P, DEPTH * GT, D_TAPS])
        cconv = sb("cconv", [P, DEPTH * GT, C_TAPS])
        dvec = sb("dvec", [P, DEPTH, 3, GT])
        sink = sb("sink", [P, DEPTH, 4])
        sink_m = sb("sink_m", [P, DEPTH, 2])
        nsink = sb("nsink", [P, DEPTH, 4])
        nsink_m = sb("nsink_m", [P, DEPTH, 2])
        rope = sb("rope", [P, 2, TOK])
        mats = sb("mats", [P, 3, P])
        eps = sb("eps", [P, 1])
        warm = sb("warm", [P, 1])
        mx = sb("mx", [P, 8])
        nm = sb("nm", [P, 8])
        rs = sb("rs", [P, 8])
        es = sb("es", [P, 8])
        rd = sb("rd", [P, 8])

        first = slice(FIRST, FIRST + 2)
        meta_o = sb("meta_o", [P, 64])

        ident, ones, rotate = mats[:, 0, :], mats[:, 1, :], mats[:, 2, :]
        cos, sin = rope[:, 0, :], rope[:, 1, :]
        prob = attn[:, 0, :].rearrange("p (b n) -> p b n", b=2)
        prob_t = attn[:, 1, :]
        tail_p, tail_t = work[:, 6, :], work[:, 7, :]
        tail_v = prob_t[0:META, 5 * P:6 * P]
        sumsq = rot_tmp = lat_rstd[:, 1, :]
        meta_t = lat_rstd[0:META, 1, 0:2 * P]
        a_q, a_k = q_nope[:, :, :].rearrange("p t n -> p (t n)"), k_nope[:, 0:2, :]
        a_q_chunks = a_q[:, 4 * META:].rearrange("p (g c i q) -> p g i c q", g=2, c=4, i=2)
        a_v = k_nope[:, 2:4, :].rearrange("p t n -> p (t n)")[:, 0:4 * P].rearrange("p (c n) -> p c n", c=4)
        lat_sq_q = gate_ab[:, 0, :, :]
        lat_sq_kv = q_nope[:, 0:2, :]

        ukv_hi, ukv_lo = (m[:, 0:2 * GT, :].rearrange("p t n -> p (t n)")[:, 0:2 * UNIT].rearrange("p (k n) -> p k n", k=2)
                          for m in (mix_hi, mix_lo))

        main = [bank("main0"), bank("main1")]
        stat = bank("stat")
        score = [bank("score0"), bank("score1")]
        turn_a, turn_b = bank("turn_a"), bank("turn_b")
        outp = bank("outp")

        ln_stat = stat[:, 64:64 + TOK]

        x_in = [sem(f"x_in{i}") for i in range(4)]
        const_in = [sem(f"const_in{i}") for i in range(15)]
        landed = [signal(f"landed{i}", 16 * UNITS // RING) for i in range(RING)]
        ukv_in = signal("ukv_in", 16)
        ukv_high = signal("ukv_high", 2)
        ukv_split = signal("ukv_split", 2)
        hi_done = signal("hi_done", UNITS)
        split_done = signal("split_done", UNITS)
        out_done = signal("out_done", OUTS, 2)
        evacuated = signal("evacuated", OUTS, 2)
        h_hi_done = signal("h_hi_done", KT)
        h_lo_done = signal("h_lo_done", KT)
        sq_done = signal("sq_done", 2 * KT - 2)
        sq_pool, sq_first = sem("sq_pool"), sem("sq_first")
        norm_in = signal("norm_in", 1)
        norm_sum = signal("norm_sum", 1)
        norm_root = signal("norm_root", 1)
        norm_done = signal("norm_done", 1)
        glu_gate = signal("glu_gate", GT)
        glu_done = signal("glu_done", GT)
        gate_done = signal("gate_done", 4 * GT)
        tap_done = signal("tap_done", 2 * D_TAPS)
        lat_sq = signal("lat_sq", 2)
        lat_add = signal("lat_add", 3)
        lat_sum = signal("lat_sum", 2)
        lat_root = signal("lat_root", 2)
        lat_recip = signal("lat_recip", 2)
        lat_norm = signal("lat_norm", 6)
        lat_hi = signal("lat_hi", 6)
        lat_lo = signal("lat_lo", 6)
        rotated = signal("rotated", 8)
        rope_cos = signal("rope_cos", 8)
        rope_sin = signal("rope_sin", 8)
        roped = signal("roped", 5 + 2 * 4 + 4)
        b_score = signal("b_score", 5)
        b_max = signal("b_max", 9)
        b_negmax = signal("b_negmax", 5)
        b_exp = signal("b_exp", 9)
        b_recip = signal("b_recip", 5)
        b_prob = signal("b_prob", 9)
        b_turned = signal("b_turned", 5)
        b_turn_copied = signal("b_turn_copied", 14)
        b_pv = signal("b_pv", 4)
        v_turned = signal("v_turned", 1)
        v_copied = signal("v_copied", 2)
        a_score = signal("a_score", 5)
        a_max = signal("a_max", 9)
        a_negmax = signal("a_negmax", 5)
        a_sinkarg = signal("a_sinkarg", 1)
        a_exp = signal("a_exp", 2 + 1 + 4 * 5)
        a_den = signal("a_den", 5)
        a_recip = signal("a_recip", 5)
        a_prob = signal("a_prob", 9)
        a_turned = signal("a_turned", 5)
        a_turn_copied = signal("a_turn_copied", 1 + 4 * 3)
        a_meta_pv = signal("a_meta_pv", 1)
        a_pv = signal("a_pv", 4)
        ln_pre = signal("ln_pre", 6)
        ln_sum = signal("ln_sum", 1)
        ln_mean = signal("ln_mean", 1)
        ln_center = signal("ln_center", 1)
        ln_sq = signal("ln_sq", 1)
        ln_var = signal("ln_var", 1)
        ln_root = signal("ln_root", 1)
        ln_recip = signal("ln_recip", 1)
        ln_scaled = signal("ln_scaled", 1)
        ln_silu = signal("ln_silu", GT)
        c_prod = signal("c_prod", GT)
        c_step = signal("c_step", 4 * GT)
        y_parts = signal("y_parts", GT)
        meta_out = signal("meta_out", 1)
        y_done = signal("y_done", KT)
        y_hi = signal("y_hi", KT)
        mix_done = signal("mix_done", KT)
        zeroed = sem("zeroed")
        warmed = sem("warmed")
        nsink_done = sem("nsink_done")
        final_done = [sem(f"final_done{i}") for i in range(8)]
        weighted = sem("weighted")
        out_sent = [sem(f"out_sent{i}") for i in range(8)]

        MIX_D, MIX_B, MIX_A, MIX_C = 0, GT, 2 * GT, 3 * GT
        Y_B_LAST, Y_A1 = 4, 8

        block = ctx.enter_context(nc.Block())

        @block.sync
        def _(sp):
            def fetch(turn, slot):
                sp.dma_start(raw_w[:, slot, :], stream[bass.ds(turn, 1), slot, :, :].rearrange("u p n -> p (u n)")).then_inc(landed[slot].sem, 16)

            def const(i, dst, src):
                sp.dma_start(dst, src).then_inc(const_in[i], 16)

            const(0, norms[:, :, :], norms_d)
            for load in ("x0", "u0", "x1", "u1", "x2", "x3", "u2", "u3"):
                q = int(load[1])
                if load[0] == "x":
                    sp.dma_start(resid[:, 4 * q:4 * q + 4, :], x_d[:, 4 * q:4 * q + 4, :]).then_inc(x_in[q], 16)
                else:
                    fetch(0, q)
            const(1, mats[:, :, :], mats_d)
            const(2, bnorm[:, :, :], bnorm_d)
            const(3, dconv[:, :, :], dconv_d)
            const(4, cconv[:, :, :], cconv_d)
            const(5, dvec[:, :, :, :], dvec_d)
            const(6, rope[:, :, :], rope_d)
            const(7, k_rope[64:69, :], mask_d[:, 1, :])
            const(14, q_rope[64:69, :, :], mask_d[:, 0:1, :].broadcast_to([5, B_HEADS, TOK]))
            for i in range(2):
                const(8 + i, sink[64 * i:64 * i + 64, :, :].rearrange("p l c -> p (l c)"),
                      sinks_d[i:i + 1, :].broadcast_to([64, DEPTH * 4]))
            for i in range(4):
                const(10 + i, sink_m[32 * i:32 * i + 32, :, :].rearrange("p l g -> p (l g)"),
                      sinks_m_d[i:i + 1, :].broadcast_to([32, DEPTH * 2]))
            with sp.Fori(1, DEPTH * UNITS // RING) as turn:
                for s in range(RING):
                    sp.wait_ge(split_done.sem, (turn - 1) * RING + (s + 1))
                    fetch(turn, s)
            for q in (2, 3, 4, 0, 1, 5, 6, 7):
                sp.wait_ge(final_done[q], 1)
                sp.dma_start(out_d[:, 2 * q:2 * q + 2, :], resid[:, 2 * q:2 * q + 2, META:TOK]
                             ).then_inc(out_sent[q], 16)
            for q in range(8):
                sp.wait_ge(out_sent[q], 16)

        @block.tensor
        def _(pe):
            mm = nc.tensor.matmul

            def split_product(dst, pairs, last):
                n = len(pairs)
                for i, (whi, wlo, xhi, xlo) in enumerate(pairs):
                    mm(dst, wlo, xhi, start=(i == 0 and last[0]), stop=False)
                    mm(dst, whi, xlo, start=False, stop=False)
                    ins = mm(dst, whi, xhi, start=False, stop=(i == n - 1 and last[1]))
                return ins

            def tile(l, out, u, b, slot, hi, lo, ready=None, cols=slice(0, TOK)):
                pe.wait_ge(evacuated.sem, evacuated.at(l, out - 1))
                for half in range(2):
                    pe.wait_ge(split_done.sem, split_done.at(l, u + (half + 1)))
                    s = slot + half
                    for kk in range(HALF):
                        k = half * HALF + kk
                        if ready:
                            ready(k)
                        c = slice(kk * P, kk * P + P)
                        ins = split_product(main[b][:, cols],
                                            [(w_hi[:, s, c], w_lo[:, s, c], hi[:, k, cols], lo[:, k, cols])],
                                            (k == 0, k == KT - 1))
                ins.then_inc(out_done.sem, 1)

            def pair(l, out, u, hi, lo, ready=None, cols=slice(0, TOK)):
                tile(l, out, u, 0, 0, hi, lo, ready, cols)
                tile(l, out + 1, u + 2, 1, 2, hi, lo, None, cols)

            def norm_stat(l):
                pe.wait_ge(norm_in.sem, norm_in.at(l, 1))
                mm(stat[:, 0:TOK], ones, sumsq[:, :], start=True, stop=True).then_inc(norm_sum.sem, 1)

            def main_out(l, out, rows=P, n=TOK):
                pe.wait_ge(evacuated.sem, evacuated.at(l, out - 1))
                return main[out % 2][0:rows, 0:n]

            def b_up(l):
                dst = main_out(l, OUT_KR, 64)
                pe.wait_ge(split_done.sem, split_done.at(l, U_KR + 1))
                split_product(dst, [(w_hi[:, 0, 64 * k:64 * k + 64], w_lo[:, 0, 64 * k:64 * k + 64],
                                     h_hi[:, k, :], h_lo[:, k, :]) for k in range(KT)],
                              (True, True)).then_inc(out_done.sem, 1)
                pe.wait_ge(lat_lo.sem, lat_lo.at(l, 4))
                for n in range(6):
                    out = OUT_QR + n
                    s = 1 + n // 2
                    dst = main_out(l, out)
                    pe.wait_ge(split_done.sem, split_done.at(l, U_UQ + n // 2 + 1))
                    cols = [slice(256 * k + P * (n % 2), 256 * k + P * (n % 2) + P) for k in range(GT)]
                    split_product(dst, [(w_hi[:, s, c], w_lo[:, s, c], mix_hi[:, MIX_C + k, :], mix_lo[:, MIX_C + k, :])
                                        for k, c in enumerate(cols)], (True, True)).then_inc(out_done.sem, 1)
                pe.wait_ge(lat_lo.sem, lat_lo.at(l, 6))
                pe.wait_ge(ukv_split.sem, ukv_split.at(l, 2))
                for h in range(B_HEADS):
                    dst = main_out(l, OUT_KN + h)
                    c = slice(P * h, P * h + P)
                    split_product(dst, [(ukv_hi[:, k, c], ukv_lo[:, k, c], mix_hi[:, MIX_A + k, :], mix_lo[:, MIX_A + k, :])
                                        for k in range(2)], (True, True)).then_inc(out_done.sem, 1)
                for t in range(3):
                    rows = min(P, TOK - P * t)
                    dst = main_out(l, OUT_V + t, rows, 512)
                    r = slice(P * t, P * t + rows)
                    split_product(dst, [(mix_hi[:, MIX_A + k, r], mix_lo[:, MIX_A + k, r], ukv_hi[:, k, 512:], ukv_lo[:, k, 512:])
                                        for k in range(2)], (True, True)).then_inc(out_done.sem, 1)
                pe.wait_ge(evacuated.sem, evacuated.at(l, OUT_QR + 2))
                for dst, src, r in ((score[0], 0, P), (score[1], 1, P), (stat, 6, 64)):
                    mm(dst[0:r, 0:TOK], rotate[0:r, 0:r], work[0:r, src, :], start=True, stop=True).then_inc(rotated.sem, 1)

            def b_tail_scores(l):
                pe.wait_ge(roped.sem, roped.at(l, 5))
                pe.wait_ge(evacuated.sem, evacuated.at(l, OUT_V + 3))
                for h in range(B_HEADS):
                    dst = turn_b[32 * h:32 * h + 32, 0:TOK]
                    mm(dst, q_nope[:, h, B_TAIL:TOK], k_nope[:, h, :], start=True, stop=False)
                    ins = mm(dst, q_rope[0:64, h, B_TAIL:TOK], k_rope[0:64, :], start=False, stop=True)
                ins.then_inc(b_score.sem, 1)

            def b_scores(l, h):
                if h >= 2:
                    pe.wait_ge(b_exp.sem, b_exp.at(l, 2 * h - 1))
                for (q0, n, keys), at in ((B_Q0, 0), (B_Q1, B_Q0[2])):
                    dst = score[h % 2][:, at:at + keys]
                    mm(dst, q_nope[:, h, q0:q0 + n], k_nope[:, h, 0:keys], start=True, stop=False)
                    ins = mm(dst, q_rope[:, h, q0:q0 + n], k_rope[:, 0:keys], start=False, stop=True)
                ins.then_inc(b_score.sem, 1)

            def b_turn_tail(l):
                pe.wait_ge(b_prob.sem, b_prob.at(l, 1))
                nc.tensor.transpose(outp[:, 0:P], tail_p[:, 0:P], ident)
                nc.tensor.transpose(outp[:, P:2 * P], tail_p[:, P:2 * P], ident)
                nc.tensor.transpose(outp[0:META, 2 * P:3 * P], tail_p[:, 2 * P:TOK], ident).then_inc(b_turned.sem, 1)

            def b_turn(l, h):
                pe.wait_ge(b_prob.sem, b_prob.at(l, 3 + 2 * h))
                if h:
                    pe.wait_ge(b_turn_copied.sem, b_turn_copied.at(l, 2 + 3 * h))
                p = prob[:, h % 2, :]
                nc.tensor.transpose(turn_a[:, 0:P], p[:, 0:P], ident)
                nc.tensor.transpose(turn_a[:, P:2 * P], p[:, 144:144 + P], ident)
                nc.tensor.transpose(turn_a[:, 2 * P:3 * P], p[:, 144 + P:144 + 2 * P], ident)
                nc.tensor.transpose(turn_a[0:META, 3 * P:4 * P], p[:, P:144], ident)
                nc.tensor.transpose(turn_b[0:META, 0:P], p[:, 144 + 2 * P:144 + TOK], ident).then_inc(b_turned.sem, 1)

            def b_values(l, h):
                pe.wait_ge(b_turn_copied.sem, b_turn_copied.at(l, 2 + 3 * (h + 1)))
                if h:
                    pe.wait_ge(y_done.sem, y_done.at(l, h))
                v = [v_b[0:rows, t, P * h:P * h + P] for t, rows in ((0, P), (1, P), (2, META))]
                c = slice(32 * h + 16, 32 * h + 32)
                groups = (((0, P), (v[0], prob_t[:, 0:P]), (v_b[0:META, 1, P * h:P * h + P], prob_t[0:META, 3 * P:4 * P])),
                          ((P, 2 * P), (v[0], prob_t[:, P:2 * P]), (v[1], prob_t[:, 2 * P:3 * P]),
                           (v[2], prob_t[0:META, 4 * P:5 * P])),
                          ((2 * P, TOK), (v[0], tail_t[:, c]), (v[1], tail_t[:, P + c.start:P + c.stop]),
                           (v[2], tail_v[:, c])))
                for (a, b), *terms in groups:
                    for i, (val, pt) in enumerate(terms):
                        ins = mm(outp[:, a:b], val, pt, start=(i == 0), stop=(i == len(terms) - 1))
                ins.then_inc(b_pv.sem, 1)

            def a_rotate(l, n):
                if n in (0, 1):
                    pe.wait_ge(b_exp.sem, b_exp.at(l, 9))
                if n in (2, 3):
                    pe.wait_ge(roped.sem, roped.at(l, 5 + 2 * (n - 1)))
                if n == 4:
                    pe.wait_ge(evacuated.sem, evacuated.at(l, OUT_A + 6))
                dst = stat if n == 4 else score[n % 2]
                mm(dst[:, 0:TOK], rotate, work[:, n, :], start=True, stop=True).then_inc(rotated.sem, 1)

            def a_turn_values(l):
                pe.wait_ge(b_turn_copied.sem, b_turn_copied.at(l, 14))
                nc.tensor.transpose(turn_a[0:80, 0:P], work[:, 5, 0:80], ident)
                for c in range(3):
                    ins = nc.tensor.transpose(turn_a[:, P * (c + 1):P * (c + 2)],
                                              work[:, 5, META + CHUNK * c:META + CHUNK * c + P], ident)
                ins.then_inc(v_turned.sem, 1)

            def a_meta_scores(l):
                for g in range(2):
                    for i in range(4):
                        r = slice(64 * (i % 2), 64 * (i % 2) + 64)
                        ins = mm(score[0][32 * i:32 * i + 32, META * g:META * g + META],
                                 a_q[r, META * (2 * g + i // 2):META * (2 * g + i // 2) + 32], a_k[r, g, 0:META], start=True, stop=True)
                ins.then_inc(a_score.sem, 1)

            def a_scores(l, n):
                g, par = divmod(n - 1, 2)
                if n >= 2:
                    pe.wait_ge(a_exp.sem, a_exp.at(l, 3 + 5 * (n - 2)))
                r = slice(64 * par, 64 * par + 64)
                dst = score[n % 2]
                queries = [a_q[r, 4 * META + 512 * g + P * c:4 * META + 512 * g + P * c + P] for c in range(4)]
                mm(dst[:, 0:80], queries[0], a_k[r, g, 0:80], start=True, stop=True)
                mm(dst[:, 80:224], queries[1], a_k[r, g, 0:144], start=True, stop=True)
                for c in (1, 2):
                    at = 80 + 144 * c
                    mm(dst[:, at:at + META], queries[c + 1], a_k[r, g, 0:META], start=True, stop=True)
                    k0 = META + CHUNK * c
                    ins = mm(dst[:, at + META:at + 144], queries[c + 1], a_k[r, g, k0:k0 + P],
                             start=True, stop=True)
                ins.then_inc(a_score.sem, 1)

            def a_turn_meta(l):
                pe.wait_ge(y_done.sem, y_done.at(l, Y_B_LAST))
                pe.wait_ge(a_prob.sem, a_prob.at(l, 1))
                for g in range(2):
                    ins = nc.tensor.transpose(outp[0:META, P * g:P * g + P], meta_p[:, META * g:META * g + META], ident)
                ins.then_inc(a_turned.sem, 1)

            def a_meta_values(l):
                pe.wait_ge(a_turn_copied.sem, a_turn_copied.at(l, 1))
                pe.wait_ge(v_copied.sem, v_copied.at(l, 2))
                pe.wait_ge(ln_root.sem, ln_root.at(l, 1))
                for g in range(2):
                    for par in range(2):
                        pt = meta_t[:, P * g:P * g + P].rearrange("p (i r q) -> p r i q", i=2, r=2)[:, par, :, 0:META]
                        ins = mm(stat[64 * par:64 * par + 64, 32 * g:32 * g + 32], a_v[0:META, 0, 64 * g:64 * g + 64], pt,
                                 start=True, stop=True)
                ins.then_inc(a_meta_pv.sem, 1)

            def a_turn(l, n):
                pe.wait_ge(a_prob.sem, a_prob.at(l, 1 + 2 * n))
                if n >= 2:
                    pe.wait_ge(a_turn_copied.sem, a_turn_copied.at(l, 1 + 3 * (n - 1)))
                p = prob[:, n % 2, :]
                nc.tensor.transpose(turn_a[0:80, 0:P], p[:, 0:80], ident)
                for c in range(3):
                    at = 80 + 144 * c
                    nc.tensor.transpose(turn_a[:, P * (c + 1):P * (c + 2)], p[:, at + META:at + 144], ident)
                    ins = nc.tensor.transpose(turn_b[0:META, P * c:P * c + P], p[:, at:at + META], ident)
                ins.then_inc(a_turned.sem, 1)

            def a_values(l, n):
                g, par = divmod(n - 1, 2)
                pe.wait_ge(a_turn_copied.sem, a_turn_copied.at(l, 1 + 3 * n))
                r, cols = slice(64 * par, 64 * par + 64), slice(64 * g, 64 * g + 64)
                if n == 3:
                    pe.wait_ge(y_done.sem, y_done.at(l, Y_A1))
                mm(outp[r, 0:P], a_v[0:80, 0, cols], prob_t[0:80, 0:P], start=True, stop=True)
                for c in range(3):
                    d = outp[r, P * (c + 1):P * (c + 2)]
                    mm(d, a_v[:, c + 1, cols], prob_t[:, P * (c + 1):P * (c + 2)], start=True, stop=False)
                    ins = mm(d, a_v[0:META, 0, cols], prob_t[0:META, 512 + P * c:512 + P * c + P], start=False, stop=True)
                ins.then_inc(a_pv.sem, 1)

            def feature_sum(src, dst, sig):
                mm(dst, ones, src, start=True, stop=True).then_inc(sig.sem, 1)

            pe.sem_inc(out_done.sem, 2)
            def layer(l, last):
                asked = wanted(last)
                def resid_ready(k):
                    pe.wait_ge(h_lo_done.sem, h_lo_done.at(l, k + 1))
                tile(l, OUT_D, 0, 0, 0, h_hi, h_lo, resid_ready)
                for i in (1, 7, 14):
                    pe.wait_ge(const_in[i], 16)

                def norm_midway(k):
                    if k == HALF:
                        norm_stat(l)
                tile(l, OUT_D + 1, 2, 1, 2, h_hi, h_lo, norm_midway)
                with pe.Fori(1, 4) as i:
                    pair(l, 2 * i, 4 * i, h_hi, h_lo)
                with pe.Fori(4, 6) as i:
                    pair(l, 2 * i, 4 * i, h_hi, h_lo, cols=asked)
                with pe.Fori(0, 2) as i:
                    pair(l, OUT_B + 2 * i, 2 * OUT_B + 4 * i, h_hi, h_lo, cols=asked)
                pair(l, OUT_B + 4, 2 * OUT_B + 8, h_hi, h_lo)
                pair(l, OUT_BG, 2 * OUT_BG, h_hi, h_lo, cols=asked)
                pe.wait_ge(lat_add.sem, lat_add.at(l, 3))
                feature_sum(lat_sq_q[:, 0, :], stat[:, 0:TOK], lat_sum)
                feature_sum(lat_sq_kv[:, 0, :], score[0][:, 0:TOK], lat_sum)
                pair(l, OUT_BG + 2, 2 * OUT_BG + 4, h_hi, h_lo, cols=asked)
                b_up(l)
                for i in range(5):
                    pair(l, OUT_A + 2 * i, 48 + 4 * i, h_hi, h_lo, cols=slice(0, TOK) if i == 2 else asked)
                    if i == 0:
                        b_tail_scores(l)
                    if i < 4:
                        b_scores(l, i)
                    if i == 1:
                        b_turn_tail(l)
                    if i >= 1:
                        b_turn(l, i - 1)
                    if i >= 2:
                        b_values(l, i - 2)
                a_rotate(l, 0)
                a_rotate(l, 1)
                for i in range(8):
                    pair(l, OUT_C + 2 * i, 68 + 4 * i, h_hi, h_lo, cols=asked if i % 2 else slice(0, TOK))
                    if i == 0:
                        b_values(l, 3)
                        for n in (2, 3, 4):
                            a_rotate(l, n)
                        a_turn_values(l)
                    if i == 1:
                        pe.wait_ge(roped.sem, roped.at(l, 17))
                        pe.wait_ge(ln_pre.sem, ln_pre.at(l, 3))
                        feature_sum(conv_tmp[:, 0, :], ln_stat, ln_sum)
                        a_meta_scores(l)
                    if 1 <= i <= 4:
                        a_scores(l, i)
                    if i == 2:
                        a_turn_meta(l)
                    if 2 <= i <= 5:
                        a_turn(l, i - 1)
                    if i == 4:
                        a_meta_values(l)
                    if 3 <= i <= 6:
                        a_values(l, i - 2)
                    if i == 3:
                        pe.wait_ge(ln_pre.sem, ln_pre.at(l, 6))
                        feature_sum(conv_tmp[:, 0, :], ln_stat, ln_var)
                def mix_ready(k):
                    if k == 0:
                        pe.wait_ge(mix_done.sem, mix_done.at(l, KT - 1))
                    if k == KT - 1:
                        pe.wait_ge(mix_done.sem, mix_done.at(l, KT))
                pair(l, OUT_O, 100, mix_hi, mix_lo, mix_ready, asked)
                with pe.Fori(1, 8) as i:
                    pair(l, OUT_O + 2 * i, 100 + 4 * i, mix_hi, mix_lo, cols=asked)

            with pe.Fori(0, DEPTH - 1) as l:
                layer(l, False)
            layer(DEPTH - 1, True)
            norm_stat(DEPTH)

        @block.scalar
        def _(act):
            fn = nc.scalar.activation

            def hi(l, u, slot, freed):
                act.wait_ge(landed[slot].sem, landed[slot].at(l, 4 * (u - slot) + 16))
                act.wait_ge(out_done.sem, out_done.at(l, freed + 1))
                nc.scalar.copy(w_hi[:, slot, :], raw_w[:, slot, :]).then_inc(hi_done.sem, 1)

            def ahead(l, out, u, slot):
                hi(l, u, slot, out - 1)
                hi(l, u + 1, slot + 1, out - 1)

            def root(dst, src, n, done, wait):
                act.wait_ge(wait[0], wait[1])
                fn(dst, src, ACT.Sqrt, bias=eps[:, 0:1], scale=1.0 / n).then_inc(done.sem, 1)

            def norm_root_of(l):
                root(rstd[:, :], stat[:, 0:TOK], D_MODEL, norm_root, (norm_sum.sem, norm_sum.at(l, 1)))

            def silu(l, out, dst):
                act.wait_ge(evacuated.sem, evacuated.at(l, out + 1))
                fn(dst, dst, ACT.Silu).then_inc(gate_done.sem, 1)

            seq = [0]

            def mix_high(l, place):
                k = seq[0]
                seq[0] += 1
                act.wait_ge(y_done.sem, y_done.at(l, k + 1))
                nc.scalar.copy(mix_hi[:, place, :], y_tmp[:, k % 2, :]).then_inc(y_hi.sem, 1)

            def b_exps(l, n):
                act.wait_ge(b_negmax.sem, b_negmax.at(l, n + 1))
                if n == 0:
                    fn(tail_p, turn_b[:, 0:TOK], ACT.Exp, bias=nm[:, FIRST:FIRST + 1], scale=B_SCALE,
                       accum_out=rs[:, FIRST:FIRST + 1]).then_inc(b_exp.sem, 1)
                    return
                h = n - 1
                if h >= 2:
                    act.wait_ge(b_turned.sem, b_turned.at(l, h))
                for j, (a, b) in enumerate(((0, 144), (144, 144 + TOK))):
                    fn(prob[:, h % 2, a:b], score[h % 2][:, a:b], ACT.Exp, bias=nm[:, j:j + 1], scale=B_SCALE,
                       accum_out=rs[:, j:j + 1]).then_inc(b_exp.sem, 1)

            def b_copy_tail(l):
                act.wait_ge(b_turned.sem, b_turned.at(l, 1))
                nc.scalar.copy(tail_t[:, 0:2 * P], outp[:, 0:2 * P]).then_inc(b_turn_copied.sem, 1)
                nc.scalar.copy(tail_v, outp[0:META, 2 * P:3 * P]).then_inc(b_turn_copied.sem, 1)

            def b_copy(l, h):
                act.wait_ge(b_turned.sem, b_turned.at(l, h + 2))
                if h:
                    act.wait_ge(b_pv.sem, b_pv.at(l, h))
                nc.scalar.copy(prob_t[:, 0:3 * P], turn_a[:, 0:3 * P]).then_inc(b_turn_copied.sem, 1)
                nc.scalar.copy(prob_t[0:META, 3 * P:4 * P], turn_a[0:META, 3 * P:4 * P]).then_inc(b_turn_copied.sem, 1)
                nc.scalar.copy(prob_t[0:META, 4 * P:5 * P], turn_b[0:META, 0:P]).then_inc(b_turn_copied.sem, 1)

            def a_exps(l, n):
                act.wait_ge(a_negmax.sem, a_negmax.at(l, n + 1))
                if n == 0:
                    for g in range(2):
                        c = slice(META * g, META * g + META)
                        fn(meta_p[:, c], score[0][:, c], ACT.Exp, bias=nm[:, FIRST + g:FIRST + g + 1], scale=A_SCALE,
                           accum_out=rs[:, FIRST + g:FIRST + g + 1]).then_inc(a_exp.sem, 1)
                    act.wait_ge(a_sinkarg.sem, a_sinkarg.at(l, 1))
                    fn(es[:, first], es[:, first], ACT.Exp).then_inc(a_exp.sem, 1)
                    return
                if n >= 3:
                    act.wait_ge(a_turned.sem, a_turned.at(l, n - 1))
                for c in range(4):
                    a, b = (0, 80) if c == 0 else (80 + 144 * (c - 1), 80 + 144 * c)
                    fn(prob[:, n % 2, a:b], score[n % 2][:, a:b], ACT.Exp, bias=nm[:, c:c + 1], scale=A_SCALE,
                       accum_out=rs[:, c:c + 1]).then_inc(a_exp.sem, 1)
                fn(es[:, 0:4], nm[:, 0:4], ACT.Exp, bias=sink[:, bass.ds(l, 1), n - 1:n].rearrange("p a b -> p (a b)")
                   ).then_inc(a_exp.sem, 1)

            def a_copy(l, n):
                act.wait_ge(a_turned.sem, a_turned.at(l, n + 1))
                if n == 0:
                    act.wait_ge(ln_center.sem, ln_center.at(l, 1))
                    nc.scalar.copy(meta_t, outp[0:META, 0:2 * P]).then_inc(a_turn_copied.sem, 1)
                    return
                if n >= 2:
                    act.wait_ge(a_pv.sem, a_pv.at(l, n - 1))
                nc.scalar.copy(prob_t[:, P:4 * P], turn_a[:, P:4 * P]).then_inc(a_turn_copied.sem, 1)
                nc.scalar.copy(prob_t[0:80, 0:P], turn_a[0:80, 0:P]).then_inc(a_turn_copied.sem, 1)
                nc.scalar.copy(prob_t[0:META, 512:512 + 3 * P], turn_b[0:META, 0:3 * P]).then_inc(a_turn_copied.sem, 1)

            act.wait_ge(zeroed, 1)
            fn(warm[:, :], eps[:, :], ACT.Square).then_inc(warmed, 1)
            act.wait_ge(const_in[0], 16)
            for k in range(KT):
                if k % 4 == 0:
                    act.wait_ge(x_in[k // 4], 16)
                fn(h_hi[:, k, :], resid[:, k, :], ACT.Copy, scale=norms[:, 0, k:k + 1]).then_inc(h_hi_done.sem, 1)
                for s in FIRST_UNITS.get(k, ()):
                    act.wait_ge(landed[s].sem, 16)
                    nc.scalar.copy(w_hi[:, s, :], raw_w[:, s, :]).then_inc(hi_done.sem, 1)
            fn(work[:, 0:4, :], resid[:, 12:16, :], ACT.Square).then_inc(sq_first, 1)
            act.wait_ge(const_in[5], 16)
            for i in range(8, 14):
                act.wait_ge(const_in[i], 16)
            def layer(l, last):
                seq[0] = 0
                act.wait_ge(warmed, 1)
                fn(warm[:, :], eps[:, :], ACT.Sqrt).then_inc(warmed, 1)
                hi(l, 4, 0, 0)
                norm_root_of(l)
                hi(l, 5, 1, 0)
                act.dma_start(attn[:, :, :], ukv_d[bass.ds(l, 1), :, :, :].rearrange("l p k n -> p (l k) n")).then_inc(ukv_in.sem, 16)
                def sigmoid(t):
                    act.wait_ge(evacuated.sem, evacuated.at(l, 2 * t + 2))
                    fn(work[:, 1, :], work[:, 1, :], ACT.Sigmoid).then_inc(glu_gate.sem, 1)
                sigmoid(0)
                with act.Fori(1, 4) as i:
                    ahead(l, 2 * i, 4 * i + 2, 2)
                    ahead(l, 2 * i + 1, 4 * i + 4, 0)
                    sigmoid(i)
                with act.Fori(0, 2) as i:
                    ahead(l, 8 + 2 * i, 18 + 4 * i, 2)
                    silu(l, 8 + 2 * i, flat(gate_d[:, bass.ds(2 * i, 1), :]))
                    ahead(l, 9 + 2 * i, 20 + 4 * i, 0)
                    silu(l, 9 + 2 * i, flat(gate_d[:, bass.ds(2 * i + 1, 1), :]))
                    act.wait_ge(ukv_in.sem, ukv_in.at(l, 16))
                    nc.scalar.copy(ukv_hi[:, bass.ds(i, 1), :], attn[:, bass.ds(i, 1), :]).then_inc(ukv_high.sem, 1)
                with act.Fori(0, 3) as i:
                    ahead(l, OUT_B + 2 * i, 26 + 4 * i, 2)
                    ahead(l, OUT_B + 1 + 2 * i, 28 + 4 * i, 0)
                act.wait_ge(evacuated.sem, evacuated.at(l, OUT_B + 4))
                fn(lat_sq_q, work[:, 0:4, :], ACT.Square).then_inc(lat_sq.sem, 1)
                ahead(l, OUT_BG, 38, 2)
                act.wait_ge(evacuated.sem, evacuated.at(l, OUT_B + 6))
                fn(lat_sq_kv, work[:, 4:6, :], ACT.Square).then_inc(lat_sq.sem, 1)
                silu(l, OUT_BG, gate_ab[:, 1, 0, :])
                ahead(l, OUT_BG + 1, 40, 0)
                silu(l, OUT_BG + 1, gate_ab[:, 1, 1, :])
                ahead(l, OUT_BG + 2, 42, 2)
                root(lat_rstd[:, 0, :], stat[:, 0:TOK], 512, lat_root, (lat_sum.sem, lat_sum.at(l, 1)))
                root(lat_rstd[:, 1, :], score[0][:, 0:TOK], 256, lat_root, (lat_sum.sem, lat_sum.at(l, 2)))
                for k in range(4):
                    act.wait_ge(lat_norm.sem, lat_norm.at(l, k + 1))
                    nc.scalar.copy(mix_hi[:, MIX_C + k, :], work[:, k, :]).then_inc(lat_hi.sem, 1)
                ahead(l, OUT_BG + 3, 44, 0)
                silu(l, OUT_BG + 2, gate_ab[:, 1, 2, :])
                hi(l, 46, 2, OUT_BG + 3)
                hi(l, 47, 3, OUT_BG + 3)
                for k in range(2):
                    act.wait_ge(lat_norm.sem, lat_norm.at(l, k + 5))
                    nc.scalar.copy(mix_hi[:, MIX_A + k, :], work[:, 4 + k, :]).then_inc(lat_hi.sem, 1)
                silu(l, OUT_BG + 3, gate_ab[:, 1, 3, :])
                hi(l, 48, 0, OUT_KR)
                hi(l, 49, 1, OUT_QR + 1)
                def b_attention(i):
                    if i == 0:
                        b_exps(l, 0)
                    if i < 4:
                        b_exps(l, 1 + i)
                    if i == 1:
                        b_copy_tail(l)
                    if i >= 1:
                        b_copy(l, i - 1)
                    if i >= 2:
                        mix_high(l, MIX_B + i - 2)

                for i in range(5):
                    out = OUT_A + 2 * i
                    if i == 0:
                        hi(l, 50, 2, out_of_unit(46))
                        hi(l, 51, 3, out_of_unit(47))
                    else:
                        ahead(l, out, 50 + 4 * i, 2)
                        b_attention(i - 1)
                    ahead(l, out + 1, 52 + 4 * i, 0)
                    if i >= 3:
                        silu(l, out, gate_ab[:, 0, 2 * (i - 3), :])
                    if i >= 4:
                        silu(l, out - 1, gate_ab[:, 0, 1, :])
                def a_attention(i):
                    if i == 0:
                        mix_high(l, MIX_B + 3)
                        act.wait_ge(v_turned.sem, v_turned.at(l, 1))
                        nc.scalar.copy(a_v[0:80, 0, :], turn_a[0:80, 0:P]).then_inc(v_copied.sem, 1)
                        nc.scalar.copy(a_v[:, 1:4, :], turn_a[:, P:4 * P].rearrange("p (c n) -> p c n", c=3)
                                       ).then_inc(v_copied.sem, 1)
                    if i == 1:
                        a_exps(l, 0)
                    if 1 <= i <= 4:
                        a_exps(l, i)
                    if i == 1:
                        act.wait_ge(ln_sum.sem, ln_sum.at(l, 1))
                        nc.scalar.mul(lat_rstd[:, 1, :], ln_stat, 1.0 / 512).then_inc(ln_mean.sem, 1)
                    if i == 2:
                        a_copy(l, 0)
                    if 2 <= i <= 5:
                        a_copy(l, i - 1)
                    if i % 2 == 1:
                        silu(l, OUT_C + 2 * i + 1, work[:, 4 * (i // 2 % 2) + 3, :])
                        mix_high(l, MIX_C + i // 2)
                    if i in (4, 6):
                        mix_high(l, MIX_A + i - 4)
                        mix_high(l, MIX_A + i - 3)

                for i in range(8):
                    out = OUT_C + 2 * i
                    ahead(l, out, 70 + 4 * i, 2)
                    if i == 0:
                        b_attention(4)
                        silu(l, OUT_A + 9, gate_ab[:, 0, 3, :])
                    else:
                        a_attention(i - 1)
                    if i == 4:
                        root(lat_rstd[:, 0, :], ln_stat, 512, ln_root, (ln_var.sem, ln_var.at(l, 1)))
                    if i == 6:
                        mix_high(l, MIX_D)
                        mix_high(l, MIX_D + 1)
                    ahead(l, out + 1, 72 + 4 * i, 0)
                    if i == 5:
                        act.wait_ge(ln_scaled.sem, ln_scaled.at(l, 1))
                        for t in range(GT):
                            fn(conv[:, t, :], conv[:, t, :], ACT.Silu,
                               scale=dvec[:, bass.ds(l, 1), 1, t:t + 1].rearrange("p a b -> p (a b)"),
                               bias=dvec[:, bass.ds(l, 1), 2, t:t + 1].rearrange("p a b -> p (a b)")
                               ).then_inc(ln_silu.sem, 1)
                    if i == 6:
                        mix_high(l, MIX_D + 2)
                        mix_high(l, MIX_D + 3)
                a_attention(7)
                def h_high(k):
                    if last:
                        return
                    act.wait_ge(evacuated.sem, evacuated.at(l, OUT_O + k + 1))
                    fn(flat(h_hi[:, bass.ds(k, 1), :]), flat(resid[:, bass.ds(k, 1), :]), ACT.Copy,
                       scale=flat(norms[:, bass.ds(l + 1, 1), bass.ds(k, 1)])).then_inc(h_hi_done.sem, 1)
                with act.Fori(0, 7) as i:
                    ahead(l, OUT_O + 2 * i, 102 + 4 * i, 2)
                    h_high(2 * i)
                    ahead(l, OUT_O + 1 + 2 * i, 104 + 4 * i, 0)
                    h_high(2 * i + 1)
                ahead(l, OUT_O + 14, 130, 2)
                h_high(14)
                if not last:
                    hi(l + 1, 0, 0, -2)
                    hi(l + 1, 1, 1, -2)
                h_high(15)
                if not last:
                    hi(l + 1, 2, 2, -1)
                    hi(l + 1, 3, 3, -1)

            with act.Fori(0, DEPTH - 1) as l:
                layer(l, False)
            layer(DEPTH - 1, True)
            act.wait_ge(warmed, 1 + DEPTH)
            fn(warm[:, :], eps[:, :], ACT.Sqrt).then_inc(warmed, 1)
            norm_root_of(DEPTH)

        @block.vector
        def _(dve):
            tt, stt, ts = nc.vector.tensor_tensor, nc.vector.scalar_tensor_tensor, nc.vector.tensor_scalar

            def lo(l, u, slot):
                dve.wait_ge(hi_done.sem, hi_done.at(l, u + 1))
                tt(w_lo[:, slot, :], raw_w[:, slot, :], w_hi[:, slot, :].bitcast(F32), ALU.subtract
                   ).then_inc(split_done.sem, 1)

            def ahead(l, u, slot):
                lo(l, u, slot)
                lo(l, u + 1, slot + 1)

            def evacuate(l, out, b, dst, cols=slice(0, TOK)):
                dve.wait_ge(out_done.sem, out_done.at(l, out + 1))
                tt(dst[:, cols], main[b][:, cols], rstd[:, cols], ALU.mult).then_inc(evacuated.sem, 1)

            def take(l, out, dst, rows=P, n=TOK):
                dve.wait_ge(out_done.sem, out_done.at(l, out + 1))
                nc.vector.tensor_copy(dst, main[out % 2][0:rows, 0:n]).then_inc(evacuated.sem, 1)

            def norm(l):
                dve.wait_ge(norm_root.sem, norm_root.at(l, 1))
                nc.vector.reciprocal(rstd[:, :], rstd[:, :]).then_inc(norm_done.sem, 1)
                dve.wait_ge(norm_done.sem, norm_done.at(l, 1))

            seq = [0]

            def mix_low(l, place):
                k = seq[0]
                seq[0] += 1
                dve.wait_ge(y_hi.sem, y_hi.at(l, k + 1))
                tt(mix_lo[:, place, :], y_tmp[:, k % 2, :], mix_hi[:, place, :].bitcast(F32), ALU.subtract
                   ).then_inc(mix_done.sem, 1)

            def y_slot(l):
                if seq[0] >= 2:
                    dve.wait_ge(mix_done.sem, mix_done.at(l, seq[0] - 1))
                return y_tmp[:, seq[0] % 2, :]

            def rope_parts(l, n, src, turned, dst):
                r = dst.shape[0]
                dve.wait_ge(rotated.sem, rotated.at(l, n + 1))
                tt(dst, src, cos[0:r, :], ALU.mult).then_inc(rope_cos.sem, 1)
                tt(rot_tmp[0:r, :], turned[0:r, 0:TOK], sin[0:r, :], ALU.mult).then_inc(rope_sin.sem, 1)
                dve.wait_ge(rope_sin.sem, rope_sin.at(l, n + 1))
                dve.wait_ge(rope_cos.sem, rope_cos.at(l, n + 1))

            def rope_b(l):
                for n in range(2):
                    if n:
                        dve.wait_ge(roped.sem, roped.at(l, 2))
                    part = y_tmp[:, n, :]
                    rope_parts(l, n, work[:, n, :], score[n], part)
                    for half in range(2):
                        r = slice(64 * half, 64 * half + 64)
                        tt(q_rope[0:64, 2 * n + half, :], part[r, :], rot_tmp[r, :], ALU.add).then_inc(roped.sem, 1)
                dve.wait_ge(roped.sem, roped.at(l, 4))
                rope_parts(l, 2, work[0:64, 6, :], stat, k_rope[0:64, :])
                tt(k_rope[0:64, :], k_rope[0:64, :], rot_tmp[0:64, :], ALU.add).then_inc(roped.sem, 1)
                dve.wait_ge(roped.sem, roped.at(l, 5))

            def rope_a_query(l, n):
                part = y_tmp[:, 0, :]
                dve.wait_ge(mix_done.sem, mix_done.at(l, seq[0]))
                rope_parts(l, 3 + n, work[:, n, :], score[n % 2], part)
                tt(a_q[:, META * n:META * n + META], part[:, 0:META], rot_tmp[:, 0:META], ALU.add).then_inc(roped.sem, 1)
                chunks = [x[:, META:TOK].rearrange("p (c q) -> p c q", c=4) for x in (part, rot_tmp)]
                tt(a_q_chunks[:, n // 2, n % 2], chunks[0], chunks[1], ALU.add).then_inc(roped.sem, 1)
                dve.wait_ge(roped.sem, roped.at(l, 5 + 2 * (n + 1)))

            def rope_a_key(l):
                part = y_tmp[:, 0, :]
                rope_parts(l, 7, work[:, 4, :], stat, part)
                for g in range(2):
                    src = slice(64 * g, 64 * g + 64)
                    for half in range(2):
                        tt(a_k[64 * half:64 * half + 64, g, :], part[src, :], rot_tmp[src, :], ALU.add
                           ).then_inc(roped.sem, 1)
                dve.wait_ge(roped.sem, roped.at(l, 17))

            def b_softmax_in(l, n):
                dve.wait_ge(b_score.sem, b_score.at(l, n + 1))
                parts = [turn_b[:, 0:TOK]] if n == 0 else [score[(n - 1) % 2][:, 0:144], score[(n - 1) % 2][:, 144:144 + TOK]]
                c0 = FIRST if n == 0 else 0
                for j, p in enumerate(parts):
                    nc.vector.reduce_max(mx[:, c0 + j:c0 + j + 1], p, AX).then_inc(b_max.sem, 1)
                w = c0 + len(parts)
                dve.wait_ge(b_max.sem, b_max.at(l, 1 if n == 0 else 1 + 2 * n))
                ts(nm[:, c0:w], mx[:, c0:w], -B_SCALE, None, ALU.mult).then_inc(b_negmax.sem, 1)

            def b_softmax_out(l, n):
                c = slice(FIRST, FIRST + 1) if n == 0 else slice(0, 2)
                dve.wait_ge(b_exp.sem, b_exp.at(l, 1 + 2 * n))
                nc.vector.reciprocal(rd[:, c], rs[:, c]).then_inc(b_recip.sem, 1)
                dve.wait_ge(b_recip.sem, b_recip.at(l, n + 1))
                if n == 0:
                    ts(tail_p, tail_p, rd[:, c], None, ALU.mult).then_inc(b_prob.sem, 1)
                    return
                for j, (a, b) in enumerate(((0, 144), (144, 144 + TOK))):
                    p = prob[:, (n - 1) % 2, a:b]
                    ts(p, p, rd[:, j:j + 1], None, ALU.mult).then_inc(b_prob.sem, 1)

            def b_output(l, h):
                dve.wait_ge(b_pv.sem, b_pv.at(l, h + 1))
                dve.wait_ge(gate_done.sem, gate_done.at(l, GT + h + 1))
                tt(y_slot(l), outp[:, 0:TOK], gate_ab[:, 1, h, :], ALU.mult).then_inc(y_done.sem, 1)
                mix_low(l, MIX_B + h)

            def a_softmax_in(l, n):
                dve.wait_ge(a_score.sem, a_score.at(l, n + 1))
                if n == 0:
                    nc.vector.reduce_max(mx[:, first], score[0][:, 0:2 * META].rearrange("p (g k) -> p g k", g=2), AX
                                         ).then_inc(a_max.sem, 1)
                    dve.wait_ge(a_max.sem, a_max.at(l, 1))
                    one = bass.ds(l, 1)
                    stt(out=nm[:, first], in0=mx[:, first], scalar=-A_SCALE,
                        in1=nsink_m[:, one, :].rearrange("p a b -> p (a b)"), op0=ALU.mult, op1=ALU.min
                        ).then_inc(a_negmax.sem, 1)
                    dve.wait_ge(a_negmax.sem, a_negmax.at(l, 1))
                    tt(es[:, first], nm[:, first], sink_m[:, one, :].rearrange("p a b -> p (a b)"), ALU.add
                       ).then_inc(a_sinkarg.sem, 1)
                    return
                s = score[n % 2]
                nc.vector.reduce_max(mx[:, 0:1], s[:, 0:80], AX).then_inc(a_max.sem, 1)
                nc.vector.reduce_max(mx[:, 1:4], s[:, 80:512].rearrange("p (c k) -> p c k", c=3), AX
                                     ).then_inc(a_max.sem, 1)
                dve.wait_ge(a_max.sem, a_max.at(l, 1 + 2 * n))
                ts(nm[:, 0:4], mx[:, 0:4], -A_SCALE, nsink[:, bass.ds(l, 1), n - 1:n].rearrange("p a b -> p (a b)"),
                   ALU.mult, ALU.min).then_inc(a_negmax.sem, 1)

            def a_softmax_out(l, n):
                c = first if n == 0 else slice(0, 4)
                dve.wait_ge(a_exp.sem, a_exp.at(l, 3 + 5 * n))
                tt(rs[:, c], rs[:, c], es[:, c], ALU.add).then_inc(a_den.sem, 1)
                dve.wait_ge(a_den.sem, a_den.at(l, n + 1))
                nc.vector.reciprocal(rd[:, c], rs[:, c]).then_inc(a_recip.sem, 1)
                dve.wait_ge(a_recip.sem, a_recip.at(l, n + 1))
                if n == 0:
                    p = meta_p[:, :].rearrange("p (g k) -> p g k", g=2)
                    tt(p, p, rd[:, first].unsqueeze(2).broadcast_to([P, 2, META]), ALU.mult).then_inc(a_prob.sem, 1)
                    return
                p = prob[:, n % 2, 0:80]
                ts(p, p, rd[:, 0:1], None, ALU.mult).then_inc(a_prob.sem, 1)
                p = prob[:, n % 2, 80:512].rearrange("p (c k) -> p c k", c=3)
                tt(p, p, rd[:, 1:4].unsqueeze(2).broadcast_to([P, 3, 144]), ALU.mult).then_inc(a_prob.sem, 1)

            def a_output(l, g):
                dve.wait_ge(a_pv.sem, a_pv.at(l, 2 * (g + 1)))
                dve.wait_ge(gate_done.sem, gate_done.at(l, 3 * GT))
                dve.wait_ge(meta_out.sem, meta_out.at(l, 1))
                for i in range(2):
                    y, gate = y_slot(l), gate_ab[:, 0, 2 * g + i, :]
                    tt(y[:, META:TOK].rearrange("p (c q) -> p c q", c=4),
                       outp[:, :].rearrange("p (c i q) -> p i c q", c=4, i=2)[:, i],
                       gate[:, META:TOK].rearrange("p (c q) -> p c q", c=4), ALU.mult).then_inc(y_parts.sem, 1)
                    tt(y[:, 0:META], meta_o[:, 32 * g + META * i:32 * g + META * i + META], gate[:, 0:META], ALU.mult
                       ).then_inc(y_done.sem, 1)
                    mix_low(l, MIX_A + 2 * g + i)
            def c_tile(l, t):
                b = 4 * (t % 2)
                lw = [cconv[:, bass.ds(l * GT + t, 1), j:j + 1].rearrange("p a b -> p (a b)") for j in range(C_TAPS)]
                y = y_slot(l)
                dve.wait_ge(c_prod.sem, c_prod.at(l, t + 1))
                ts(y, c_pad[:, 0:TOK], lw[0], None, ALU.mult).then_inc(c_step.sem, 1)
                for j in (1, 2):
                    dve.wait_ge(c_step.sem, c_step.at(l, 4 * t + j))
                    stt(out=y, in0=c_pad[:, j:j + TOK], scalar=lw[j], in1=y, op0=ALU.mult, op1=ALU.add
                        ).then_inc(c_step.sem, 1)
                dve.wait_ge(c_step.sem, c_step.at(l, 4 * t + 3))
                tt(y, y, work[:, b + 2, :], ALU.mult).then_inc(c_step.sem, 1)

            def d_output(l, n):
                dve.wait_ge(ln_silu.sem, ln_silu.at(l, n + 1))
                tt(y_slot(l), conv[:, n, :], gate_d[:, n, :], ALU.mult).then_inc(y_done.sem, 1)
                mix_low(l, MIX_D + n)

            def c_gate(l, t):
                y = y_slot(l)
                dve.wait_ge(c_step.sem, c_step.at(l, 4 * t + 4))
                dve.wait_ge(gate_done.sem, gate_done.at(l, 3 * GT + t + 1))
                tt(y, y, work[:, 4 * (t % 2) + 3, :], ALU.mult).then_inc(y_done.sem, 1)
                mix_low(l, MIX_C + t)

            dve.sem_inc(evacuated.sem, 2)
            nc.vector.memset(eps[:, :], EPS).then_inc(zeroed, 1)
            nc.vector.memset(c_pad[:, 0:C_PAD], 0.0).then_inc(zeroed, 1)
            dve.wait_ge(const_in[0], 16)
            for k in range(KT):
                if k % 4 == 0:
                    dve.wait_ge(x_in[k // 4], 16)
                dve.wait_ge(h_hi_done.sem, k + 1)
                stt(out=h_lo[:, k, :], in0=resid[:, k, :], scalar=norms[:, 0, k:k + 1], in1=h_hi[:, k, :].bitcast(F32),
                    op0=ALU.mult, op1=ALU.subtract).then_inc(h_lo_done.sem, 1)
                for s in FIRST_UNITS.get(k, ()):
                    dve.wait_ge(hi_done.sem, s + 1)
                    tt(w_lo[:, s, :], raw_w[:, s, :], w_hi[:, s, :].bitcast(F32), ALU.subtract).then_inc(split_done.sem, 1)
            dve.wait_ge(sq_first, 2)
            tt(conv[:, :, :], conv[:, :, :], work[:, 0:4, :], ALU.add).then_inc(sq_first, 1)
            dve.wait_ge(sq_first, 3)
            tt(conv[:, 0:2, :], conv[:, 0:2, :], conv[:, 2:4, :], ALU.add).then_inc(sq_first, 1)
            dve.wait_ge(sq_first, 4)
            tt(sumsq, conv[:, 0, :], conv[:, 1, :], ALU.add).then_inc(norm_in.sem, 1)
            for i in (2, 4, 6, 8, 9, 10, 11, 12, 13):
                dve.wait_ge(const_in[i], 16)
            ts(nsink[:, :, :], sink[:, :, :], -1.0, None, ALU.mult).then_inc(nsink_done, 1)
            ts(nsink_m[:, :, :], sink_m[:, :, :], -1.0, None, ALU.mult).then_inc(nsink_done, 1)
            dve.wait_ge(nsink_done, 2)
            dve.wait_ge(zeroed, 2)
            def layer(l, last):
                asked = wanted(last)
                seq[0] = 0
                lo(l, 4, 0)
                norm(l)

                def glu(t):
                    dve.wait_ge(glu_gate.sem, glu_gate.at(l, t + 1))
                    tt(u_pad[:, bass.ds(t, 1), D_PAD:D_PAD + TOK].rearrange("p a n -> p (a n)"),
                       work[:, 0, :], work[:, 1, :], ALU.mult).then_inc(glu_done.sem, 1)

                evacuate(l, 0, 0, work[:, 0, :])
                lo(l, 5, 1)
                evacuate(l, 1, 1, work[:, 1, :])
                glu(0)
                with dve.Fori(1, 4) as i:
                    ahead(l, 4 * i + 2, 2)
                    dve.wait_ge(glu_done.sem, glu_done.at(l, i))
                    evacuate(l, 2 * i, 0, work[:, 0, :])
                    ahead(l, 4 * i + 4, 0)
                    evacuate(l, 2 * i + 1, 1, work[:, 1, :])
                    glu(i)
                with dve.Fori(0, 2) as i:
                    ahead(l, 18 + 4 * i, 2)
                    evacuate(l, 8 + 2 * i, 0, flat(gate_d[:, bass.ds(2 * i, 1), :]), asked)
                    ahead(l, 20 + 4 * i, 0)
                    evacuate(l, 9 + 2 * i, 1, flat(gate_d[:, bass.ds(2 * i + 1, 1), :]), asked)
                    dve.wait_ge(ukv_high.sem, ukv_high.at(l, i + 1))
                    tt(ukv_lo[:, bass.ds(i, 1), :], attn[:, bass.ds(i, 1), :], ukv_hi[:, bass.ds(i, 1), :].bitcast(F32),
                       ALU.subtract).then_inc(ukv_split.sem, 1)
                with dve.Fori(0, 2) as i:
                    ahead(l, 26 + 4 * i, 2)
                    evacuate(l, OUT_B + 2 * i, 0, flat(work[:, bass.ds(2 * i, 1), :]), asked)
                    ahead(l, 28 + 4 * i, 0)
                    evacuate(l, OUT_B + 1 + 2 * i, 1, flat(work[:, bass.ds(2 * i + 1, 1), :]), asked)
                ahead(l, 34, 2)
                evacuate(l, OUT_B + 4, 0, work[:, 4, :])
                ahead(l, 36, 0)
                evacuate(l, OUT_B + 5, 1, work[:, 5, :])
                ahead(l, 38, 2)
                dve.wait_ge(lat_sq.sem, lat_sq.at(l, 1))
                tt(lat_sq_q[:, 0:2, :], lat_sq_q[:, 0:2, :], lat_sq_q[:, 2:4, :], ALU.add).then_inc(lat_add.sem, 1)
                dve.wait_ge(lat_add.sem, lat_add.at(l, 1))
                tt(lat_sq_q[:, 0, :], lat_sq_q[:, 0, :], lat_sq_q[:, 1, :], ALU.add).then_inc(lat_add.sem, 1)
                evacuate(l, OUT_BG, 0, gate_ab[:, 1, 0, :], asked)
                dve.wait_ge(lat_sq.sem, lat_sq.at(l, 2))
                tt(lat_sq_kv[:, 0, :], lat_sq_kv[:, 0, :], lat_sq_kv[:, 1, :], ALU.add).then_inc(lat_add.sem, 1)
                ahead(l, 40, 0)
                evacuate(l, OUT_BG + 1, 1, gate_ab[:, 1, 1, :], asked)

                def latent_scale(j):
                    dve.wait_ge(lat_root.sem, lat_root.at(l, j + 1))
                    nc.vector.reciprocal(lat_rstd[:, j, :], lat_rstd[:, j, :]).then_inc(lat_recip.sem, 1)

                def latent_norm(j, tiles):
                    dve.wait_ge(lat_recip.sem, lat_recip.at(l, j + 1))
                    for t in tiles:
                        stt(out=work[:, t, :], in0=work[:, t, :],
                            scalar=bnorm[:, bass.ds(l, 1), t:t + 1].rearrange("p a b -> p (a b)"),
                            in1=lat_rstd[:, j, :], op0=ALU.mult, op1=ALU.mult).then_inc(lat_norm.sem, 1)

                ahead(l, 42, 2)
                latent_scale(0)
                latent_norm(0, range(4))
                evacuate(l, OUT_BG + 2, 0, gate_ab[:, 1, 2, :], asked)
                latent_scale(1)
                ahead(l, 44, 0)

                def latent_low(k, place):
                    dve.wait_ge(lat_hi.sem, lat_hi.at(l, k + 1))
                    tt(mix_lo[:, place, :], work[:, k, :], mix_hi[:, place, :].bitcast(F32), ALU.subtract
                       ).then_inc(lat_lo.sem, 1)

                for k in range(4):
                    latent_low(k, MIX_C + k)
                latent_norm(1, range(4, 6))
                evacuate(l, OUT_BG + 3, 1, gate_ab[:, 1, 3, :], asked)
                ahead(l, 46, 2)
                dve.wait_ge(out_done.sem, out_done.at(l, OUT_KR + 1))
                tt(work[0:64, 6, :], main[0][0:64, 0:TOK], rstd[0:64, :], ALU.mult).then_inc(evacuated.sem, 1)
                latent_low(4, MIX_A)
                latent_low(5, MIX_A + 1)
                take(l, OUT_QR, work[:, 0, :])
                take(l, OUT_QR + 1, work[:, 1, :])
                for h in range(B_HEADS):
                    take(l, OUT_QN + h, q_nope[:, h, :])
                for h in range(B_HEADS):
                    take(l, OUT_KN + h, k_nope[:, h, :])
                for t in range(3):
                    rows = min(P, TOK - P * t)
                    take(l, OUT_V + t, v_b[0:rows, t, :], rows, 512)
                    if t < 2:
                        lo(l, 48 + t, t)
                dve.wait_ge(evacuated.sem, evacuated.at(l, OUT_QR + 2))
                for i in range(5):
                    out = OUT_A + 2 * i
                    dst = [work[:, 2 * i + j, :] if i < 3 else gate_ab[:, 0, 2 * (i - 3) + j, :] for j in range(2)]
                    cols = slice(0, TOK) if i == 2 else asked
                    if i == 1:
                        b_softmax_in(l, 0)
                    if i >= 1:
                        b_softmax_in(l, i)
                    ahead(l, 50 + 4 * i, 2)
                    if i == 0:
                        rope_b(l)
                    if i == 1:
                        b_softmax_out(l, 0)
                    if i >= 1:
                        b_softmax_out(l, i)
                    if i >= 3:
                        b_output(l, i - 3)
                    evacuate(l, out, 0, dst[0], cols)
                    ahead(l, 52 + 4 * i, 0)
                    evacuate(l, out + 1, 1, dst[1], cols)
                for i in range(8):
                    out, t = OUT_C + 2 * i, i // 2
                    b = 4 * (t % 2) + 2 * (i % 2)
                    cols = asked if i % 2 else slice(0, TOK)
                    if i == 2:
                        a_softmax_in(l, 0)
                    if 2 <= i <= 5:
                        a_softmax_in(l, i - 1)
                    ahead(l, 70 + 4 * i, 2)
                    if i == 0:
                        b_output(l, 2)
                        rope_a_query(l, 0)
                        rope_a_query(l, 1)
                        dve.wait_ge(roped.sem, roped.at(l, 9))
                    if i == 1:
                        b_output(l, 3)
                        rope_a_query(l, 2)
                        rope_a_query(l, 3)
                        rope_a_key(l)
                    if i == 2:
                        a_softmax_out(l, 0)
                    if 2 <= i <= 5:
                        a_softmax_out(l, i - 1)
                    if i in (2, 4, 6):
                        c_gate(l, t - 1)
                    if i == 5:
                        dve.wait_ge(a_meta_pv.sem, a_meta_pv.at(l, 1))
                        nc.vector.tensor_copy(meta_o[:, :], stat[:, 0:64]).then_inc(meta_out.sem, 1)
                    if i in (5, 7):
                        a_output(l, (i - 5) // 2)
                    if i == 6:
                        d_output(l, 0)
                        d_output(l, 1)
                    evacuate(l, out, 0, work[:, b, :], cols)
                    if i % 2 == 1:
                        c_tile(l, t)
                    ahead(l, 72 + 4 * i, 0)
                    if i == 2:
                        dve.wait_ge(ln_mean.sem, ln_mean.at(l, 1))
                        tt(conv[:, :, :], conv[:, :, :], lat_rstd[:, 1:2, :].broadcast_to([P, GT, TOK]), ALU.subtract
                           ).then_inc(ln_center.sem, 1)
                    if i == 4:
                        dve.wait_ge(ln_root.sem, ln_root.at(l, 1))
                        nc.vector.reciprocal(lat_rstd[:, 0, :], lat_rstd[:, 0, :]).then_inc(ln_recip.sem, 1)
                        dve.wait_ge(ln_recip.sem, ln_recip.at(l, 1))
                        tt(conv[:, :, :], conv[:, :, :], lat_rstd[:, 0:1, :].broadcast_to([P, GT, TOK]), ALU.mult
                           ).then_inc(ln_scaled.sem, 1)
                    if i == 6:
                        d_output(l, 2)
                        d_output(l, 3)
                    evacuate(l, out + 1, 1, work[:, b + 1, :], cols)
                    if i % 2 == 0:
                        dve.wait_ge(evacuated.sem, evacuated.at(l, out + 2))
                        tt(c_pad[:, C_PAD:C_PAD + TOK], work[:, b, :], work[:, b + 1, :], ALU.mult
                           ).then_inc(c_prod.sem, 1)
                c_gate(l, GT - 1)

                def add_resid(k, b):
                    dve.wait_ge(out_done.sem, out_done.at(l, OUT_O + k + 1))
                    r = flat(resid[:, bass.ds(k, 1), :])
                    tt(r[:, asked], main[b][:, asked], r[:, asked], ALU.add).then_inc(evacuated.sem, 1)
                    if last:
                        return
                    dve.wait_ge(h_hi_done.sem, h_hi_done.at(l + 1, k + 1))
                    stt(out=flat(h_lo[:, bass.ds(k, 1), :]), in0=r, scalar=flat(norms[:, bass.ds(l + 1, 1), bass.ds(k, 1)]),
                        in1=flat(h_hi[:, bass.ds(k, 1), :]).bitcast(F32), op0=ALU.mult, op1=ALU.subtract
                        ).then_inc(h_lo_done.sem, 1)

                with dve.Fori(0, 7) as i:
                    ahead(l, 102 + 4 * i, 2)
                    add_resid(2 * i, 0)
                    ahead(l, 104 + 4 * i, 0)
                    add_resid(2 * i + 1, 1)
                ahead(l, 130, 2)
                add_resid(14, 0)
                if not last:
                    ahead(l + 1, 0, 0)
                add_resid(15, 1)
                if not last:
                    ahead(l + 1, 2, 2)

            with dve.Fori(0, DEPTH - 1) as l:
                layer(l, False)
            layer(DEPTH - 1, True)
            norm(DEPTH)
            for k in range(4, KT):
                ins = stt(out=resid[:, k, META:TOK], in0=resid[:, k, META:TOK], scalar=norms[:, DEPTH, k:k + 1],
                          in1=rstd[:, META:TOK], op0=ALU.mult, op1=ALU.mult)
                if k % 2 == 1:
                    ins.then_inc(final_done[k // 2], 1)

        @block.gpsimd
        def _(pool):
            tt = nc.gpsimd.tensor_tensor
            squares = conv_tmp[:, 0, :]

            def sum_squares(l, k, done):
                pool.wait_ge(evacuated.sem, evacuated.at(l, OUT_O + k + 1))
                x = flat(resid[:, bass.ds(k, 1), :])
                if isinstance(k, int) and k == 0:
                    tt(sumsq, x, x, ALU.mult).then_inc(sq_done.sem, 1)
                    return
                pool.wait_ge(sq_done.sem, sq_done.at(l, 2 * k - 1))
                tt(squares, x, x, ALU.mult).then_inc(sq_done.sem, 1)
                pool.wait_ge(sq_done.sem, sq_done.at(l, 2 * k))
                tt(sumsq, sumsq, squares, ALU.add).then_inc(done.sem, 1)

            nc.gpsimd.memset(u_pad[:, :, 0:D_PAD], 0.0)
            pool.wait_ge(const_in[0], 16)
            for q in range(3):
                x = resid[:, 4 * q:4 * q + 4, :]
                pool.wait_ge(x_in[q], 16)
                if q == 0:
                    tt(conv[:, :, :], x, x, ALU.mult).then_inc(sq_pool, 1)
                    continue
                if q == 2:
                    pool.wait_ge(sq_pool, 3)
                tt(conv_tmp[:, :, :], x, x, ALU.mult).then_inc(sq_pool, 1)
                pool.wait_ge(sq_pool, 2 * q)
                tt(conv[:, :, :], conv[:, :, :], conv_tmp[:, :, :], ALU.add).then_inc(sq_pool if q == 1 else sq_first, 1)
            pool.wait_ge(const_in[3], 16)
            pool.wait_ge(const_in[5], 16)
            def layer(l, last):
                def tap(j, acc):
                    w = dconv[:, bass.ds(l * GT, GT), bass.ds(j, 1)].broadcast_to([P, GT, TOK])
                    tt(conv_tmp[:, :, :], u_pad[:, :, bass.ds(j, TOK)], w, ALU.mult).then_inc(tap_done.sem, 1)
                    pool.wait_ge(tap_done.sem, tap_done.at(l, 2 * j + 1))
                    tt(conv[:, :, :], acc, conv_tmp[:, :, :], ALU.add).then_inc(tap_done.sem, 1)

                pool.wait_ge(glu_done.sem, glu_done.at(l, GT))
                tap(0, dvec[:, bass.ds(l, 1), 0, :].rearrange("p a b -> p b a").broadcast_to([P, GT, TOK]))
                with pool.Fori(1, D_TAPS) as j:
                    pool.wait_ge(tap_done.sem, tap_done.at(l, 2 * j))
                    tap(j, conv[:, :, :])

                def tile_sums(l, k, src):
                    acc = conv_tmp[:, 0, :]
                    tt(acc, src[:, 0, :], src[:, 1, :], ALU.add).then_inc(ln_pre.sem, 1)
                    for n in (2, 3):
                        pool.wait_ge(ln_pre.sem, ln_pre.at(l, 3 * k + n - 1))
                        tt(acc, acc, src[:, n, :], ALU.add).then_inc(ln_pre.sem, 1)

                pool.wait_ge(tap_done.sem, tap_done.at(l, 2 * D_TAPS))
                tile_sums(l, 0, conv)
                pool.wait_ge(ln_center.sem, ln_center.at(l, 1))
                tt(conv_tmp[:, :, :], conv[:, :, :], conv[:, :, :], ALU.mult).then_inc(ln_sq.sem, 1)
                pool.wait_ge(ln_sq.sem, ln_sq.at(l, 1))
                tile_sums(l, 1, conv_tmp)

                sum_squares(l, 0, sq_done)
                with pool.Fori(1, KT - 1) as k:
                    sum_squares(l, k, sq_done)
                sum_squares(l, KT - 1, norm_in)

            with pool.Fori(0, DEPTH - 1) as l:
                layer(l, False)
            layer(DEPTH - 1, True)
            x = resid[:, 0:4, META:TOK]
            tt(x, x, norms[:, DEPTH, 0:4].unsqueeze(2).broadcast_to([P, 4, TOK - META]), ALU.mult).then_inc(weighted, 1)
            pool.wait_ge(weighted, 1)
            pool.wait_ge(norm_done.sem, norm_done.at(DEPTH, 1))
            for q in range(2):
                x = resid[:, 2 * q:2 * q + 2, META:TOK]
                tt(x, x, rstd[:, META:TOK].unsqueeze(1).broadcast_to([P, 2, TOK - META]), ALU.mult).then_inc(final_done[q], 1)


def kernel(x, meta_tokens, norm_w, w_in, a_sinks, b_q_norm, b_kv_norm, b_w_uq, b_w_ukv,
           c_conv_w, d_conv_w, d_conv_b, d_ln_w, d_ln_b, w_out, final_norm_w):
    import concourse.bacc as bacc
    from concourse.bass_utils import run_bass_kernel_spmd

    arr = {k: np.asarray(v) for k, v in dict(
        x=x, meta=meta_tokens, norm_w=norm_w, w_in=w_in, sinks=a_sinks, bq=b_q_norm, bkv=b_kv_norm, uq=b_w_uq,
        ukv=b_w_ukv, cw=c_conv_w, dw=d_conv_w, db=d_conv_b, lw=d_ln_w, lb=d_ln_b, w_out=w_out, fw=final_norm_w).items()}

    def by_feature(a):
        t = a.reshape(a.shape[:-1] + (a.shape[-1] // P, P))
        return np.ascontiguousarray(np.moveaxis(t, -1, 0))

    sizes = [512, 128, 128, 512, 512, 256, 64, 512, 512, 512, 512, 512, 512, 512, 512]
    names = ["aq", "ak", "av", "ag", "bcq", "bckv", "bkr", "bg", "cb", "cc", "cx", "cg", "da", "dgl", "dg"]
    start = dict(zip(names, np.cumsum([0] + sizes[:-1])))
    w_in_a, uq, w_o = arr["w_in"], arr["uq"], arr["w_out"]
    units = []

    def put(w):
        k, n = w.shape[0] // P, w.shape[1]
        per = UNIT // n
        t = w.reshape(k // per, per, P, n).transpose(0, 2, 1, 3).reshape(k // per, P, UNIT)
        units.extend(t)

    def tile(l, name, t):
        c = start[name] + P * t
        put(w_in_a[l][:, c:c + P])

    for l in range(DEPTH):
        for t in range(GT):
            tile(l, "da", t), tile(l, "dgl", t)
        for t in range(GT):
            tile(l, "dg", t)
        for t in range(GT):
            tile(l, "bcq", t)
        for t in range(2):
            tile(l, "bckv", t)
        for t in range(GT):
            tile(l, "bg", t)
        put(w_in_a[l][:, start["bkr"]:start["bkr"] + 64])
        q = uq[l].reshape(512, B_HEADS, 192)
        put(q[:, :, P:].reshape(512, 256))
        put(q[:, 0:2, :P].reshape(512, 256))
        put(q[:, 2:4, :P].reshape(512, 256))
        for t in range(GT):
            tile(l, "aq", t)
        tile(l, "ak", 0), tile(l, "av", 0)
        for t in range(GT):
            tile(l, "ag", t)
        for t in range(GT):
            tile(l, "cc", t), tile(l, "cx", t), tile(l, "cb", t), tile(l, "cg", t)
        rows = w_o[l].reshape(4, 512, D_MODEL)[[3, 1, 0, 2]].reshape(D_MODEL, D_MODEL)
        for t in range(KT):
            put(rows[:, P * t:P * t + P])
    assert len(units) == DEPTH * UNITS
    stream = np.stack(units).reshape(len(units) // RING, RING, P, UNIT)

    kv = arr["ukv"].reshape(DEPTH, 2, P, B_HEADS, 2, P)
    ukv = np.ascontiguousarray(kv.transpose(0, 2, 1, 4, 3, 5)).reshape(DEPTH, P, 2, UNIT)
    tokens = np.concatenate([arr["meta"], arr["x"][0]], axis=0)
    x_t = np.ascontiguousarray(by_feature(tokens).transpose(0, 2, 1))
    norms = by_feature(np.concatenate([arr["norm_w"], arr["fw"][None]], axis=0))
    bnorm = by_feature(np.concatenate([arr["bq"], arr["bkv"]], axis=1))
    dconv = np.ascontiguousarray(by_feature(arr["dw"]).transpose(0, 1, 3, 2)).reshape(P, DEPTH * GT, D_TAPS)
    cconv = np.ascontiguousarray(by_feature(arr["cw"]).transpose(0, 1, 3, 2)).reshape(P, DEPTH * GT, C_TAPS)
    dvec = by_feature(np.stack([arr["db"], arr["lw"], arr["lb"]], axis=1))

    inv = (1.0 / (np.float32(10000.0) ** (np.arange(0, 64, 2, dtype=np.float32) / np.float32(64)))).astype(np.float32)
    ang = (np.arange(TOK, dtype=np.float32)[:, None] * inv[None, :]).astype(np.float32)
    rope = np.stack([np.tile(np.cos(ang).T, (4, 1)), np.tile(np.sin(ang).T, (4, 1))], axis=1).astype(np.float32)
    chunk = np.where(np.arange(TOK) < META, 0, (np.arange(TOK) - META) // CHUNK + 1)
    mask = np.stack([(chunk[None] == np.arange(5)[:, None]) * 1.0, (chunk[None] > np.arange(5)[:, None]) * NEG],
                    axis=1).astype(np.float32)
    rot = np.zeros((P, P), np.float32)
    for m in range(P):
        if m % 64 < 32:
            rot[m + 32, m] = -1.0
        else:
            rot[m - 32, m] = 1.0
    mats = np.stack([np.eye(P, dtype=np.float32), np.ones((P, P), np.float32), rot], axis=1)

    nc = bacc.Bacc("TRN2", target_bir_lowering=False, num_devices=1)
    arrays = dict(stream=stream, ukv=ukv, x=x_t, norms=norms, bnorm=bnorm, dconv=dconv, cconv=cconv, dvec=dvec,
                  sinks=np.ascontiguousarray(arr["sinks"].reshape(DEPTH, 2, 2, 2).transpose(2, 0, 1, 3)).reshape(2, -1),
                  sinks_m=np.ascontiguousarray(arr["sinks"].reshape(DEPTH, 2, 4).transpose(2, 0, 1)).reshape(4, -1),
                  rope=rope, mask=mask, mats=mats)
    args = [nc.dram_tensor(f"{n}_dram", a.shape, F32, kind="ExternalInput").ap() for n, a in arrays.items()]
    out_ap = nc.dram_tensor("out_dram", (P, KT, TOK - META), F32, kind="ExternalOutput").ap()
    build(nc, *args, out_ap)
    r = run_bass_kernel_spmd(nc, [{f"{n}_dram": a for n, a in arrays.items()}], core_ids=[0])
    y = np.asarray(r.results[0]["out_dram"])
    return np.ascontiguousarray(y.transpose(2, 1, 0)).reshape(1, TOK - META, D_MODEL)
```

```python
import numpy as np
import concourse.bass as bass
import concourse.mybir as mybir
from concourse.alu_op_type import AluOpType as ALU
from contextlib import ExitStack

ACT = mybir.ActivationFunctionType
AX = mybir.AxisListType.X
F32 = mybir.dt.float32
F32R = mybir.dt.float32r

P = 128
D_MODEL = 2048
DEPTH = 2
META = 16
CHUNK = 64
TOK = 272
KT = D_MODEL // P
GT = KT // 4
UNIT = 1024
HALF = UNIT // P
RING = 4
UNITS = 132
OUTS = 78
EPS = 1e-6
NEG = -1e30
D_TAPS = 31
D_PAD = D_TAPS - 1
C_TAPS = 3
C_PAD = C_TAPS - 1
A_SCALE = 64 ** -0.5
B_SCALE = 192 ** -0.5
B_HEADS = 4
FIRST_UNITS = {3: [0], 7: [1], 15: [2, 3]}
FIRST = 4

OUT_D, OUT_B, OUT_BG, OUT_KR, OUT_QR, OUT_QN, OUT_KN, OUT_V, OUT_A, OUT_C, OUT_O = \
    0, 12, 18, 22, 23, 25, 29, 33, 36, 46, 62
U_KR, U_UQ = 44, 45

B_KEYS = (META + P, TOK)
B_TAIL = 240


def flat(ap):
    return ap.rearrange("p a b -> p (a b)")


def out_of_unit(u):
    if u < U_KR:
        return u // 2
    if u < U_UQ + 3:
        return OUT_KR + 2 * (u - U_KR)
    return (u + 24) // 2


def wanted(last):
    return slice(META, TOK) if last else slice(0, TOK)


def c_inputs(last):
    return slice(META - C_PAD, TOK) if last else slice(0, TOK)


class Signal:

    def __init__(self, sem, per, credit=0):
        self.sem, self.per, self.credit = sem, per, credit

    def at(self, layer, k):
        return layer * self.per + (k + self.credit)


def build(nc, stream, ukv_d, x_d, norms_d, bnorm_d, dconv_d, cconv_d, dvec_d, sinks_d, sinks_m_d,
          rope_d, mask_d, mats_d, out_d):
    ctx = ExitStack()
    with ctx:
        def sb(name, shape, dt=F32):
            return ctx.enter_context(nc.sbuf_tensor(name, shape, dt))

        def bank(name):
            return ctx.enter_context(nc.psum_tensor(name, [P, 512], F32))

        def sem(name):
            return ctx.enter_context(nc.semaphore(name))

        def signal(name, per, credit=0):
            return Signal(sem(name), per, credit)

        resid = sb("resid", [P, KT, TOK])
        h_hi = sb("h_hi", [P, KT, TOK], F32R)
        h_lo = sb("h_lo", [P, KT, TOK], F32R)
        mix_hi = sb("mix_hi", [P, KT, TOK], F32R)
        mix_lo = sb("mix_lo", [P, KT, TOK], F32R)
        raw_w = sb("raw_w", [P, RING, UNIT])
        w_hi = sb("w_hi", [P, RING, UNIT], F32R)
        w_lo = sb("w_lo", [P, RING, UNIT], F32R)
        rstd = sb("rstd", [P, TOK])
        lat_rstd = sb("lat_rstd", [P, 2, TOK])
        u_pad = sb("u_pad", [P, GT, D_PAD + TOK])
        conv = sb("conv", [P, GT, TOK])
        conv_tmp = sb("conv_tmp", [P, GT, TOK])
        gate_d = sb("gate_d", [P, GT, TOK])
        gate_ab = sb("gate_ab", [P, 2, GT, TOK])
        work = sb("work", [P, 8, TOK])
        q_nope = sb("q_nope", [P, GT, TOK])
        k_nope = sb("k_nope", [P, GT, TOK])
        q_rope = sb("q_rope", [64 + 5, B_HEADS, TOK])
        k_rope = sb("k_rope", [64 + 5, TOK])
        v_b = sb("v_b", [P, 3, B_HEADS * P])
        attn = sb("attn", [P, 2, UNIT])
        meta_p = sb("meta_p", [P, 2 * META])
        y_tmp = sb("y_tmp", [P, 2, TOK])
        c_pad = sb("c_pad", [P, C_PAD + TOK])
        norms = sb("norms", [P, DEPTH + 1, KT])
        bnorm = sb("bnorm", [P, DEPTH, 6])
        dconv = sb("dconv", [P, DEPTH * GT, D_TAPS])
        cconv = sb("cconv", [P, DEPTH * GT, C_TAPS])
        dvec = sb("dvec", [P, DEPTH, 3, GT])
        sink = sb("sink", [P, DEPTH, 4])
        sink_m = sb("sink_m", [P, DEPTH, 2])
        nsink = sb("nsink", [P, DEPTH, 4])
        nsink_m = sb("nsink_m", [P, DEPTH, 2])
        rope = sb("rope", [P, 2, TOK])
        mats = sb("mats", [P, 3, P])
        eps = sb("eps", [P, 1])
        warm = sb("warm", [P, 1])
        mx = sb("mx", [P, 8])
        nm = sb("nm", [P, 8])
        rs = sb("rs", [P, 8])
        es = sb("es", [P, 8])
        rd = sb("rd", [P, 8])

        first = slice(FIRST, FIRST + 2)
        meta_o = sb("meta_o", [P, 64])

        ident, ones, rotate = mats[:, 0, :], mats[:, 1, :], mats[:, 2, :]
        cos, sin = rope[:, 0, :], rope[:, 1, :]
        prob = attn[:, 0, :].rearrange("p (b n) -> p b n", b=2)
        prob_t = attn[:, 1, :]
        tail_p, tail_t = work[:, 6, :], work[:, 7, :]
        tail_v = prob_t[0:META, 5 * P:6 * P]
        sumsq = rot_tmp = lat_rstd[:, 1, :]
        meta_t = lat_rstd[0:META, 1, 0:2 * P]
        a_q, a_k = q_nope[:, :, :].rearrange("p t n -> p (t n)"), k_nope[:, 0:2, :]
        a_q_chunks = a_q[:, 4 * META:].rearrange("p (g c i q) -> p g i c q", g=2, c=4, i=2)
        a_windows = u_pad[:, :, D_PAD:D_PAD + 144].rearrange("p (c g) n -> p c g n", c=2)
        a_turned_sin = [u_pad[:, n, D_PAD:] for n in range(GT)] + [conv_tmp[:, 1, :]]
        a_v = k_nope[:, 2:4, :].rearrange("p t n -> p (t n)")[:, 0:4 * P].rearrange("p (c n) -> p c n", c=4)
        lat_sq_q = gate_ab[:, 0, :, :]
        lat_sq_kv = q_nope[:, 0:2, :]

        ukv_hi, ukv_lo = (m[:, 0:2 * GT, :].rearrange("p t n -> p (t n)")[:, 0:2 * UNIT].rearrange("p (k n) -> p k n", k=2)
                          for m in (mix_hi, mix_lo))

        kr_w = [w[:, 0, :].rearrange("p (k n) -> p k n", k=HALF) for w in (w_hi, w_lo)]
        kr_raw = [raw_w[:, 0, 512 * i:512 * i + 512].rearrange("p (k n) -> p k n", k=HALF) for i in range(2)]

        main = [bank("main0"), bank("main1")]
        stat = bank("stat")
        score = [bank("score0"), bank("score1")]
        turn_a, turn_b = bank("turn_a"), bank("turn_b")
        outp = bank("outp")

        ln_stat = stat[:, 64:64 + TOK]

        x_in = [sem(f"x_in{i}") for i in range(4)]
        const_in = [sem(f"const_in{i}") for i in range(15)]
        landed = [signal(f"landed{i}", 16 * UNITS // RING) for i in range(RING)]
        ukv_in = signal("ukv_in", 16)
        ukv_high = signal("ukv_high", 2)
        ukv_split = signal("ukv_split", 2)
        hi_done = signal("hi_done", UNITS)
        split_done = signal("split_done", UNITS)
        out_done = signal("out_done", OUTS, 2)
        evacuated = signal("evacuated", OUTS, 2)
        h_hi_done = signal("h_hi_done", KT)
        h_lo_done = signal("h_lo_done", KT)
        sq_done = signal("sq_done", 2 * KT - 2)
        sq_pool, sq_first = sem("sq_pool"), sem("sq_first")
        norm_in = signal("norm_in", 1)
        norm_sum = signal("norm_sum", 1)
        norm_root = signal("norm_root", 1)
        norm_done = signal("norm_done", 1)
        glu_gate = signal("glu_gate", GT)
        glu_done = signal("glu_done", GT)
        gate_done = signal("gate_done", 4 * GT)
        tap_done = signal("tap_done", 2 * D_TAPS)
        lat_sq = signal("lat_sq", 2)
        lat_add = signal("lat_add", 3)
        lat_sum = signal("lat_sum", 2)
        lat_root = signal("lat_root", 2)
        lat_recip = signal("lat_recip", 2)
        lat_norm = signal("lat_norm", 6)
        lat_hi = signal("lat_hi", 6)
        lat_lo = signal("lat_lo", 6)
        kr_part = signal("kr_part", 4)
        rotated = signal("rotated", 3)
        rope_cos = signal("rope_cos", 8)
        rope_sin = signal("rope_sin", 3)
        window_done = signal("window_done", 4)
        a_sin = signal("a_sin", 5 * 4)
        roped = signal("roped", 5 + 2 * 4 + 4)
        tail_score = signal("tail_score", 1)
        tail_max = signal("tail_max", 1)
        tail_negmax = signal("tail_negmax", 1)
        tail_exp = signal("tail_exp", 1)
        tail_recip = signal("tail_recip", 1)
        tail_prob = signal("tail_prob", 1)
        tail_turned = signal("tail_turned", 1)
        tail_copied = signal("tail_copied", 2)
        b_score = signal("b_score", 4)
        b_max = signal("b_max", 8)
        b_negmax = signal("b_negmax", 4)
        b_exp = signal("b_exp", 8)
        b_recip = signal("b_recip", 4)
        b_prob = signal("b_prob", 8)
        b_turned = signal("b_turned", 4)
        b_turn_copied = signal("b_turn_copied", 12)
        b_pv = signal("b_pv", 4)
        v_turned = signal("v_turned", 1)
        v_copied = signal("v_copied", 2)
        meta_score = signal("meta_score", 1)
        meta_max = signal("meta_max", 1)
        meta_negmax = signal("meta_negmax", 1)
        meta_sinkarg = signal("meta_sinkarg", 1)
        meta_exp = signal("meta_exp", 3)
        meta_den = signal("meta_den", 1)
        meta_recip = signal("meta_recip", 1)
        meta_prob = signal("meta_prob", 1)
        meta_turned = signal("meta_turned", 1)
        meta_copied = signal("meta_copied", 1)
        a_score = signal("a_score", 4)
        a_max = signal("a_max", 8)
        a_negmax = signal("a_negmax", 4)
        a_exp = signal("a_exp", 4 * 5)
        a_den = signal("a_den", 4)
        a_recip = signal("a_recip", 4)
        a_prob = signal("a_prob", 8)
        a_turned = signal("a_turned", 4)
        a_turn_copied = signal("a_turn_copied", 4 * 3)
        meta_pv = signal("meta_pv", 1)
        a_pv = signal("a_pv", 4)
        ln_pre = signal("ln_pre", 6)
        ln_sum = signal("ln_sum", 1)
        ln_mean = signal("ln_mean", 1)
        ln_center = signal("ln_center", 1)
        ln_sq = signal("ln_sq", 1)
        ln_var = signal("ln_var", 1)
        ln_root = signal("ln_root", 1)
        ln_recip = signal("ln_recip", 1)
        ln_scaled = signal("ln_scaled", 1)
        ln_silu = signal("ln_silu", GT)
        c_prod = signal("c_prod", GT)
        c_step = signal("c_step", 4 * GT)
        y_parts = signal("y_parts", GT)
        meta_out = signal("meta_out", 1)
        y_done = signal("y_done", KT)
        y_hi = signal("y_hi", KT)
        mix_done = signal("mix_done", KT)
        zeroed = sem("zeroed")
        warmed = sem("warmed")
        nsink_done = sem("nsink_done")
        final_done = [sem(f"final_done{i}") for i in range(8)]
        weighted = sem("weighted")
        last_sq = sem("last_sq")
        out_sent = [sem(f"out_sent{i}") for i in range(8)]

        MIX_D, MIX_B, MIX_A, MIX_C = 0, GT, 2 * GT, 3 * GT
        Y_B_LAST, Y_A1 = 4, 8

        block = ctx.enter_context(nc.Block())

        @block.sync
        def _(sp):
            def fetch(turn, slot):
                sp.dma_start(raw_w[:, slot, :], stream[bass.ds(turn, 1), slot, :, :].rearrange("u p n -> p (u n)")).then_inc(landed[slot].sem, 16)

            def const(i, dst, src):
                sp.dma_start(dst, src).then_inc(const_in[i], 16)

            const(0, norms[:, :, :], norms_d)
            for load in ("x0", "u0", "x1", "u1", "x2", "x3", "u2", "u3"):
                q = int(load[1])
                if load[0] == "x":
                    sp.dma_start(resid[:, 4 * q:4 * q + 4, :], x_d[:, 4 * q:4 * q + 4, :]).then_inc(x_in[q], 16)
                else:
                    fetch(0, q)
            const(1, mats[:, :, :], mats_d)
            const(2, bnorm[:, :, :], bnorm_d)
            const(3, dconv[:, :, :], dconv_d)
            const(4, cconv[:, :, :], cconv_d)
            const(5, dvec[:, :, :, :], dvec_d)
            const(6, rope[:, :, :], rope_d)
            const(7, k_rope[64:69, :], mask_d[:, 1, :])
            const(14, q_rope[64:69, :, :], mask_d[:, 0:1, :].broadcast_to([5, B_HEADS, TOK]))
            for i in range(2):
                const(8 + i, sink[64 * i:64 * i + 64, :, :].rearrange("p l c -> p (l c)"),
                      sinks_d[i:i + 1, :].broadcast_to([64, DEPTH * 4]))
            for i in range(4):
                const(10 + i, sink_m[32 * i:32 * i + 32, :, :].rearrange("p l g -> p (l g)"),
                      sinks_m_d[i:i + 1, :].broadcast_to([32, DEPTH * 2]))
            with sp.Fori(1, DEPTH * UNITS // RING) as turn:
                for s in range(RING):
                    sp.wait_ge(split_done.sem, (turn - 1) * RING + (s + 1))
                    fetch(turn, s)
            for q in (2, 3, 4, 0, 1, 5, 6, 7):
                sp.wait_ge(final_done[q], 1)
                sp.dma_start(out_d[:, 2 * q:2 * q + 2, :], resid[:, 2 * q:2 * q + 2, META:TOK]
                             ).then_inc(out_sent[q], 16)
            for q in range(8):
                sp.wait_ge(out_sent[q], 16)

        @block.tensor
        def _(pe):
            mm = nc.tensor.matmul

            def split_product(dst, pairs, last):
                n = len(pairs)
                for i, (whi, wlo, xhi, xlo) in enumerate(pairs):
                    mm(dst, wlo, xhi, start=(i == 0 and last[0]), stop=False)
                    mm(dst, whi, xlo, start=False, stop=False)
                    ins = mm(dst, whi, xhi, start=False, stop=(i == n - 1 and last[1]))
                return ins

            def tile(l, out, u, b, slot, hi, lo, ready=None, cols=slice(0, TOK)):
                pe.wait_ge(evacuated.sem, evacuated.at(l, out - 1))
                for half in range(2):
                    pe.wait_ge(split_done.sem, split_done.at(l, u + (half + 1)))
                    s = slot + half
                    for kk in range(HALF):
                        k = half * HALF + kk
                        if ready:
                            ready(k)
                        c = slice(kk * P, kk * P + P)
                        ins = split_product(main[b][:, cols],
                                            [(w_hi[:, s, c], w_lo[:, s, c], hi[:, k, cols], lo[:, k, cols])],
                                            (k == 0, k == KT - 1))
                ins.then_inc(out_done.sem, 1)

            def pair(l, out, u, hi, lo, ready=None, cols=slice(0, TOK)):
                tile(l, out, u, 0, 0, hi, lo, ready, cols)
                tile(l, out + 1, u + 2, 1, 2, hi, lo, None, cols)

            def norm_stat(l):
                pe.wait_ge(norm_in.sem, norm_in.at(l, 1))
                mm(stat[:, 0:TOK], ones, sumsq[:, :], start=True, stop=True).then_inc(norm_sum.sem, 1)

            def main_out(l, out, rows=P, n=TOK):
                pe.wait_ge(evacuated.sem, evacuated.at(l, out - 1))
                return main[out % 2][0:rows, 0:n]

            def b_up(l, asked):
                dst = main_out(l, OUT_KR)
                pe.wait_ge(split_done.sem, split_done.at(l, U_KR + 1))
                pe.wait_ge(lat_root.sem, lat_root.at(l, 1))
                for k in range(KT):
                    w = kr_w[k // HALF][:, k % HALF, :]
                    mm(dst, w, h_hi[:, k, :], start=(k == 0), stop=(k == KT - 1))
                    ins = mm(stat[0:64, 0:TOK], w[:, 64:128], h_lo[:, k, :], start=(k == 0), stop=(k == KT - 1))
                ins.then_inc(out_done.sem, 1)
                pe.wait_ge(lat_lo.sem, lat_lo.at(l, 4))
                for n in range(6):
                    out = OUT_QR + n
                    s = 1 + n // 2
                    dst = main_out(l, out)
                    pe.wait_ge(split_done.sem, split_done.at(l, U_UQ + n // 2 + 1))
                    cols = [slice(256 * k + P * (n % 2), 256 * k + P * (n % 2) + P) for k in range(GT)]
                    split_product(dst[:, asked], [(w_hi[:, s, c], w_lo[:, s, c], mix_hi[:, MIX_C + k, asked], mix_lo[:, MIX_C + k, asked])
                                        for k, c in enumerate(cols)], (True, True)).then_inc(out_done.sem, 1)
                pe.wait_ge(lat_lo.sem, lat_lo.at(l, 6))
                pe.wait_ge(ukv_split.sem, ukv_split.at(l, 2))
                for h in range(B_HEADS):
                    dst = main_out(l, OUT_KN + h)
                    c = slice(P * h, P * h + P)
                    split_product(dst, [(ukv_hi[:, k, c], ukv_lo[:, k, c], mix_hi[:, MIX_A + k, :], mix_lo[:, MIX_A + k, :])
                                        for k in range(2)], (True, True)).then_inc(out_done.sem, 1)
                for t in range(3):
                    rows = min(P, TOK - P * t)
                    dst = main_out(l, OUT_V + t, rows, 512)
                    r = slice(P * t, P * t + rows)
                    split_product(dst, [(mix_hi[:, MIX_A + k, r], mix_lo[:, MIX_A + k, r], ukv_hi[:, k, 512:], ukv_lo[:, k, 512:])
                                        for k in range(2)], (True, True)).then_inc(out_done.sem, 1)
                pe.wait_ge(evacuated.sem, evacuated.at(l, OUT_QR + 2))
                pe.wait_ge(kr_part.sem, kr_part.at(l, 4))
                for dst, src, r in ((score[0], 0, P), (score[1], 1, P), (stat, 6, 64)):
                    mm(dst[0:r, 0:TOK], rotate[0:r, 0:r], work[0:r, src, :], start=True, stop=True).then_inc(rotated.sem, 1)

            def b_tail_scores(l):
                for h in range(B_HEADS):
                    dst = turn_b[32 * h:32 * h + 32, 0:TOK]
                    mm(dst, q_nope[:, h, B_TAIL:TOK], k_nope[:, h, :], start=True, stop=False)
                    ins = mm(dst, q_rope[0:64, h, B_TAIL:TOK], k_rope[0:64, :], start=False, stop=True)
                ins.then_inc(tail_score.sem, 1)

            def b_scores(l, h, asked):
                if h >= 2:
                    pe.wait_ge(b_exp.sem, b_exp.at(l, 2 * h - 2))
                for tile, (keys, at) in enumerate(zip(B_KEYS, (0, B_KEYS[0]))):
                    q = slice(asked.start + P * tile, asked.start + P * tile + P)
                    dst = score[h % 2][:, at:at + keys]
                    mm(dst, q_nope[:, h, q], k_nope[:, h, 0:keys], start=True, stop=False)
                    ins = mm(dst, q_rope[:, h, q], k_rope[:, 0:keys], start=False, stop=True)
                ins.then_inc(b_score.sem, 1)

            def b_turn_tail(l):
                pe.wait_ge(tail_prob.sem, tail_prob.at(l, 1))
                nc.tensor.transpose(outp[:, 0:P], tail_p[:, 0:P], ident)
                nc.tensor.transpose(outp[:, P:2 * P], tail_p[:, P:2 * P], ident)
                nc.tensor.transpose(outp[0:META, 2 * P:3 * P], tail_p[:, 2 * P:TOK], ident).then_inc(tail_turned.sem, 1)

            def b_turn(l, h):
                pe.wait_ge(b_prob.sem, b_prob.at(l, 2 + 2 * h))
                if h:
                    pe.wait_ge(b_turn_copied.sem, b_turn_copied.at(l, 3 * h))
                p = prob[:, h % 2, :]
                nc.tensor.transpose(turn_a[:, 0:P], p[:, 0:P], ident)
                nc.tensor.transpose(turn_a[:, P:2 * P], p[:, 144:144 + P], ident)
                nc.tensor.transpose(turn_a[:, 2 * P:3 * P], p[:, 144 + P:144 + 2 * P], ident)
                nc.tensor.transpose(turn_a[0:META, 3 * P:4 * P], p[:, P:144], ident)
                nc.tensor.transpose(turn_b[0:META, 0:P], p[:, 144 + 2 * P:144 + TOK], ident).then_inc(b_turned.sem, 1)

            def b_values(l, h, last):
                pe.wait_ge(b_turn_copied.sem, b_turn_copied.at(l, 3 * (h + 1)))
                if h == 0 and not last:
                    pe.wait_ge(tail_copied.sem, tail_copied.at(l, 2))
                if h:
                    pe.wait_ge(y_done.sem, y_done.at(l, h))
                v = [v_b[0:rows, t, P * h:P * h + P] for t, rows in ((0, P), (1, P), (2, META))]
                c = slice(32 * h + 16, 32 * h + 32)
                q0 = META if last else 0
                groups = [((q0, q0 + P), (v[0], prob_t[:, 0:P]), (v_b[0:META, 1, P * h:P * h + P], prob_t[0:META, 3 * P:4 * P])),
                          ((q0 + P, q0 + 2 * P), (v[0], prob_t[:, P:2 * P]), (v[1], prob_t[:, 2 * P:3 * P]),
                           (v[2], prob_t[0:META, 4 * P:5 * P]))]
                if not last:
                    groups.append(((2 * P, TOK), (v[0], tail_t[:, c]), (v[1], tail_t[:, P + c.start:P + c.stop]),
                                   (v[2], tail_v[:, c])))
                for (a, b), *terms in groups:
                    for i, (val, pt) in enumerate(terms):
                        ins = mm(outp[:, a:b], val, pt, start=(i == 0), stop=(i == len(terms) - 1))
                ins.then_inc(b_pv.sem, 1)

            def a_turn_values(l):
                pe.wait_ge(b_turn_copied.sem, b_turn_copied.at(l, 12))
                nc.tensor.transpose(turn_a[0:80, 0:P], work[:, 5, 0:80], ident)
                for c in range(3):
                    ins = nc.tensor.transpose(turn_a[:, P * (c + 1):P * (c + 2)],
                                              work[:, 5, META + CHUNK * c:META + CHUNK * c + P], ident)
                ins.then_inc(v_turned.sem, 1)

            def a_meta_scores(l):
                for g in range(2):
                    for i in range(4):
                        r = slice(64 * (i % 2), 64 * (i % 2) + 64)
                        ins = mm(score[0][32 * i:32 * i + 32, META * g:META * g + META],
                                 a_q[r, META * (2 * g + i // 2):META * (2 * g + i // 2) + 32], a_k[r, g, 0:META], start=True, stop=True)
                ins.then_inc(meta_score.sem, 1)

            def a_scores(l, n, last):
                g, par = divmod(n - 1, 2)
                if n == 1:
                    pe.wait_ge(window_done.sem, window_done.at(l, 4))
                if n == 2 and not last:
                    pe.wait_ge(meta_exp.sem, meta_exp.at(l, 2))
                if n >= 3:
                    pe.wait_ge(a_exp.sem, a_exp.at(l, 5 * (n - 2)))
                r = slice(64 * par, 64 * par + 64)
                dst = score[n % 2]
                queries = [a_q[r, 4 * META + 512 * g + P * c:4 * META + 512 * g + P * c + P] for c in range(4)]
                mm(dst[:, 0:80], queries[0], a_k[r, g, 0:80], start=True, stop=True)
                mm(dst[:, 80:224], queries[1], a_k[r, g, 0:144], start=True, stop=True)
                for c in (1, 2):
                    at = 80 + 144 * c
                    ins = mm(dst[:, at:at + 144], queries[c + 1], a_windows[r, c - 1, g, :], start=True, stop=True)
                ins.then_inc(a_score.sem, 1)

            def a_turn_meta(l):
                pe.wait_ge(y_done.sem, y_done.at(l, Y_B_LAST))
                pe.wait_ge(meta_prob.sem, meta_prob.at(l, 1))
                for g in range(2):
                    ins = nc.tensor.transpose(outp[0:META, P * g:P * g + P], meta_p[:, META * g:META * g + META], ident)
                ins.then_inc(meta_turned.sem, 1)

            def a_meta_values(l):
                pe.wait_ge(meta_copied.sem, meta_copied.at(l, 1))
                pe.wait_ge(v_copied.sem, v_copied.at(l, 2))
                pe.wait_ge(ln_root.sem, ln_root.at(l, 1))
                for g in range(2):
                    for par in range(2):
                        pt = meta_t[:, P * g:P * g + P].rearrange("p (i r q) -> p r i q", i=2, r=2)[:, par, :, 0:META]
                        ins = mm(stat[64 * par:64 * par + 64, 32 * g:32 * g + 32], a_v[0:META, 0, 64 * g:64 * g + 64], pt,
                                 start=True, stop=True)
                ins.then_inc(meta_pv.sem, 1)

            def a_turn(l, n):
                pe.wait_ge(a_prob.sem, a_prob.at(l, 2 * n))
                if n >= 2:
                    pe.wait_ge(a_turn_copied.sem, a_turn_copied.at(l, 3 * (n - 1)))
                p = prob[:, n % 2, :]
                nc.tensor.transpose(turn_a[0:80, 0:P], p[:, 0:80], ident)
                for c in range(3):
                    at = 80 + 144 * c
                    nc.tensor.transpose(turn_a[:, P * (c + 1):P * (c + 2)], p[:, at + META:at + 144], ident)
                    ins = nc.tensor.transpose(turn_b[0:META, P * c:P * c + P], p[:, at:at + META], ident)
                ins.then_inc(a_turned.sem, 1)

            def a_values(l, n):
                g, par = divmod(n - 1, 2)
                pe.wait_ge(a_turn_copied.sem, a_turn_copied.at(l, 3 * n))
                r, cols = slice(64 * par, 64 * par + 64), slice(64 * g, 64 * g + 64)
                if n == 1:
                    pe.wait_ge(y_done.sem, y_done.at(l, Y_B_LAST))
                if n == 3:
                    pe.wait_ge(y_done.sem, y_done.at(l, Y_A1))
                mm(outp[r, 0:P], a_v[0:80, 0, cols], prob_t[0:80, 0:P], start=True, stop=True)
                for c in range(3):
                    d = outp[r, P * (c + 1):P * (c + 2)]
                    mm(d, a_v[:, c + 1, cols], prob_t[:, P * (c + 1):P * (c + 2)], start=True, stop=False)
                    ins = mm(d, a_v[0:META, 0, cols], prob_t[0:META, 512 + P * c:512 + P * c + P], start=False, stop=True)
                ins.then_inc(a_pv.sem, 1)

            def feature_sum(src, dst, sig):
                mm(dst, ones, src, start=True, stop=True).then_inc(sig.sem, 1)

            pe.sem_inc(out_done.sem, 2)
            def layer(l, last):
                asked = wanted(last)
                def resid_ready(k):
                    pe.wait_ge(h_lo_done.sem, h_lo_done.at(l, k + 1))
                tile(l, OUT_D, 0, 0, 0, h_hi, h_lo, resid_ready)
                for i in (1, 7, 14):
                    pe.wait_ge(const_in[i], 16)

                def norm_midway(k):
                    if k == HALF:
                        norm_stat(l)
                tile(l, OUT_D + 1, 2, 1, 2, h_hi, h_lo, norm_midway)
                with pe.Fori(1, 4) as i:
                    pair(l, 2 * i, 4 * i, h_hi, h_lo)
                with pe.Fori(4, 6) as i:
                    pair(l, 2 * i, 4 * i, h_hi, h_lo, cols=asked)
                with pe.Fori(0, 2) as i:
                    pair(l, OUT_B + 2 * i, 2 * OUT_B + 4 * i, h_hi, h_lo, cols=asked)
                pair(l, OUT_B + 4, 2 * OUT_B + 8, h_hi, h_lo)
                pair(l, OUT_BG, 2 * OUT_BG, h_hi, h_lo, cols=asked)
                pe.wait_ge(lat_add.sem, lat_add.at(l, 3))
                feature_sum(lat_sq_q[:, 0, :], stat[:, 0:TOK], lat_sum)
                feature_sum(lat_sq_kv[:, 0, :], score[0][:, 0:TOK], lat_sum)
                pair(l, OUT_BG + 2, 2 * OUT_BG + 4, h_hi, h_lo, cols=asked)
                b_up(l, asked)
                for i in range(5):
                    pair(l, OUT_A + 2 * i, 48 + 4 * i, h_hi, h_lo, cols=slice(0, TOK) if i == 2 else asked)
                    if i == 0:
                        pe.wait_ge(roped.sem, roped.at(l, 5))
                        pe.wait_ge(evacuated.sem, evacuated.at(l, OUT_V + 3))
                    if i == 0 and not last:
                        b_tail_scores(l)
                    if i < 4:
                        b_scores(l, i, asked)
                    if i == 1 and not last:
                        b_turn_tail(l)
                    if i >= 1:
                        b_turn(l, i - 1)
                    if i >= 2:
                        b_values(l, i - 2, last)
                for i in range(8):
                    pair(l, OUT_C + 2 * i, 68 + 4 * i, h_hi, h_lo, cols=asked if i % 2 else c_inputs(last))
                    if i == 0:
                        b_values(l, 3, last)
                        a_turn_values(l)
                    if i == 1:
                        pe.wait_ge(roped.sem, roped.at(l, 17))
                        pe.wait_ge(ln_pre.sem, ln_pre.at(l, 3))
                        feature_sum(conv_tmp[:, 0, :], ln_stat, ln_sum)
                        if not last:
                            a_meta_scores(l)
                    if 1 <= i <= 4:
                        a_scores(l, i, last)
                    if i == 2 and not last:
                        a_turn_meta(l)
                    if 2 <= i <= 5:
                        a_turn(l, i - 1)
                    if i == 4 and not last:
                        a_meta_values(l)
                    if 3 <= i <= 6:
                        a_values(l, i - 2)
                    if i == 3:
                        pe.wait_ge(ln_pre.sem, ln_pre.at(l, 6))
                        feature_sum(conv_tmp[:, 0, :], ln_stat, ln_var)
                def mix_ready(k):
                    if k == 0:
                        pe.wait_ge(mix_done.sem, mix_done.at(l, KT - 1))
                    if k == KT - 1:
                        pe.wait_ge(mix_done.sem, mix_done.at(l, KT))
                pair(l, OUT_O, 100, mix_hi, mix_lo, mix_ready, asked)
                with pe.Fori(1, 8) as i:
                    pair(l, OUT_O + 2 * i, 100 + 4 * i, mix_hi, mix_lo, cols=asked)

            with pe.Fori(0, DEPTH - 1) as l:
                layer(l, False)
            layer(DEPTH - 1, True)
            norm_stat(DEPTH)

        @block.scalar
        def _(act):
            fn = nc.scalar.activation

            def hi(l, u, slot, freed):
                act.wait_ge(landed[slot].sem, landed[slot].at(l, 4 * (u - slot) + 16))
                act.wait_ge(out_done.sem, out_done.at(l, freed + 1))
                nc.scalar.copy(w_hi[:, slot, :], raw_w[:, slot, :]).then_inc(hi_done.sem, 1)

            def ahead(l, out, u, slot):
                hi(l, u, slot, out - 1)
                hi(l, u + 1, slot + 1, out - 1)

            def root(dst, src, n, done, wait):
                act.wait_ge(wait[0], wait[1])
                fn(dst, src, ACT.Sqrt, bias=eps[:, 0:1], scale=1.0 / n).then_inc(done.sem, 1)

            def norm_root_of(l):
                root(rstd[:, :], stat[:, 0:TOK], D_MODEL, norm_root, (norm_sum.sem, norm_sum.at(l, 1)))

            def silu(l, out, dst):
                act.wait_ge(evacuated.sem, evacuated.at(l, out + 1))
                fn(dst, dst, ACT.Silu).then_inc(gate_done.sem, 1)

            seq = [0]

            def mix_high(l, place):
                k = seq[0]
                seq[0] += 1
                act.wait_ge(y_done.sem, y_done.at(l, k + 1))
                nc.scalar.copy(mix_hi[:, place, :], y_tmp[:, k % 2, :]).then_inc(y_hi.sem, 1)

            def b_exps(l, n):
                if n == 0:
                    act.wait_ge(tail_negmax.sem, tail_negmax.at(l, 1))
                    fn(tail_p, turn_b[:, 0:TOK], ACT.Exp, bias=nm[:, FIRST:FIRST + 1], scale=B_SCALE,
                       accum_out=rs[:, FIRST:FIRST + 1]).then_inc(tail_exp.sem, 1)
                    return
                h = n - 1
                act.wait_ge(b_negmax.sem, b_negmax.at(l, n))
                if h >= 2:
                    act.wait_ge(b_turned.sem, b_turned.at(l, h - 1))
                for j, (a, b) in enumerate(((0, 144), (144, 144 + TOK))):
                    fn(prob[:, h % 2, a:b], score[h % 2][:, a:b], ACT.Exp, bias=nm[:, j:j + 1], scale=B_SCALE,
                       accum_out=rs[:, j:j + 1]).then_inc(b_exp.sem, 1)

            def b_copy_tail(l):
                act.wait_ge(tail_turned.sem, tail_turned.at(l, 1))
                nc.scalar.copy(tail_t[:, 0:2 * P], outp[:, 0:2 * P]).then_inc(tail_copied.sem, 1)
                nc.scalar.copy(tail_v, outp[0:META, 2 * P:3 * P]).then_inc(tail_copied.sem, 1)

            def b_copy(l, h):
                act.wait_ge(b_turned.sem, b_turned.at(l, h + 1))
                if h:
                    act.wait_ge(b_pv.sem, b_pv.at(l, h))
                nc.scalar.copy(prob_t[:, 0:3 * P], turn_a[:, 0:3 * P]).then_inc(b_turn_copied.sem, 1)
                nc.scalar.copy(prob_t[0:META, 3 * P:4 * P], turn_a[0:META, 3 * P:4 * P]).then_inc(b_turn_copied.sem, 1)
                nc.scalar.copy(prob_t[0:META, 4 * P:5 * P], turn_b[0:META, 0:P]).then_inc(b_turn_copied.sem, 1)

            def a_exps(l, n):
                if n == 0:
                    act.wait_ge(meta_negmax.sem, meta_negmax.at(l, 1))
                    for g in range(2):
                        c = slice(META * g, META * g + META)
                        fn(meta_p[:, c], score[0][:, c], ACT.Exp, bias=nm[:, FIRST + g:FIRST + g + 1], scale=A_SCALE,
                           accum_out=rs[:, FIRST + g:FIRST + g + 1]).then_inc(meta_exp.sem, 1)
                    act.wait_ge(meta_sinkarg.sem, meta_sinkarg.at(l, 1))
                    fn(es[:, first], es[:, first], ACT.Exp).then_inc(meta_exp.sem, 1)
                    return
                act.wait_ge(a_negmax.sem, a_negmax.at(l, n))
                if n >= 3:
                    act.wait_ge(a_turned.sem, a_turned.at(l, n - 2))
                for c in range(4):
                    a, b = (0, 80) if c == 0 else (80 + 144 * (c - 1), 80 + 144 * c)
                    fn(prob[:, n % 2, a:b], score[n % 2][:, a:b], ACT.Exp, bias=nm[:, c:c + 1], scale=A_SCALE,
                       accum_out=rs[:, c:c + 1]).then_inc(a_exp.sem, 1)
                fn(es[:, 0:4], nm[:, 0:4], ACT.Exp, bias=sink[:, bass.ds(l, 1), n - 1:n].rearrange("p a b -> p (a b)")
                   ).then_inc(a_exp.sem, 1)

            def a_copy(l, n):
                if n == 0:
                    act.wait_ge(meta_turned.sem, meta_turned.at(l, 1))
                    act.wait_ge(ln_center.sem, ln_center.at(l, 1))
                    nc.scalar.copy(meta_t, outp[0:META, 0:2 * P]).then_inc(meta_copied.sem, 1)
                    return
                act.wait_ge(a_turned.sem, a_turned.at(l, n))
                if n >= 2:
                    act.wait_ge(a_pv.sem, a_pv.at(l, n - 1))
                nc.scalar.copy(prob_t[:, P:4 * P], turn_a[:, P:4 * P]).then_inc(a_turn_copied.sem, 1)
                nc.scalar.copy(prob_t[0:80, 0:P], turn_a[0:80, 0:P]).then_inc(a_turn_copied.sem, 1)
                nc.scalar.copy(prob_t[0:META, 512:512 + 3 * P], turn_b[0:META, 0:3 * P]).then_inc(a_turn_copied.sem, 1)

            act.wait_ge(zeroed, 1)
            fn(warm[:, :], eps[:, :], ACT.Square).then_inc(warmed, 1)
            act.wait_ge(const_in[0], 16)
            for k in range(KT):
                if k % 4 == 0:
                    act.wait_ge(x_in[k // 4], 16)
                fn(h_hi[:, k, :], resid[:, k, :], ACT.Copy, scale=norms[:, 0, k:k + 1]).then_inc(h_hi_done.sem, 1)
                for s in FIRST_UNITS.get(k, ()):
                    act.wait_ge(landed[s].sem, 16)
                    nc.scalar.copy(w_hi[:, s, :], raw_w[:, s, :]).then_inc(hi_done.sem, 1)
            fn(work[:, 0:4, :], resid[:, 12:16, :], ACT.Square).then_inc(sq_first, 1)
            act.wait_ge(const_in[5], 16)
            for i in range(8, 14):
                act.wait_ge(const_in[i], 16)
            def layer(l, last):
                seq[0] = 0
                act.wait_ge(warmed, 1)
                fn(warm[:, :], eps[:, :], ACT.Sqrt).then_inc(warmed, 1)
                hi(l, 4, 0, 0)
                norm_root_of(l)
                hi(l, 5, 1, 0)
                act.dma_start(attn[:, :, :], ukv_d[bass.ds(l, 1), :, :, :].rearrange("l p k n -> p (l k) n")).then_inc(ukv_in.sem, 16)
                def sigmoid(t):
                    act.wait_ge(evacuated.sem, evacuated.at(l, 2 * t + 2))
                    fn(work[:, 1, :], work[:, 1, :], ACT.Sigmoid).then_inc(glu_gate.sem, 1)
                sigmoid(0)
                with act.Fori(1, 4) as i:
                    ahead(l, 2 * i, 4 * i + 2, 2)
                    ahead(l, 2 * i + 1, 4 * i + 4, 0)
                    sigmoid(i)
                with act.Fori(0, 2) as i:
                    ahead(l, 8 + 2 * i, 18 + 4 * i, 2)
                    silu(l, 8 + 2 * i, flat(gate_d[:, bass.ds(2 * i, 1), :]))
                    ahead(l, 9 + 2 * i, 20 + 4 * i, 0)
                    silu(l, 9 + 2 * i, flat(gate_d[:, bass.ds(2 * i + 1, 1), :]))
                with act.Fori(0, 2) as i:
                    ahead(l, OUT_B + 2 * i, 26 + 4 * i, 2)
                    act.wait_ge(ukv_in.sem, ukv_in.at(l, 16))
                    nc.scalar.copy(ukv_hi[:, bass.ds(i, 1), :], attn[:, bass.ds(i, 1), :]).then_inc(ukv_high.sem, 1)
                    ahead(l, OUT_B + 1 + 2 * i, 28 + 4 * i, 0)
                ahead(l, OUT_B + 4, 34, 2)
                ahead(l, OUT_B + 5, 36, 0)
                act.wait_ge(evacuated.sem, evacuated.at(l, OUT_B + 4))
                fn(lat_sq_q, work[:, 0:4, :], ACT.Square).then_inc(lat_sq.sem, 1)
                ahead(l, OUT_BG, 38, 2)
                act.wait_ge(evacuated.sem, evacuated.at(l, OUT_B + 6))
                fn(lat_sq_kv, work[:, 4:6, :], ACT.Square).then_inc(lat_sq.sem, 1)
                silu(l, OUT_BG, gate_ab[:, 1, 0, :])
                ahead(l, OUT_BG + 1, 40, 0)
                silu(l, OUT_BG + 1, gate_ab[:, 1, 1, :])
                ahead(l, OUT_BG + 2, 42, 2)
                root(lat_rstd[:, 0, :], stat[:, 0:TOK], 512, lat_root, (lat_sum.sem, lat_sum.at(l, 1)))
                root(lat_rstd[:, 1, :], score[0][:, 0:TOK], 256, lat_root, (lat_sum.sem, lat_sum.at(l, 2)))
                for k in range(4):
                    act.wait_ge(lat_norm.sem, lat_norm.at(l, k + 1))
                    nc.scalar.copy(mix_hi[:, MIX_C + k, :], work[:, k, :]).then_inc(lat_hi.sem, 1)
                act.wait_ge(landed[0].sem, landed[0].at(l, 4 * U_KR + 16))
                act.wait_ge(out_done.sem, out_done.at(l, OUT_BG + 3))
                nc.scalar.copy(kr_w[0][:, :, 64:128], kr_raw[0])
                nc.scalar.copy(kr_w[1][:, :, 64:128], kr_raw[1]).then_inc(hi_done.sem, 1)
                hi(l, 45, 1, OUT_BG + 2)
                silu(l, OUT_BG + 2, gate_ab[:, 1, 2, :])
                hi(l, 46, 2, OUT_BG + 3)
                hi(l, 47, 3, OUT_BG + 3)
                for k in range(2):
                    act.wait_ge(lat_norm.sem, lat_norm.at(l, k + 5))
                    nc.scalar.copy(mix_hi[:, MIX_A + k, :], work[:, 4 + k, :]).then_inc(lat_hi.sem, 1)
                silu(l, OUT_BG + 3, gate_ab[:, 1, 3, :])
                hi(l, 48, 0, OUT_KR)
                hi(l, 49, 1, OUT_QR + 1)
                def b_attention(i):
                    if i == 0 and not last:
                        b_exps(l, 0)
                    if i < 4:
                        b_exps(l, 1 + i)
                    if i == 1 and not last:
                        b_copy_tail(l)
                    if i >= 1:
                        b_copy(l, i - 1)
                    if i >= 2:
                        mix_high(l, MIX_B + i - 2)

                for i in range(5):
                    out = OUT_A + 2 * i
                    if i == 0:
                        hi(l, 50, 2, out_of_unit(46))
                        hi(l, 51, 3, out_of_unit(47))
                    else:
                        ahead(l, out, 50 + 4 * i, 2)
                        b_attention(i - 1)
                    ahead(l, out + 1, 52 + 4 * i, 0)
                    if i >= 3:
                        silu(l, out, gate_ab[:, 0, 2 * (i - 3), :])
                    if i >= 4:
                        silu(l, out - 1, gate_ab[:, 0, 1, :])
                def a_attention(i):
                    if i == 0:
                        mix_high(l, MIX_B + 3)
                        act.wait_ge(v_turned.sem, v_turned.at(l, 1))
                        nc.scalar.copy(a_v[0:80, 0, :], turn_a[0:80, 0:P]).then_inc(v_copied.sem, 1)
                        nc.scalar.copy(a_v[:, 1:4, :], turn_a[:, P:4 * P].rearrange("p (c n) -> p c n", c=3)
                                       ).then_inc(v_copied.sem, 1)
                    if i == 1 and not last:
                        a_exps(l, 0)
                    if 1 <= i <= 4:
                        a_exps(l, i)
                    if i == 1:
                        act.wait_ge(ln_sum.sem, ln_sum.at(l, 1))
                        nc.scalar.mul(lat_rstd[:, 1, :], ln_stat, 1.0 / 512).then_inc(ln_mean.sem, 1)
                    if i == 2 and not last:
                        a_copy(l, 0)
                    if 2 <= i <= 5:
                        a_copy(l, i - 1)
                    if i % 2 == 1:
                        silu(l, OUT_C + 2 * i + 1, work[:, 4 * (i // 2 % 2) + 3, :])
                        mix_high(l, MIX_C + i // 2)
                    if i in (4, 6):
                        mix_high(l, MIX_A + i - 4)
                        mix_high(l, MIX_A + i - 3)

                for i in range(8):
                    out = OUT_C + 2 * i
                    ahead(l, out, 70 + 4 * i, 2)
                    if i == 0:
                        b_attention(4)
                        silu(l, OUT_A + 9, gate_ab[:, 0, 3, :])
                    else:
                        a_attention(i - 1)
                    if i == 4:
                        root(lat_rstd[:, 0, :], ln_stat, 512, ln_root, (ln_var.sem, ln_var.at(l, 1)))
                    if i == 6:
                        mix_high(l, MIX_D)
                        mix_high(l, MIX_D + 1)
                    ahead(l, out + 1, 72 + 4 * i, 0)
                    if i == 5:
                        act.wait_ge(ln_scaled.sem, ln_scaled.at(l, 1))
                        for t in range(GT):
                            fn(conv[:, t, :], conv[:, t, :], ACT.Silu,
                               scale=dvec[:, bass.ds(l, 1), 1, t:t + 1].rearrange("p a b -> p (a b)"),
                               bias=dvec[:, bass.ds(l, 1), 2, t:t + 1].rearrange("p a b -> p (a b)")
                               ).then_inc(ln_silu.sem, 1)
                    if i == 6:
                        mix_high(l, MIX_D + 2)
                        mix_high(l, MIX_D + 3)
                a_attention(7)
                def h_high(k):
                    if last:
                        return
                    act.wait_ge(evacuated.sem, evacuated.at(l, OUT_O + k + 1))
                    fn(flat(h_hi[:, bass.ds(k, 1), :]), flat(resid[:, bass.ds(k, 1), :]), ACT.Copy,
                       scale=flat(norms[:, bass.ds(l + 1, 1), bass.ds(k, 1)])).then_inc(h_hi_done.sem, 1)
                with act.Fori(0, 7) as i:
                    ahead(l, OUT_O + 2 * i, 102 + 4 * i, 2)
                    h_high(2 * i)
                    ahead(l, OUT_O + 1 + 2 * i, 104 + 4 * i, 0)
                    h_high(2 * i + 1)
                ahead(l, OUT_O + 14, 130, 2)
                h_high(14)
                if not last:
                    hi(l + 1, 0, 0, -2)
                    hi(l + 1, 1, 1, -2)
                h_high(15)
                if not last:
                    hi(l + 1, 2, 2, -1)
                    hi(l + 1, 3, 3, -1)

            with act.Fori(0, DEPTH - 1) as l:
                layer(l, False)
            layer(DEPTH - 1, True)
            act.wait_ge(warmed, 1 + DEPTH)
            fn(warm[:, :], eps[:, :], ACT.Sqrt).then_inc(warmed, 1)
            norm_root_of(DEPTH)

        @block.vector
        def _(dve):
            tt, stt, ts = nc.vector.tensor_tensor, nc.vector.scalar_tensor_tensor, nc.vector.tensor_scalar

            def lo(l, u, slot):
                dve.wait_ge(hi_done.sem, hi_done.at(l, u + 1))
                tt(w_lo[:, slot, :], raw_w[:, slot, :], w_hi[:, slot, :].bitcast(F32), ALU.subtract
                   ).then_inc(split_done.sem, 1)

            def ahead(l, u, slot):
                lo(l, u, slot)
                lo(l, u + 1, slot + 1)

            def evacuate(l, out, b, dst, cols=slice(0, TOK)):
                dve.wait_ge(out_done.sem, out_done.at(l, out + 1))
                tt(dst[:, cols], main[b][:, cols], rstd[:, cols], ALU.mult).then_inc(evacuated.sem, 1)

            def take(l, out, dst, rows=P, n=TOK):
                dve.wait_ge(out_done.sem, out_done.at(l, out + 1))
                nc.vector.tensor_copy(dst, main[out % 2][0:rows, 0:n]).then_inc(evacuated.sem, 1)

            def norm(l):
                dve.wait_ge(norm_root.sem, norm_root.at(l, 1))
                nc.vector.reciprocal(rstd[:, :], rstd[:, :]).then_inc(norm_done.sem, 1)
                dve.wait_ge(norm_done.sem, norm_done.at(l, 1))

            seq = [0]

            def mix_low(l, place):
                k = seq[0]
                seq[0] += 1
                dve.wait_ge(y_hi.sem, y_hi.at(l, k + 1))
                tt(mix_lo[:, place, :], y_tmp[:, k % 2, :], mix_hi[:, place, :].bitcast(F32), ALU.subtract
                   ).then_inc(mix_done.sem, 1)

            def y_slot(l):
                if seq[0] >= 2:
                    dve.wait_ge(mix_done.sem, mix_done.at(l, seq[0] - 1))
                return y_tmp[:, seq[0] % 2, :]

            def rope_parts(l, n, src, turned, dst):
                r = dst.shape[0]
                dve.wait_ge(rotated.sem, rotated.at(l, n + 1))
                tt(dst, src, cos[0:r, :], ALU.mult).then_inc(rope_cos.sem, 1)
                tt(rot_tmp[0:r, :], turned[0:r, 0:TOK], sin[0:r, :], ALU.mult).then_inc(rope_sin.sem, 1)
                dve.wait_ge(rope_sin.sem, rope_sin.at(l, n + 1))
                dve.wait_ge(rope_cos.sem, rope_cos.at(l, n + 1))

            def rope_b(l):
                for n in range(2):
                    if n:
                        dve.wait_ge(roped.sem, roped.at(l, 2))
                    part = y_tmp[:, n, :]
                    rope_parts(l, n, work[:, n, :], score[n], part)
                    for half in range(2):
                        r = slice(64 * half, 64 * half + 64)
                        tt(q_rope[0:64, 2 * n + half, :], part[r, :], rot_tmp[r, :], ALU.add).then_inc(roped.sem, 1)
                dve.wait_ge(roped.sem, roped.at(l, 4))
                rope_parts(l, 2, work[0:64, 6, :], stat, k_rope[0:64, :])
                tt(k_rope[0:64, :], k_rope[0:64, :], rot_tmp[0:64, :], ALU.add).then_inc(roped.sem, 1)
                dve.wait_ge(roped.sem, roped.at(l, 5))

            def rope_a_parts(l, n):
                part = y_tmp[:, 0, :]
                tt(part, work[:, n, :], cos, ALU.mult).then_inc(rope_cos.sem, 1)
                dve.wait_ge(rope_cos.sem, rope_cos.at(l, 4 + n))
                dve.wait_ge(a_sin.sem, a_sin.at(l, 4 * (n + 1)))
                return part, a_turned_sin[n]

            def rope_a_query(l, n):
                dve.wait_ge(mix_done.sem, mix_done.at(l, seq[0]))
                parts = rope_a_parts(l, n)
                tt(a_q[:, META * n:META * n + META], parts[0][:, 0:META], parts[1][:, 0:META], ALU.add).then_inc(roped.sem, 1)
                chunks = [x[:, META:TOK].rearrange("p (c q) -> p c q", c=4) for x in parts]
                tt(a_q_chunks[:, n // 2, n % 2], chunks[0], chunks[1], ALU.add).then_inc(roped.sem, 1)
                dve.wait_ge(roped.sem, roped.at(l, 5 + 2 * (n + 1)))

            def rope_a_key(l):
                parts = rope_a_parts(l, 4)
                for g in range(2):
                    src = slice(64 * g, 64 * g + 64)
                    for half in range(2):
                        tt(a_k[64 * half:64 * half + 64, g, :], parts[0][src, :], parts[1][src, :], ALU.add
                           ).then_inc(roped.sem, 1)
                dve.wait_ge(roped.sem, roped.at(l, 17))

            def b_softmax_in(l, n):
                scored, at_max, negated = (tail_score, tail_max, tail_negmax) if n == 0 else (b_score, b_max, b_negmax)
                dve.wait_ge(scored.sem, scored.at(l, max(n, 1)))
                parts = [turn_b[:, 0:TOK]] if n == 0 else [score[(n - 1) % 2][:, 0:144], score[(n - 1) % 2][:, 144:144 + TOK]]
                c0 = FIRST if n == 0 else 0
                for j, p in enumerate(parts):
                    nc.vector.reduce_max(mx[:, c0 + j:c0 + j + 1], p, AX).then_inc(at_max.sem, 1)
                w = c0 + len(parts)
                dve.wait_ge(at_max.sem, at_max.at(l, max(2 * n, 1)))
                ts(nm[:, c0:w], mx[:, c0:w], -B_SCALE, None, ALU.mult).then_inc(negated.sem, 1)

            def b_softmax_out(l, n):
                c = slice(FIRST, FIRST + 1) if n == 0 else slice(0, 2)
                summed, inverted = (tail_exp, tail_recip) if n == 0 else (b_exp, b_recip)
                dve.wait_ge(summed.sem, summed.at(l, max(2 * n, 1)))
                nc.vector.reciprocal(rd[:, c], rs[:, c]).then_inc(inverted.sem, 1)
                dve.wait_ge(inverted.sem, inverted.at(l, max(n, 1)))
                if n == 0:
                    ts(tail_p, tail_p, rd[:, c], None, ALU.mult).then_inc(tail_prob.sem, 1)
                    return
                for j, (a, b) in enumerate(((0, 144), (144, 144 + TOK))):
                    p = prob[:, (n - 1) % 2, a:b]
                    ts(p, p, rd[:, j:j + 1], None, ALU.mult).then_inc(b_prob.sem, 1)

            def b_output(l, h, asked):
                dve.wait_ge(b_pv.sem, b_pv.at(l, h + 1))
                dve.wait_ge(gate_done.sem, gate_done.at(l, GT + h + 1))
                tt(y_slot(l)[:, asked], outp[:, asked], gate_ab[:, 1, h, asked], ALU.mult).then_inc(y_done.sem, 1)
                mix_low(l, MIX_B + h)

            def a_softmax_in(l, n):
                if n == 0:
                    dve.wait_ge(meta_score.sem, meta_score.at(l, 1))
                    nc.vector.reduce_max(mx[:, first], score[0][:, 0:2 * META].rearrange("p (g k) -> p g k", g=2), AX
                                         ).then_inc(meta_max.sem, 1)
                    dve.wait_ge(meta_max.sem, meta_max.at(l, 1))
                    one = bass.ds(l, 1)
                    stt(out=nm[:, first], in0=mx[:, first], scalar=-A_SCALE,
                        in1=nsink_m[:, one, :].rearrange("p a b -> p (a b)"), op0=ALU.mult, op1=ALU.min
                        ).then_inc(meta_negmax.sem, 1)
                    dve.wait_ge(meta_negmax.sem, meta_negmax.at(l, 1))
                    tt(es[:, first], nm[:, first], sink_m[:, one, :].rearrange("p a b -> p (a b)"), ALU.add
                       ).then_inc(meta_sinkarg.sem, 1)
                    return
                dve.wait_ge(a_score.sem, a_score.at(l, n))
                s = score[n % 2]
                nc.vector.reduce_max(mx[:, 0:1], s[:, 0:80], AX).then_inc(a_max.sem, 1)
                nc.vector.reduce_max(mx[:, 1:4], s[:, 80:512].rearrange("p (c k) -> p c k", c=3), AX
                                     ).then_inc(a_max.sem, 1)
                dve.wait_ge(a_max.sem, a_max.at(l, 2 * n))
                ts(nm[:, 0:4], mx[:, 0:4], -A_SCALE, nsink[:, bass.ds(l, 1), n - 1:n].rearrange("p a b -> p (a b)"),
                   ALU.mult, ALU.min).then_inc(a_negmax.sem, 1)

            def a_softmax_out(l, n):
                c = first if n == 0 else slice(0, 4)
                summed, added, inverted = (meta_exp, meta_den, meta_recip) if n == 0 else (a_exp, a_den, a_recip)
                dve.wait_ge(summed.sem, summed.at(l, 3 if n == 0 else 5 * n))
                tt(rs[:, c], rs[:, c], es[:, c], ALU.add).then_inc(added.sem, 1)
                dve.wait_ge(added.sem, added.at(l, max(n, 1)))
                nc.vector.reciprocal(rd[:, c], rs[:, c]).then_inc(inverted.sem, 1)
                dve.wait_ge(inverted.sem, inverted.at(l, max(n, 1)))
                if n == 0:
                    p = meta_p[:, :].rearrange("p (g k) -> p g k", g=2)
                    tt(p, p, rd[:, first].unsqueeze(2).broadcast_to([P, 2, META]), ALU.mult).then_inc(meta_prob.sem, 1)
                    return
                p = prob[:, n % 2, 0:80]
                ts(p, p, rd[:, 0:1], None, ALU.mult).then_inc(a_prob.sem, 1)
                p = prob[:, n % 2, 80:512].rearrange("p (c k) -> p c k", c=3)
                tt(p, p, rd[:, 1:4].unsqueeze(2).broadcast_to([P, 3, 144]), ALU.mult).then_inc(a_prob.sem, 1)

            def a_output(l, g, last):
                dve.wait_ge(a_pv.sem, a_pv.at(l, 2 * (g + 1)))
                dve.wait_ge(gate_done.sem, gate_done.at(l, 3 * GT))
                if not last:
                    dve.wait_ge(meta_out.sem, meta_out.at(l, 1))
                for i in range(2):
                    y, gate = y_slot(l), gate_ab[:, 0, 2 * g + i, :]
                    tt(y[:, META:TOK].rearrange("p (c q) -> p c q", c=4),
                       outp[:, :].rearrange("p (c i q) -> p i c q", c=4, i=2)[:, i],
                       gate[:, META:TOK].rearrange("p (c q) -> p c q", c=4), ALU.mult).then_inc(y_done.sem if last else y_parts.sem, 1)
                    if not last:
                        tt(y[:, 0:META], meta_o[:, 32 * g + META * i:32 * g + META * i + META], gate[:, 0:META], ALU.mult
                           ).then_inc(y_done.sem, 1)
                    mix_low(l, MIX_A + 2 * g + i)
            def c_tile(l, t):
                b = 4 * (t % 2)
                lw = [cconv[:, bass.ds(l * GT + t, 1), j:j + 1].rearrange("p a b -> p (a b)") for j in range(C_TAPS)]
                y = y_slot(l)
                dve.wait_ge(c_prod.sem, c_prod.at(l, t + 1))
                ts(y, c_pad[:, 0:TOK], lw[0], None, ALU.mult).then_inc(c_step.sem, 1)
                for j in (1, 2):
                    dve.wait_ge(c_step.sem, c_step.at(l, 4 * t + j))
                    stt(out=y, in0=c_pad[:, j:j + TOK], scalar=lw[j], in1=y, op0=ALU.mult, op1=ALU.add
                        ).then_inc(c_step.sem, 1)
                dve.wait_ge(c_step.sem, c_step.at(l, 4 * t + 3))
                tt(y, y, work[:, b + 2, :], ALU.mult).then_inc(c_step.sem, 1)

            def d_output(l, n):
                dve.wait_ge(ln_silu.sem, ln_silu.at(l, n + 1))
                tt(y_slot(l), conv[:, n, :], gate_d[:, n, :], ALU.mult).then_inc(y_done.sem, 1)
                mix_low(l, MIX_D + n)

            def c_gate(l, t):
                y = y_slot(l)
                dve.wait_ge(c_step.sem, c_step.at(l, 4 * t + 4))
                dve.wait_ge(gate_done.sem, gate_done.at(l, 3 * GT + t + 1))
                tt(y, y, work[:, 4 * (t % 2) + 3, :], ALU.mult).then_inc(y_done.sem, 1)
                mix_low(l, MIX_C + t)

            dve.sem_inc(evacuated.sem, 2)
            nc.vector.memset(eps[:, :], EPS).then_inc(zeroed, 1)
            nc.vector.memset(c_pad[:, 0:C_PAD], 0.0).then_inc(zeroed, 1)
            dve.wait_ge(const_in[0], 16)
            for k in range(KT):
                if k % 4 == 0:
                    dve.wait_ge(x_in[k // 4], 16)
                dve.wait_ge(h_hi_done.sem, k + 1)
                stt(out=h_lo[:, k, :], in0=resid[:, k, :], scalar=norms[:, 0, k:k + 1], in1=h_hi[:, k, :].bitcast(F32),
                    op0=ALU.mult, op1=ALU.subtract).then_inc(h_lo_done.sem, 1)
                for s in FIRST_UNITS.get(k, ()):
                    dve.wait_ge(hi_done.sem, s + 1)
                    tt(w_lo[:, s, :], raw_w[:, s, :], w_hi[:, s, :].bitcast(F32), ALU.subtract).then_inc(split_done.sem, 1)
            dve.wait_ge(sq_first, 2)
            tt(conv[:, :, :], conv[:, :, :], work[:, 0:4, :], ALU.add).then_inc(sq_first, 1)
            dve.wait_ge(sq_first, 3)
            tt(conv[:, 0:2, :], conv[:, 0:2, :], conv[:, 2:4, :], ALU.add).then_inc(sq_first, 1)
            dve.wait_ge(sq_first, 4)
            tt(sumsq, conv[:, 0, :], conv[:, 1, :], ALU.add).then_inc(norm_in.sem, 1)
            for i in (2, 4, 6, 8, 9, 10, 11, 12, 13):
                dve.wait_ge(const_in[i], 16)
            ts(nsink[:, :, :], sink[:, :, :], -1.0, None, ALU.mult).then_inc(nsink_done, 1)
            ts(nsink_m[:, :, :], sink_m[:, :, :], -1.0, None, ALU.mult).then_inc(nsink_done, 1)
            dve.wait_ge(nsink_done, 2)
            dve.wait_ge(zeroed, 2)
            def layer(l, last):
                asked = wanted(last)
                seq[0] = 0
                lo(l, 4, 0)
                norm(l)

                def glu(t):
                    dve.wait_ge(glu_gate.sem, glu_gate.at(l, t + 1))
                    tt(u_pad[:, bass.ds(t, 1), D_PAD:D_PAD + TOK].rearrange("p a n -> p (a n)"),
                       work[:, 0, :], work[:, 1, :], ALU.mult).then_inc(glu_done.sem, 1)

                evacuate(l, 0, 0, work[:, 0, :])
                lo(l, 5, 1)
                evacuate(l, 1, 1, work[:, 1, :])
                glu(0)
                with dve.Fori(1, 4) as i:
                    ahead(l, 4 * i + 2, 2)
                    dve.wait_ge(glu_done.sem, glu_done.at(l, i))
                    evacuate(l, 2 * i, 0, work[:, 0, :])
                    ahead(l, 4 * i + 4, 0)
                    evacuate(l, 2 * i + 1, 1, work[:, 1, :])
                    glu(i)
                with dve.Fori(0, 2) as i:
                    ahead(l, 18 + 4 * i, 2)
                    evacuate(l, 8 + 2 * i, 0, flat(gate_d[:, bass.ds(2 * i, 1), :]), asked)
                    ahead(l, 20 + 4 * i, 0)
                    evacuate(l, 9 + 2 * i, 1, flat(gate_d[:, bass.ds(2 * i + 1, 1), :]), asked)
                with dve.Fori(0, 2) as i:
                    ahead(l, 26 + 4 * i, 2)
                    evacuate(l, OUT_B + 2 * i, 0, flat(work[:, bass.ds(2 * i, 1), :]), asked)
                    dve.wait_ge(ukv_high.sem, ukv_high.at(l, i + 1))
                    tt(ukv_lo[:, bass.ds(i, 1), :], attn[:, bass.ds(i, 1), :], ukv_hi[:, bass.ds(i, 1), :].bitcast(F32),
                       ALU.subtract).then_inc(ukv_split.sem, 1)
                    ahead(l, 28 + 4 * i, 0)
                    evacuate(l, OUT_B + 1 + 2 * i, 1, flat(work[:, bass.ds(2 * i + 1, 1), :]), asked)
                ahead(l, 34, 2)
                evacuate(l, OUT_B + 4, 0, work[:, 4, :])
                ahead(l, 36, 0)
                evacuate(l, OUT_B + 5, 1, work[:, 5, :])
                ahead(l, 38, 2)
                dve.wait_ge(lat_sq.sem, lat_sq.at(l, 1))
                tt(lat_sq_q[:, 0:2, :], lat_sq_q[:, 0:2, :], lat_sq_q[:, 2:4, :], ALU.add).then_inc(lat_add.sem, 1)
                dve.wait_ge(lat_add.sem, lat_add.at(l, 1))
                tt(lat_sq_q[:, 0, :], lat_sq_q[:, 0, :], lat_sq_q[:, 1, :], ALU.add).then_inc(lat_add.sem, 1)
                evacuate(l, OUT_BG, 0, gate_ab[:, 1, 0, :], asked)
                dve.wait_ge(lat_sq.sem, lat_sq.at(l, 2))
                tt(lat_sq_kv[:, 0, :], lat_sq_kv[:, 0, :], lat_sq_kv[:, 1, :], ALU.add).then_inc(lat_add.sem, 1)
                ahead(l, 40, 0)
                evacuate(l, OUT_BG + 1, 1, gate_ab[:, 1, 1, :], asked)

                def latent_scale(j):
                    dve.wait_ge(lat_root.sem, lat_root.at(l, j + 1))
                    nc.vector.reciprocal(lat_rstd[:, j, :], lat_rstd[:, j, :]).then_inc(lat_recip.sem, 1)

                def latent_norm(j, tiles):
                    dve.wait_ge(lat_recip.sem, lat_recip.at(l, j + 1))
                    for t in tiles:
                        stt(out=work[:, t, :], in0=work[:, t, :],
                            scalar=bnorm[:, bass.ds(l, 1), t:t + 1].rearrange("p a b -> p (a b)"),
                            in1=lat_rstd[:, j, :], op0=ALU.mult, op1=ALU.mult).then_inc(lat_norm.sem, 1)

                ahead(l, 42, 2)
                latent_scale(0)
                latent_norm(0, range(4))
                evacuate(l, OUT_BG + 2, 0, gate_ab[:, 1, 2, :], asked)
                latent_scale(1)
                dve.wait_ge(hi_done.sem, hi_done.at(l, U_KR + 1))
                tt(kr_w[0][:, :, 0:64], kr_raw[0], kr_w[0][:, :, 64:128].bitcast(F32), ALU.subtract)
                tt(kr_w[1][:, :, 0:64], kr_raw[1], kr_w[1][:, :, 64:128].bitcast(F32), ALU.subtract
                   ).then_inc(split_done.sem, 1)
                lo(l, 45, 1)

                def latent_low(k, place):
                    dve.wait_ge(lat_hi.sem, lat_hi.at(l, k + 1))
                    tt(mix_lo[:, place, :], work[:, k, :], mix_hi[:, place, :].bitcast(F32), ALU.subtract
                       ).then_inc(lat_lo.sem, 1)

                for k in range(4):
                    latent_low(k, MIX_C + k)
                latent_norm(1, range(4, 6))
                evacuate(l, OUT_BG + 3, 1, gate_ab[:, 1, 3, :], asked)
                dve.wait_ge(out_done.sem, out_done.at(l, OUT_KR + 1))
                tt(work[0:64, 6, :], main[0][0:64, 0:TOK], rstd[0:64, :], ALU.mult).then_inc(kr_part.sem, 1)
                tt(work[0:64, 7, :], main[0][64:128, 0:TOK], rstd[64:128, :], ALU.mult).then_inc(evacuated.sem, 1)
                lo(l, 46, 2)
                take(l, OUT_QR, work[:, 0, :])
                lo(l, 47, 3)
                take(l, OUT_QR + 1, work[:, 1, :])
                latent_low(4, MIX_A)
                latent_low(5, MIX_A + 1)
                for h in range(B_HEADS):
                    take(l, OUT_QN + h, q_nope[:, h, :])
                    if h in (1, 2):
                        if h == 2:
                            tt(work[0:64, 7, :], stat[0:64, 0:TOK], rstd[0:64, :], ALU.mult).then_inc(kr_part.sem, 1)
                        dve.wait_ge(kr_part.sem, kr_part.at(l, 2 * h - 1))
                        dve.wait_ge(evacuated.sem, evacuated.at(l, OUT_KR + 1))
                        tt(work[0:64, 6, :], work[0:64, 6, :], work[0:64, 7, :], ALU.add).then_inc(kr_part.sem, 1)
                        dve.wait_ge(kr_part.sem, kr_part.at(l, 2 * h))
                for h in range(B_HEADS):
                    take(l, OUT_KN + h, k_nope[:, h, :])
                for t in range(3):
                    rows = min(P, TOK - P * t)
                    take(l, OUT_V + t, v_b[0:rows, t, :], rows, 512)
                    if t < 2:
                        lo(l, 48 + t, t)
                dve.wait_ge(evacuated.sem, evacuated.at(l, OUT_QR + 2))
                for i in range(5):
                    out = OUT_A + 2 * i
                    dst = [work[:, 2 * i + j, :] if i < 3 else gate_ab[:, 0, 2 * (i - 3) + j, :] for j in range(2)]
                    cols = slice(0, TOK) if i == 2 else asked
                    if i == 1 and not last:
                        b_softmax_in(l, 0)
                    if i >= 1:
                        b_softmax_in(l, i)
                    ahead(l, 50 + 4 * i, 2)
                    if i == 0:
                        rope_b(l)
                    if i == 1 and not last:
                        b_softmax_out(l, 0)
                    if i >= 1:
                        b_softmax_out(l, i)
                    if i >= 3:
                        b_output(l, i - 3, asked)
                    evacuate(l, out, 0, dst[0], cols)
                    ahead(l, 52 + 4 * i, 0)
                    evacuate(l, out + 1, 1, dst[1], cols)
                for i in range(8):
                    out, t = OUT_C + 2 * i, i // 2
                    b = 4 * (t % 2) + 2 * (i % 2)
                    cols = asked if i % 2 else c_inputs(last)
                    if i == 2 and not last:
                        a_softmax_in(l, 0)
                    if 2 <= i <= 5:
                        a_softmax_in(l, i - 1)
                    ahead(l, 70 + 4 * i, 2)
                    if i == 0:
                        b_output(l, 2, asked)
                        rope_a_query(l, 0)
                        rope_a_query(l, 1)
                        dve.wait_ge(roped.sem, roped.at(l, 9))
                    if i == 1:
                        b_output(l, 3, asked)
                        rope_a_query(l, 2)
                        rope_a_query(l, 3)
                        rope_a_key(l)
                    if i == 2 and not last:
                        a_softmax_out(l, 0)
                    if 2 <= i <= 5:
                        a_softmax_out(l, i - 1)
                    if i in (2, 4, 6):
                        c_gate(l, t - 1)
                    if i == 5 and not last:
                        dve.wait_ge(meta_pv.sem, meta_pv.at(l, 1))
                        nc.vector.tensor_copy(meta_o[:, :], stat[:, 0:64]).then_inc(meta_out.sem, 1)
                    if i in (5, 7):
                        a_output(l, (i - 5) // 2, last)
                    if i == 6:
                        d_output(l, 0)
                        d_output(l, 1)
                    evacuate(l, out, 0, work[:, b, :], cols)
                    if i % 2 == 1:
                        c_tile(l, t)
                    ahead(l, 72 + 4 * i, 0)
                    if i == 2:
                        dve.wait_ge(ln_mean.sem, ln_mean.at(l, 1))
                        tt(conv[:, :, :], conv[:, :, :], lat_rstd[:, 1:2, :].broadcast_to([P, GT, TOK]), ALU.subtract
                           ).then_inc(ln_center.sem, 1)
                    if i == 4:
                        dve.wait_ge(ln_root.sem, ln_root.at(l, 1))
                        nc.vector.reciprocal(lat_rstd[:, 0, :], lat_rstd[:, 0, :]).then_inc(ln_recip.sem, 1)
                        dve.wait_ge(ln_recip.sem, ln_recip.at(l, 1))
                        tt(conv[:, :, :], conv[:, :, :], lat_rstd[:, 0:1, :].broadcast_to([P, GT, TOK]), ALU.mult
                           ).then_inc(ln_scaled.sem, 1)
                    if i == 6:
                        d_output(l, 2)
                        d_output(l, 3)
                    evacuate(l, out + 1, 1, work[:, b + 1, :], cols)
                    if i % 2 == 0:
                        dve.wait_ge(evacuated.sem, evacuated.at(l, out + 2))
                        tt(c_pad[:, C_PAD:C_PAD + TOK], work[:, b, :], work[:, b + 1, :], ALU.mult
                           ).then_inc(c_prod.sem, 1)
                c_gate(l, GT - 1)

                def add_resid(k, b):
                    dve.wait_ge(out_done.sem, out_done.at(l, OUT_O + k + 1))
                    r = flat(resid[:, bass.ds(k, 1), :])
                    tt(r[:, asked], main[b][:, asked], r[:, asked], ALU.add).then_inc(evacuated.sem, 1)
                    if last:
                        return
                    dve.wait_ge(h_hi_done.sem, h_hi_done.at(l + 1, k + 1))
                    stt(out=flat(h_lo[:, bass.ds(k, 1), :]), in0=r, scalar=flat(norms[:, bass.ds(l + 1, 1), bass.ds(k, 1)]),
                        in1=flat(h_hi[:, bass.ds(k, 1), :]).bitcast(F32), op0=ALU.mult, op1=ALU.subtract
                        ).then_inc(h_lo_done.sem, 1)

                with dve.Fori(0, 7) as i:
                    ahead(l, 102 + 4 * i, 2)
                    add_resid(2 * i, 0)
                    ahead(l, 104 + 4 * i, 0)
                    add_resid(2 * i + 1, 1)
                ahead(l, 130, 2)
                add_resid(14, 0)
                if not last:
                    ahead(l + 1, 0, 0)
                add_resid(15, 1)
                if not last:
                    ahead(l + 1, 2, 2)
                else:
                    dve.wait_ge(evacuated.sem, evacuated.at(l, OUTS))
                    tt(y_tmp[:, 0, :], resid[:, 15, :], resid[:, 15, :], ALU.mult).then_inc(last_sq, 1)
                    dve.wait_ge(last_sq, 1)
                    dve.wait_ge(sq_done.sem, sq_done.at(l, 2 * KT - 3))
                    tt(sumsq, sumsq, y_tmp[:, 0, :], ALU.add).then_inc(norm_in.sem, 1)

            with dve.Fori(0, DEPTH - 1) as l:
                layer(l, False)
            layer(DEPTH - 1, True)
            norm(DEPTH)
            for k in range(4, KT):
                ins = stt(out=resid[:, k, META:TOK], in0=resid[:, k, META:TOK], scalar=norms[:, DEPTH, k:k + 1],
                          in1=rstd[:, META:TOK], op0=ALU.mult, op1=ALU.mult)
                if k % 2 == 1:
                    ins.then_inc(final_done[k // 2], 1)

        @block.gpsimd
        def _(pool):
            tt = nc.gpsimd.tensor_tensor
            squares = conv_tmp[:, 0, :]

            def sum_squares(l, k, done):
                pool.wait_ge(evacuated.sem, evacuated.at(l, OUT_O + k + 1))
                x = flat(resid[:, bass.ds(k, 1), :])
                if isinstance(k, int) and k == 0:
                    tt(sumsq, x, x, ALU.mult).then_inc(sq_done.sem, 1)
                    return
                pool.wait_ge(sq_done.sem, sq_done.at(l, 2 * k - 1))
                tt(squares, x, x, ALU.mult).then_inc(sq_done.sem, 1)
                pool.wait_ge(sq_done.sem, sq_done.at(l, 2 * k))
                tt(sumsq, sumsq, squares, ALU.add).then_inc(done.sem, 1)

            nc.gpsimd.memset(u_pad[:, :, 0:D_PAD], 0.0)
            pool.wait_ge(const_in[0], 16)
            for q in range(3):
                x = resid[:, 4 * q:4 * q + 4, :]
                pool.wait_ge(x_in[q], 16)
                if q == 0:
                    tt(conv[:, :, :], x, x, ALU.mult).then_inc(sq_pool, 1)
                    continue
                if q == 2:
                    pool.wait_ge(sq_pool, 3)
                tt(conv_tmp[:, :, :], x, x, ALU.mult).then_inc(sq_pool, 1)
                pool.wait_ge(sq_pool, 2 * q)
                tt(conv[:, :, :], conv[:, :, :], conv_tmp[:, :, :], ALU.add).then_inc(sq_pool if q == 1 else sq_first, 1)
            pool.wait_ge(const_in[3], 16)
            pool.wait_ge(const_in[5], 16)
            pool.wait_ge(const_in[6], 16)

            def layer(l, last):
                def tap(j, acc):
                    w = dconv[:, bass.ds(l * GT, GT), bass.ds(j, 1)].broadcast_to([P, GT, TOK])
                    tt(conv_tmp[:, :, :], u_pad[:, :, bass.ds(j, TOK)], w, ALU.mult).then_inc(tap_done.sem, 1)
                    pool.wait_ge(tap_done.sem, tap_done.at(l, 2 * j + 1))
                    tt(conv[:, :, :], acc, conv_tmp[:, :, :], ALU.add).then_inc(tap_done.sem, 1)

                pool.wait_ge(glu_done.sem, glu_done.at(l, GT))
                tap(0, dvec[:, bass.ds(l, 1), 0, :].rearrange("p a b -> p b a").broadcast_to([P, GT, TOK]))
                with pool.Fori(1, D_TAPS) as j:
                    pool.wait_ge(tap_done.sem, tap_done.at(l, 2 * j))
                    tap(j, conv[:, :, :])

                def tile_sums(l, k, src):
                    acc = conv_tmp[:, 0, :]
                    tt(acc, src[:, 0, :], src[:, 1, :], ALU.add).then_inc(ln_pre.sem, 1)
                    for n in (2, 3):
                        pool.wait_ge(ln_pre.sem, ln_pre.at(l, 3 * k + n - 1))
                        tt(acc, acc, src[:, n, :], ALU.add).then_inc(ln_pre.sem, 1)

                pool.wait_ge(tap_done.sem, tap_done.at(l, 2 * D_TAPS))
                for n in range(5):
                    pool.wait_ge(evacuated.sem, evacuated.at(l, OUT_A + n + 1))
                    for q in range(4):
                        if n or q:
                            pool.wait_ge(a_sin.sem, a_sin.at(l, 4 * n + q))
                        src, dst = slice(32 * q, 32 * q + 32), slice(32 * (q ^ 1), 32 * (q ^ 1) + 32)
                        tt(a_turned_sin[n][dst, :], work[src, n, :], sin[src, :], ALU.mult).then_inc(a_sin.sem, 1)
                pool.wait_ge(a_sin.sem, a_sin.at(l, 4 * 5))
                tile_sums(l, 0, conv)
                pool.wait_ge(roped.sem, roped.at(l, 17))
                for c in (1, 2):
                    k0 = META + CHUNK * c
                    nc.gpsimd.tensor_copy(a_windows[:, c - 1, :, 0:META], a_k[:, :, 0:META]).then_inc(window_done.sem, 1)
                    nc.gpsimd.tensor_copy(a_windows[:, c - 1, :, META:144], a_k[:, :, k0:k0 + P]).then_inc(window_done.sem, 1)
                pool.wait_ge(ln_center.sem, ln_center.at(l, 1))
                tt(conv_tmp[:, :, :], conv[:, :, :], conv[:, :, :], ALU.mult).then_inc(ln_sq.sem, 1)
                pool.wait_ge(ln_sq.sem, ln_sq.at(l, 1))
                tile_sums(l, 1, conv_tmp)

                sum_squares(l, 0, sq_done)
                with pool.Fori(1, KT - 1) as k:
                    sum_squares(l, k, sq_done)
                if not last:
                    sum_squares(l, KT - 1, norm_in)

            with pool.Fori(0, DEPTH - 1) as l:
                layer(l, False)
            layer(DEPTH - 1, True)
            x = resid[:, 0:4, META:TOK]
            tt(x, x, norms[:, DEPTH, 0:4].unsqueeze(2).broadcast_to([P, 4, TOK - META]), ALU.mult).then_inc(weighted, 1)
            pool.wait_ge(weighted, 1)
            pool.wait_ge(norm_done.sem, norm_done.at(DEPTH, 1))
            for q in range(2):
                x = resid[:, 2 * q:2 * q + 2, META:TOK]
                tt(x, x, rstd[:, META:TOK].unsqueeze(1).broadcast_to([P, 2, TOK - META]), ALU.mult).then_inc(final_done[q], 1)


def kernel(x, meta_tokens, norm_w, w_in, a_sinks, b_q_norm, b_kv_norm, b_w_uq, b_w_ukv,
           c_conv_w, d_conv_w, d_conv_b, d_ln_w, d_ln_b, w_out, final_norm_w):
    import concourse.bacc as bacc
    from concourse.bass_utils import run_bass_kernel_spmd

    arr = {k: np.asarray(v) for k, v in dict(
        x=x, meta=meta_tokens, norm_w=norm_w, w_in=w_in, sinks=a_sinks, bq=b_q_norm, bkv=b_kv_norm, uq=b_w_uq,
        ukv=b_w_ukv, cw=c_conv_w, dw=d_conv_w, db=d_conv_b, lw=d_ln_w, lb=d_ln_b, w_out=w_out, fw=final_norm_w).items()}

    def by_feature(a):
        t = a.reshape(a.shape[:-1] + (a.shape[-1] // P, P))
        return np.ascontiguousarray(np.moveaxis(t, -1, 0))

    sizes = [512, 128, 128, 512, 512, 256, 64, 512, 512, 512, 512, 512, 512, 512, 512]
    names = ["aq", "ak", "av", "ag", "bcq", "bckv", "bkr", "bg", "cb", "cc", "cx", "cg", "da", "dgl", "dg"]
    start = dict(zip(names, np.cumsum([0] + sizes[:-1])))
    w_in_a, uq, w_o = arr["w_in"], arr["uq"], arr["w_out"]
    units = []

    def put(w):
        k, n = w.shape[0] // P, w.shape[1]
        per = UNIT // n
        t = w.reshape(k // per, per, P, n).transpose(0, 2, 1, 3).reshape(k // per, P, UNIT)
        units.extend(t)

    def tile(l, name, t):
        c = start[name] + P * t
        put(w_in_a[l][:, c:c + P])

    for l in range(DEPTH):
        for t in range(GT):
            tile(l, "da", t), tile(l, "dgl", t)
        for t in range(GT):
            tile(l, "dg", t)
        for t in range(GT):
            tile(l, "bcq", t)
        for t in range(2):
            tile(l, "bckv", t)
        for t in range(GT):
            tile(l, "bg", t)
        put(w_in_a[l][:, start["bkr"]:start["bkr"] + 64])
        q = uq[l].reshape(512, B_HEADS, 192)
        put(q[:, :, P:].reshape(512, 256))
        put(q[:, 0:2, :P].reshape(512, 256))
        put(q[:, 2:4, :P].reshape(512, 256))
        for t in range(GT):
            tile(l, "aq", t)
        tile(l, "ak", 0), tile(l, "av", 0)
        for t in range(GT):
            tile(l, "ag", t)
        for t in range(GT):
            tile(l, "cc", t), tile(l, "cx", t), tile(l, "cb", t), tile(l, "cg", t)
        rows = w_o[l].reshape(4, 512, D_MODEL)[[3, 1, 0, 2]].reshape(D_MODEL, D_MODEL)
        for t in range(KT):
            put(rows[:, P * t:P * t + P])
    assert len(units) == DEPTH * UNITS
    stream = np.stack(units).reshape(len(units) // RING, RING, P, UNIT)

    kv = arr["ukv"].reshape(DEPTH, 2, P, B_HEADS, 2, P)
    ukv = np.ascontiguousarray(kv.transpose(0, 2, 1, 4, 3, 5)).reshape(DEPTH, P, 2, UNIT)
    tokens = np.concatenate([arr["meta"], arr["x"][0]], axis=0)
    x_t = np.ascontiguousarray(by_feature(tokens).transpose(0, 2, 1))
    norms = by_feature(np.concatenate([arr["norm_w"], arr["fw"][None]], axis=0))
    bnorm = by_feature(np.concatenate([arr["bq"], arr["bkv"]], axis=1))
    dconv = np.ascontiguousarray(by_feature(arr["dw"]).transpose(0, 1, 3, 2)).reshape(P, DEPTH * GT, D_TAPS)
    cconv = np.ascontiguousarray(by_feature(arr["cw"]).transpose(0, 1, 3, 2)).reshape(P, DEPTH * GT, C_TAPS)
    dvec = by_feature(np.stack([arr["db"], arr["lw"], arr["lb"]], axis=1))

    inv = (1.0 / (np.float32(10000.0) ** (np.arange(0, 64, 2, dtype=np.float32) / np.float32(64)))).astype(np.float32)
    ang = (np.arange(TOK, dtype=np.float32)[:, None] * inv[None, :]).astype(np.float32)
    sines = np.tile(np.sin(ang).T, (4, 1))
    sign = np.where(np.arange(P)[:, None] % 64 < 32, 1.0, -1.0)
    rope = np.stack([np.tile(np.cos(ang).T, (4, 1)), sines * sign], axis=1).astype(np.float32)
    chunk = np.where(np.arange(TOK) < META, 0, (np.arange(TOK) - META) // CHUNK + 1)
    mask = np.stack([(chunk[None] == np.arange(5)[:, None]) * 1.0, (chunk[None] > np.arange(5)[:, None]) * NEG],
                    axis=1).astype(np.float32)
    rot = -np.eye(P, dtype=np.float32).reshape(P, 2, 2, 32)[:, :, ::-1].reshape(P, P)
    mats = np.stack([np.eye(P, dtype=np.float32), np.ones((P, P), np.float32), rot], axis=1)

    nc = bacc.Bacc("TRN2", target_bir_lowering=False, num_devices=1)
    arrays = dict(stream=stream, ukv=ukv, x=x_t, norms=norms, bnorm=bnorm, dconv=dconv, cconv=cconv, dvec=dvec,
                  sinks=np.ascontiguousarray(arr["sinks"].reshape(DEPTH, 2, 2, 2).transpose(2, 0, 1, 3)).reshape(2, -1),
                  sinks_m=np.ascontiguousarray(arr["sinks"].reshape(DEPTH, 2, 4).transpose(2, 0, 1)).reshape(4, -1),
                  rope=rope, mask=mask, mats=mats)
    args = [nc.dram_tensor(f"{n}_dram", a.shape, F32, kind="ExternalInput").ap() for n, a in arrays.items()]
    out_ap = nc.dram_tensor("out_dram", (P, KT, TOK - META), F32, kind="ExternalOutput").ap()
    build(nc, *args, out_ap)
    r = run_bass_kernel_spmd(nc, [{f"{n}_dram": a for n, a in arrays.items()}], core_ids=[0])
    y = np.asarray(r.results[0]["out_dram"])
    return np.ascontiguousarray(y.transpose(2, 1, 0)).reshape(1, TOK - META, D_MODEL)
```
